# Optimizing a Trainium2 kernel written in Bass

```python
import math
import jax
import jax.numpy as jnp
from jax import lax
import numpy as np

D_MODEL = 1024
BATCH = 1
SEQ = 256
DEPTH = 2

GRID_W = 64
CTX_LEN = 256
N_EVEN = (DEPTH + 1) // 2
N_ODD = DEPTH // 2
N_MOD = 9
DEEPNORM_ALPHA = (2.0 * DEPTH) ** 0.25
DEEPNORM_BETA = (8.0 * DEPTH) ** -0.25
LN_EPS = 1e-5
RMS_EPS = 1e-6
MACARON_WEIGHT = 0.5
FFN_HIDDEN = ((8 * D_MODEL // 3 + 255) // 256) * 256

HYENA_WIDTH = D_MODEL // 2
HYENA_ORDER = 2
HYENA_FILTERS = HYENA_ORDER - 1
HYENA_PROJ = (HYENA_ORDER + 1) * HYENA_WIDTH
HYENA_BANDS = 16
HYENA_EMB = 1 + 2 * HYENA_BANDS
HYENA_FILTER_HIDDEN = 64
HYENA_FAST_DECAY = 0.3
HYENA_SLOW_DECAY = 1.5
HYENA_TARGET = 1e-2

GLA_WIDTH = D_MODEL - HYENA_WIDTH
GLA_HEADS = 4
GLA_DV = GLA_WIDTH // GLA_HEADS
GLA_DK = GLA_DV // 2
GLA_QK = GLA_HEADS * GLA_DK
GLA_RANK = 16
GLA_TAU = 16.0
GLA_CHUNK = 64
EVEN_SIZES = (HYENA_PROJ, GLA_QK, GLA_QK, GLA_WIDTH, GLA_WIDTH, GLA_RANK, GLA_RANK)
EVEN_IN = HYENA_PROJ + 2 * GLA_QK + 2 * GLA_WIDTH + 2 * GLA_RANK

ATTN_HEAD_DIM = 128
ATTN_Q_HEADS = D_MODEL // ATTN_HEAD_DIM
ATTN_KV_HEADS = 2
ATTN_GROUP = ATTN_Q_HEADS // ATTN_KV_HEADS
ATTN_BLOCK = 128
ATTN_Q_WIDTH = ATTN_Q_HEADS * ATTN_HEAD_DIM
ATTN_KV_WIDTH = ATTN_KV_HEADS * ATTN_HEAD_DIM
ODD_IN = ATTN_Q_WIDTH + 2 * ATTN_KV_WIDTH
ROPE_THETA = 10000.0
ROPE_AXIS_PAIRS = ATTN_HEAD_DIM // 4

kernel_name = 'hybrid_hyena_gla_gqa_diffusion_trunk'

def layer_norm(x, g, b):
    xf = x.astype(jnp.float32)
    mu = jnp.mean(xf, -1, keepdims=True)
    var = jnp.mean(jnp.square(xf - mu), -1, keepdims=True)
    return ((xf - mu) * lax.rsqrt(var + LN_EPS) * g + b).astype(x.dtype)

def rms_norm(x, g):
    xf = x.astype(jnp.float32)
    return (xf * lax.rsqrt(jnp.mean(xf * xf, -1, keepdims=True) + RMS_EPS) * g).astype(x.dtype)

def mod_input(z, mm, slot):
    return z * (1.0 + mm[:, 3 * slot + 1]) + mm[:, 3 * slot]

def gated_post_norm(z, y, mm, slot, g, b):
    return layer_norm(DEEPNORM_ALPHA * z + mm[:, 3 * slot + 2] * y, g, b)

def swiglu(h, w1, w2):
    gate, up = jnp.split(h @ w1, 2, axis=-1)
    return (jax.nn.silu(gate) * up) @ w2

def ffn_sublayer(z, mm, slot, w1, w2, g, b):
    y = MACARON_WEIGHT * swiglu(mod_input(z, mm, slot), w1, w2)
    return gated_post_norm(z, y, mm, slot, g, b)

def split_sizes(t, sizes):
    idx, acc = [], 0
    for s in sizes[:-1]:
        acc += s
        idx.append(acc)
    return jnp.split(t, idx, axis=-1)

def short_conv3(u, w, b):
    up = jnp.pad(u, ((0, 0), (1, 1), (0, 0)))
    return up[:, :-2] * w[0] + up[:, 1:-1] * w[1] + up[:, 2:] * w[2] + b

def hyena_filter_spectrum(length, w1, b1, fr1, w2, b2, fr2, w3, b3):
    f32 = jnp.float32
    n = jnp.arange(length, dtype=f32)[:, None]
    t = jnp.linspace(0.0, 1.0, length, dtype=f32)[:, None]
    bands = jnp.linspace(1e-4, HYENA_BANDS - 1, HYENA_BANDS, dtype=f32)[None, :]
    ang = 2.0 * math.pi * n * bands / length
    feats = jnp.concatenate([t, jnp.cos(ang), -jnp.sin(ang)], axis=-1)
    h = jnp.sin(fr1.astype(f32) * (feats @ w1.astype(f32) + b1.astype(f32)))
    h = jnp.sin(fr2.astype(f32) * (h @ w2.astype(f32) + b2.astype(f32)))
    h = (h @ w3.astype(f32) + b3.astype(f32)).reshape(length, HYENA_FILTERS, 2, HYENA_WIDTH)
    max_decay = math.log(HYENA_TARGET) / HYENA_FAST_DECAY
    min_decay = math.log(HYENA_TARGET) / HYENA_SLOW_DECAY
    deltas = jnp.abs(jnp.linspace(min_decay, max_decay, HYENA_WIDTH, dtype=f32))
    h = h * jnp.exp(-t[:, :, None, None] * deltas)
    h_fwd, h_bwd = h[:, :, 0], h[:, :, 1]
    k = jnp.concatenate([h_fwd, jnp.zeros_like(h_fwd[:1]), jnp.flip(h_bwd[1:], axis=0)], axis=0)
    k = k * lax.rsqrt(jnp.sum(jnp.square(k), axis=0, keepdims=True) + 1e-6)
    return jnp.fft.rfft(k, axis=0)

def fft_long_conv(z, k_hat, skip):
    L = z.shape[1]
    z_hat = jnp.fft.rfft(z.astype(jnp.float32), n=2 * L, axis=1)
    y = jnp.fft.irfft(z_hat * k_hat, n=2 * L, axis=1)[:, :L]
    return (y + z.astype(jnp.float32) * skip).astype(z.dtype)

def hyena_mix(u, k_hat, conv_w, conv_b, skip):
    parts = jnp.split(short_conv3(u, conv_w, conv_b), HYENA_ORDER + 1, axis=-1)
    z = parts[0]
    for n in range(HYENA_FILTERS):
        z = fft_long_conv(z * parts[n + 1], k_hat[:, n], skip[n])
    return z * parts[HYENA_ORDER]

def gla_chunked(q, k, v, log_a, s0):
    f32 = jnp.float32
    Bn, L, H, _ = q.shape
    n = L // GLA_CHUNK

    def chunks(t):
        return t.reshape(Bn, n, GLA_CHUNK, H, t.shape[-1]).astype(f32)

    qc, kc, vc, gc = chunks(q), chunks(k), chunks(v), chunks(log_a)
    b = jnp.cumsum(gc, axis=2)
    b_last = b[:, :, -1:]
    q_in = qc * jnp.exp(b)
    k_in = kc * jnp.exp(-b)
    k_st = kc * jnp.exp(b_last - b)
    mask = jnp.tril(jnp.ones((GLA_CHUNK, GLA_CHUNK), dtype=bool))
    att = jnp.where(mask, jnp.einsum('bnchd,bnshd->bnhcs', q_in, k_in), 0.0)
    o_intra = jnp.einsum('bnhcs,bnshe->bnche', att, vc)
    ds = jnp.einsum('bnchd,bnche->nbhde', k_st, vc)
    decay = jnp.moveaxis(jnp.exp(b_last[:, :, 0]), 1, 0)

    def step(s, inp):
        dec, d = inp
        return dec[..., None] * s + d, s

    s_final, s_before = lax.scan(step, s0.astype(f32), (decay, ds))
    o_inter = jnp.einsum('bnchd,nbhde->bnche', q_in, s_before)
    o = (o_intra + o_inter).reshape(Bn, L, H, v.shape[-1])
    return o.astype(v.dtype), s_final

def gla_reverse(q, k, v, log_a, s0):
    o, s = gla_chunked(jnp.flip(q, 1), jnp.flip(k, 1), jnp.flip(v, 1), jnp.flip(log_a, 1), s0)
    return jnp.flip(o, 1), s

def even_mixer(a, ac, w_in, w_out, conv_w, conv_b, f_w1, f_b1, f_fr1, f_w2, f_b2, f_fr2, f_w3, f_b3,
               skip, gate_up, gate_b, norm_g, need_ctx):

    def project(z):
        Bn, L = z.shape[:2]
        hy, q, k, v, g, af, ab = split_sizes(z @ w_in, EVEN_SIZES)

        def heads(t, d):
            return t.reshape(Bn, L, GLA_HEADS, d)

        def log_gate(lo, j):
            return heads(jax.nn.log_sigmoid((lo @ gate_up[j] + gate_b[j]).astype(jnp.float32)) / GLA_TAU, GLA_DK)

        return (hy, heads(q, GLA_DK) * GLA_DK ** -0.5, heads(k, GLA_DK), heads(v, GLA_DV), g,
                log_gate(af, 0), log_gate(ab, 1))

    def hyena(hy):
        k_hat = hyena_filter_spectrum(hy.shape[1], f_w1, f_b1, f_fr1, f_w2, f_b2, f_fr2, f_w3, f_b3)
        return hyena_mix(hy, k_hat, conv_w, conv_b, skip)

    def gla_merge(o, g):
        Bn, L = g.shape[:2]
        return rms_norm(o, norm_g).reshape(Bn, L, GLA_WIDTH) * jax.nn.silu(g)

    hy, q, k, v, g, lf, lb = project(a)
    hyc, qc, kc, vc, gc, lfc, lbc = project(ac)
    s0 = jnp.zeros((ac.shape[0], GLA_HEADS, GLA_DK, GLA_DV), jnp.float32)
    oc_f, sc_f = gla_chunked(qc, kc, vc, lfc, s0)
    oc_b, sc_b = gla_reverse(qc, kc, vc, lbc, s0)
    o_f, _ = gla_chunked(q, k, v, lf, sc_f)
    o_b, _ = gla_reverse(q, k, v, lb, sc_b)
    y = jnp.concatenate([hyena(hy), gla_merge(o_f + o_b, g)], axis=-1) @ w_out
    yc = jnp.concatenate([hyena(hyc), gla_merge(oc_f + oc_b, gc)], axis=-1) @ w_out if need_ctx else None
    return y, yc

def rope_axis(x, ang):
    c = jnp.cos(ang)[None, :, None, :]
    s = jnp.sin(ang)[None, :, None, :]
    x1, x2 = jnp.split(x.astype(jnp.float32), 2, axis=-1)
    return jnp.concatenate([x1 * c - x2 * s, x2 * c + x1 * s], axis=-1)

def rope_2d(x, ang_r, ang_c):
    xr, xc = jnp.split(x, 2, axis=-1)
    return jnp.concatenate([rope_axis(xr, ang_r), rope_axis(xc, ang_c)], axis=-1).astype(x.dtype)

def gqa_attend(q, k, v):
    Bn, Lq = q.shape[:2]
    qg = q.reshape(Bn, Lq, ATTN_KV_HEADS, ATTN_GROUP, ATTN_HEAD_DIM)
    s = jnp.einsum('bqkgd,bskd->bkgqs', qg, k, preferred_element_type=jnp.float32) * ATTN_HEAD_DIM ** -0.5
    p = jax.nn.softmax(s, axis=-1).astype(v.dtype)
    o = jnp.einsum('bkgqs,bskd->bqkgd', p, v)
    return o.reshape(Bn, Lq, ATTN_Q_WIDTH)

def odd_mixer(a, ac, w_in, w_out, q_norm, k_norm, ang_r, ang_c, need_ctx):
    def project(z):
        Bn, L = z.shape[:2]
        q, k, v = jnp.split(z @ w_in, [ATTN_Q_WIDTH, ATTN_Q_WIDTH + ATTN_KV_WIDTH], axis=-1)
        q = rms_norm(q.reshape(Bn, L, ATTN_Q_HEADS, ATTN_HEAD_DIM), q_norm)
        k = rms_norm(k.reshape(Bn, L, ATTN_KV_HEADS, ATTN_HEAD_DIM), k_norm)
        return q, k, v.reshape(Bn, L, ATTN_KV_HEADS, ATTN_HEAD_DIM)

    q, k, v = project(a)
    q, k = rope_2d(q, ang_r, ang_c), rope_2d(k, ang_r, ang_c)
    qc, kc, vc = project(ac)
    k_all = jnp.concatenate([k, kc], axis=1)
    v_all = jnp.concatenate([v, vc], axis=1)
    Bn, S = a.shape[:2]
    q_blocks = q.reshape(Bn, S // ATTN_BLOCK, ATTN_BLOCK, ATTN_Q_HEADS, ATTN_HEAD_DIM).swapaxes(0, 1)
    o = lax.map(lambda qb: gqa_attend(qb, k_all, v_all), q_blocks)
    y = o.swapaxes(0, 1).reshape(Bn, S, ATTN_Q_WIDTH) @ w_out
    yc = gqa_attend(qc, kc, vc) @ w_out if need_ctx else None
    return y, yc

def setup_inputs(seed: int = 0) -> dict:
    key = jax.random.key(seed)
    ks = iter(jax.random.split(key, 48))
    f32 = jnp.float32
    D = D_MODEL

    def nrm(shape, scale):
        return scale * jax.random.normal(next(ks), shape, f32)

    return {
        'x': nrm((BATCH, SEQ, D), 1.0),
        'c': nrm((BATCH, D), 1.0),
        'ctx': nrm((BATCH, CTX_LEN, D), 1.0),
        'c_ctx': nrm((D,), 1.0),
        'ada_w': nrm((DEPTH, D, N_MOD * D), D ** -0.5),
        'ada_b': nrm((DEPTH, N_MOD * D), 0.02),
        'ln_g': 1.0 + nrm((DEPTH, 3, D), 0.02),
        'ln_b': nrm((DEPTH, 3, D), 0.02),
        'ffn_w1': nrm((DEPTH, 2, D, 2 * FFN_HIDDEN), D ** -0.5),
        'ffn_w2': nrm((DEPTH, 2, FFN_HIDDEN, D), DEEPNORM_BETA * FFN_HIDDEN ** -0.5),
        'even_w_in': nrm((N_EVEN, D, EVEN_IN), D ** -0.5),
        'even_w_out': nrm((N_EVEN, D, D), DEEPNORM_BETA * D ** -0.5),
        'hyena_conv_w': nrm((N_EVEN, 3, HYENA_PROJ), 3 ** -0.5),
        'hyena_conv_b': nrm((N_EVEN, HYENA_PROJ), 0.02),
        'hyena_f_w1': nrm((N_EVEN, HYENA_EMB, HYENA_FILTER_HIDDEN), HYENA_EMB ** -0.5),
        'hyena_f_b1': nrm((N_EVEN, HYENA_FILTER_HIDDEN), 0.1),
        'hyena_f_fr1': 1.0 + nrm((N_EVEN, HYENA_FILTER_HIDDEN), 0.1),
        'hyena_f_w2': nrm((N_EVEN, HYENA_FILTER_HIDDEN, HYENA_FILTER_HIDDEN), HYENA_FILTER_HIDDEN ** -0.5),
        'hyena_f_b2': nrm((N_EVEN, HYENA_FILTER_HIDDEN), 0.1),
        'hyena_f_fr2': 1.0 + nrm((N_EVEN, HYENA_FILTER_HIDDEN), 0.1),
        'hyena_f_w3': nrm((N_EVEN, HYENA_FILTER_HIDDEN, HYENA_FILTERS * 2 * HYENA_WIDTH), HYENA_FILTER_HIDDEN ** -0.5),
        'hyena_f_b3': nrm((N_EVEN, HYENA_FILTERS * 2 * HYENA_WIDTH), 0.02),
        'hyena_skip': nrm((N_EVEN, HYENA_FILTERS, HYENA_WIDTH), 0.1),
        'gla_gate_up': nrm((N_EVEN, 2, GLA_RANK, GLA_QK), GLA_RANK ** -0.5),
        'gla_gate_b': nrm((N_EVEN, 2, GLA_QK), 0.1),
        'gla_norm_g': 1.0 + nrm((N_EVEN, GLA_DV), 0.02),
        'attn_w_in': nrm((N_ODD, D, ODD_IN), D ** -0.5),
        'attn_w_out': nrm((N_ODD, D, D), DEEPNORM_BETA * D ** -0.5),
        'attn_q_norm': 1.0 + nrm((N_ODD, ATTN_HEAD_DIM), 0.02),
        'attn_k_norm': 1.0 + nrm((N_ODD, ATTN_HEAD_DIM), 0.02),
    }

def reference(x, c, ctx, c_ctx, ada_w, ada_b, ln_g, ln_b, ffn_w1, ffn_w2, even_w_in, even_w_out,
              hyena_conv_w, hyena_conv_b, hyena_f_w1, hyena_f_b1, hyena_f_fr1, hyena_f_w2, hyena_f_b2,
              hyena_f_fr2, hyena_f_w3, hyena_f_b3, hyena_skip, gla_gate_up, gla_gate_b, gla_norm_g,
              attn_w_in, attn_w_out, attn_q_norm, attn_k_norm):
    f32 = jnp.float32
    Bn, S = x.shape[:2]
    rows = S // GRID_W
    row = jnp.repeat(jnp.arange(rows, dtype=f32), GRID_W)
    col = jnp.tile(jnp.arange(GRID_W, dtype=f32), rows)
    inv_freq = ROPE_THETA ** (-jnp.arange(ROPE_AXIS_PAIRS, dtype=f32) / ROPE_AXIS_PAIRS)
    ang_r = row[:, None] * inv_freq
    ang_c = col[:, None] * inv_freq
    sc = jax.nn.silu(c)
    sc_ctx = jax.nn.silu(c_ctx)
    h, hc = x, ctx
    for i in range(DEPTH):
        need_ctx = i < DEPTH - 1
        m = (sc @ ada_w[i] + ada_b[i]).reshape(Bn, N_MOD, 1, D_MODEL)
        mc = (sc_ctx @ ada_w[i] + ada_b[i]).reshape(1, N_MOD, 1, D_MODEL)
        h = ffn_sublayer(h, m, 0, ffn_w1[i, 0], ffn_w2[i, 0], ln_g[i, 0], ln_b[i, 0])
        hc = ffn_sublayer(hc, mc, 0, ffn_w1[i, 0], ffn_w2[i, 0], ln_g[i, 0], ln_b[i, 0])
        a, ac = mod_input(h, m, 1), mod_input(hc, mc, 1)
        if i % 2 == 0:
            e = i // 2
            y, yc = even_mixer(a, ac, even_w_in[e], even_w_out[e], hyena_conv_w[e], hyena_conv_b[e],
                               hyena_f_w1[e], hyena_f_b1[e], hyena_f_fr1[e], hyena_f_w2[e], hyena_f_b2[e],
                               hyena_f_fr2[e], hyena_f_w3[e], hyena_f_b3[e], hyena_skip[e],
                               gla_gate_up[e], gla_gate_b[e], gla_norm_g[e], need_ctx)
        else:
            o = i // 2
            y, yc = odd_mixer(a, ac, attn_w_in[o], attn_w_out[o], attn_q_norm[o], attn_k_norm[o],
                              ang_r, ang_c, need_ctx)
        h = gated_post_norm(h, y, m, 1, ln_g[i, 1], ln_b[i, 1])
        h = ffn_sublayer(h, m, 2, ffn_w1[i, 1], ffn_w2[i, 1], ln_g[i, 2], ln_b[i, 2])
        if need_ctx:
            hc = gated_post_norm(hc, yc, mc, 1, ln_g[i, 1], ln_b[i, 1])
            hc = ffn_sublayer(hc, mc, 2, ffn_w1[i, 1], ffn_w2[i, 1], ln_g[i, 2], ln_b[i, 2])
    return h


_drawn_inputs = setup_inputs


def setup_inputs(seed=0):
    import zlib

    import numpy as np

    out = dict(_drawn_inputs(seed))
    spreads = {}
    factors = {'ctx': 2.882,
     'hyena_conv_b': 4.658,
     'hyena_f_b3': 2.97,
     'gla_gate_b': 8.0,
     'gla_norm_g': 8.0,
     'attn_q_norm': 8.0,
     'attn_k_norm': 8.0}
    for name, (base, spread) in spreads.items():
        noise = np.random.default_rng([zlib.crc32(name.encode()), seed]).standard_normal(out[name].shape)
        drawn = base * np.exp(spread * noise) if base else spread * noise
        out[name] = jnp.asarray(drawn.astype(out[name].dtype))
    for name, factor in factors.items():
        out[name] = (out[name] * factor).astype(out[name].dtype)
    return out
```

```python
from contextlib import ExitStack

import numpy as np

import concourse.bass as bass
from concourse import mybir

ALU = mybir.AluOpType
ACT = mybir.ActivationFunctionType
F32 = mybir.dt.float32
F32R = mybir.dt.float32r
I32 = mybir.dt.int32
AX_X = mybir.AxisListType.X

P = 128
D = 1024
KC = D // P
SEQ = 256
CTX = 256
T = SEQ + CTX
TC = T // P
DEPTH = 2
FFN = ((8 * D // 3 + 255) // 256) * 256
HC = FFN // P
HH = HC // 2
ALPHA = (2.0 * DEPTH) ** 0.25
LN_EPS = 1e-5
RMS_EPS = 1e-6

HYW = D // 2
YC = HYW // P
NFREQ = 2 * SEQ
BANDS, FHID = 16, 64
EMB = 1 + 2 * BANDS

GH, GDV, GDK = 4, 128, 64
GCH = 64
NCH = T // GCH
RANK = 16
TAU = 16.0
NLAT = SEQ // GCH

HD, QH, KVH = 128, 8, 2
GRID_W = 64

RING = 4
UCOL = 1024
UW2 = (6, 5)
ADA_PIECE = 3 * D // 2
PIECES = 2 * KC
MAGIC = 0x5F3759DF
ROUND = 12582912.0
TWO_PI_HI, TWO_PI_MID = 6.28125, 0.0019353071795864769
PI_LOW = 3.1415925
BIG = float(np.finfo(np.float32).max)


def column_map():
    at, n = {}, 0
    for name, k in (
        ("ada_b", DEPTH * 9 * KC), ("ln_g", DEPTH * 3 * KC), ("ln_b", DEPTH * 3 * KC), ("c", 2 * KC),
        ("conv_w", 3 * 3 * YC), ("conv_b", 3 * YC), ("skip", YC), ("gate_b", 4), ("gla_g", 1),
        ("q_norm", 1), ("k_norm", 1), ("f_b1", 1), ("f_fr1", 1), ("f_b2", 1), ("f_fr2", 1),
    ):
        at[name] = n
        n += k
    return at, n


COL, NCOL = column_map()

FFNS = [
    (0, 0, 0, T, [(0, 1), (0, 2)]),
    (0, 1, 2, T, [(1, 0), (1, 1)]),
    (1, 0, 0, T, [(1, 2), None]),
    (1, 1, 2, SEQ, [None, None]),
]
ADA_ORDER = [(0, 0), (0, 1), (0, 2), (1, 0), (1, 1), (1, 2)]
SUB_OF_FFN = (0, 2, 3, 5)


class Plan:

    def __init__(self):
        self.units = []
        self.ready = []
        self.free = []
        self.base = {}
        self.count = {}

    def bump(self, name, n=1):
        self.count[name] = self.count.get(name, 0) + n
        return self.count[name]

    def unit(self, *u):
        self.units.append(u)
        return len(self.units)

    def job(self, ready, free):
        self.ready.append(ready)
        self.free.append(free)
        return len(self.ready) - 1

    def mark(self, name):
        self.base[name] = (len(self.units), len(self.ready))


def make_plan():
    p = Plan()

    def ffn(fi):
        layer, f, _, _, adas = FFNS[fi]
        for half in range(2):
            p.mark(("w1", fi, half))
            for j in range(HH):
                m = (fi * 2 + half) * HH + j
                for g in range(2):
                    n = p.unit("w1", (layer, f, half * HH + j, g), UCOL)
                    p.job(("w_used", n), ("hraw_ready", m + 1))
            p.mark(("w2", fi, half))
            for oc in range(KC):
                for piece in range(2):
                    n = p.unit("w2", (layer, f, half, oc, piece), UW2[piece] * P)
                p.base[("z", SUB_OF_FFN[fi], half, oc)] = p.bump("z_ready")
                p.job(("w_used", n), ("z_ready", p.count["z_ready"]))
            if adas[half]:
                a = ADA_ORDER.index(adas[half])
                p.mark(("mod", a))
                p.job(("mods_summed", a + 1), ("mods_read", a + 1))

    def proj(name, n, free):
        p.mark((name, 0))
        for e in range(n):
            if free == "z_ready":
                p.base[("z", 1 if name == "e_out" else 4, 1, e)] = p.count["z_ready"] + 1
            u = p.unit(name, (e,), UCOL)
            p.job(("w_used", u), (free, p.bump(free)))

    def jobs(name, n, free):
        p.mark((name, 0))
        for _ in range(n):
            p.job((name, p.bump(name)), (free, p.bump(free)))

    jobs("filter_h", 2, "filter_h_read")
    jobs("filter_taps", 4, "taps_read")
    jobs("spectrum", 4, "spectrum_read")
    jobs("nyquist", 1, "nyquist_read")
    jobs("tap_norm", 1, "tap_norm_read")
    p.mark(("mod", 0))
    p.job(("mods_summed", 1), ("mods_read", 1))
    ffn(0)
    proj("e_low", 1, "low_read")
    proj("e_qk", 4, "qk_read")
    p.mark(("e_v", 0))
    for m in range(4):
        p.unit("e_v", (m,), UCOL)
    jobs("gate_pre", 4, "gate_read")
    proj("e_hy", 3 * YC, "hy_read")
    jobs("att", TC, "att_read")
    jobs("kst_turned", TC, "kst_read")
    jobs("ds", NCH, "ds_read")
    proj("e_g", GH, "g_read")
    jobs("osq", 1, "osq_read")
    jobs("orms", GH, "orms_read")
    jobs("z_turned", TC, "zt_read")
    jobs("dft", 8, "dft_read")
    jobs("idft", YC, "idft_read")
    proj("e_out", KC, "z_ready")
    ffn(1)
    ffn(2)
    proj("o_k", KVH, "k_read")
    p.mark(("o_v", 0))
    for m in range(2):
        p.unit("o_v", (m,), UCOL)
    jobs("krot", 1, "krot_read")
    jobs("ksq", 1, "ksq_read")
    jobs("krms", KVH, "krms_read")
    proj("o_q", QH, "q_read")
    jobs("qrot", QH // 2, "qrot_read")
    jobs("qsq", 1, "qsq_read")
    p.mark(("attn", 0))
    for step in range(-1, 2 * QH):
        if step + 1 < 2 * QH:
            p.base[("scores", step + 1)] = p.job(("scores", p.bump("scores")), ("scores_read", p.bump("scores_read")))
        if step >= 0:
            p.base[("turned", step)] = p.job(("p_turned", p.bump("p_turned")), ("pt_read", p.bump("pt_read")))
        if step >= 0 and step % 2 == 1:
            p.base[("attn_o", step // 2)] = p.job(("attn_o", p.bump("attn_o")), ("attn_o_read", p.bump("attn_o_read")))
    proj("o_out", KC, "z_ready")
    ffn(3)
    return p


SEMAPHORES = (
    "x_in", "par_in", "filter_in", "gla_in", "dft_in", "odd_in", "ones_made", "rst_made", "silu_c",
    "hi_ready", "lo_ready", "w_used",
    "ada_used", "acc_zeroed", "mods_summed", "mods_read", "mod_cols",
    "silu_ready", "hraw_ready", "hhi_ready", "h_ready",
    "z_ready", "s1_added", "sq_ready", "s2_added", "stat_sums", "diag_ready", "stat_bcast",
    "t_ready", "ahi_ready", "a_ready", "out_ready", "out_stored", "dve_link", "act_link",
    "filter_h", "filter_h_read", "filter_sin", "filter_taps", "taps_read", "taps_mixed", "taps_squared",
    "spectrum", "spectrum_read", "nyquist", "nyquist_read", "tap_norm", "tap_norm_read",
    "low_read", "qk_read", "v_read", "gate_pre", "gate_read", "gate_abs", "gate_ln", "gate_cum",
    "gate_rest", "gate_exp", "gla_ops", "hy_mid", "hy_read", "zf_ready", "att_even", "att", "att_read", "att_masked",
    "kst_turned", "kst_read", "ds", "ds_read", "state_ready", "g_read", "o_lower", "o_done", "o_copied", "o_sq",
    "osq", "osq_read", "odiag_ready", "orms", "orms_read", "gla_out", "z_turned", "zt_read",
    "dft", "dft_read", "spec_out", "idft", "idft_read", "cat", "cat_hi", "cat_ready",
    "k_read", "ov_read", "krot", "krot_read", "ksq", "ksq_read", "kdiag_ready", "krms", "krms_read",
    "q_read", "qrot", "qrot_read", "q_ready", "qsq", "qsq_read", "scores", "scores_read", "smax",
    "p_ready", "p_turned", "pt_read", "attn_o", "attn_o_read", "attn_hi",
)


def hybrid_trunk(nc, x_t, par_d, w1_d, w2_d, ada_d, ew_d, ev_d, eo_d, ow_d, ov_d, oo_d, gu_d,
                 fw1_d, fw2_d, fw3_d, feats_d, window_d, dft_d, idft_d, bound_d, rope_d, out):
    plan = make_plan()
    NU = len(plan.units)

    with ExitStack() as ctx:
        s = {n: ctx.enter_context(nc.semaphore(n)) for n in SEMAPHORES}
        raw_in = [ctx.enter_context(nc.semaphore(f"raw_in{i}")) for i in range(RING)]
        ada_in = [ctx.enter_context(nc.semaphore(f"ada_in{i}")) for i in range(2)]

        top = [(nc.sbuf_base + 63) // 64 * 64]

        def put(name, shape, dt=F32, at=None):
            size = int(np.prod(shape[1:])) * 4
            if at is None:
                at = top[0]
                top[0] += (size + 31) // 32 * 32
            return nc.alloc_sbuf_tensor_at(name, shape, dt, offset=at)

        ident = put("ident", [P, P])
        ones = put("ones", [P, P])
        par = put("par", [P, NCOL])
        mods = put("mods", [P, 2, 3 * KC])
        acol = put("acol", [P, 6, 2, 3, KC])
        hcol = put("hcol", [P, 6, 2, KC])
        stat = put("stat", [P, 6, 16])
        att_stat = put("att_stat", [P, 4, 2 * QH])
        dec = put("dec", [P, 2, 2, NCH])
        kscale = put("kscale", [P, YC])
        scol = put("scol", [P, 2, KC])
        hz = put("hz", [P, KC, T])
        a_hi = put("a_hi", [P, KC, T], F32R)
        a_lo = put("a_lo", [P, KC, T], F32R)
        raw = put("raw", [P, RING, UCOL])
        w_hi = put("w_hi", [P, RING, UCOL], F32R)
        w_lo = put("w_lo", [P, RING, UCOL], F32R)
        ada = put("ada", [P, 2, ADA_PIECE])
        X = top[0]
        K = 1024
        acc = put("acc", [P, 2, 3 * D], at=X)
        h_hi = put("h_hi", [P, HH, T], F32R, at=X + 24 * K)
        h_lo = put("h_lo", [P, HH, T], F32R, at=X + 46 * K)
        tmp_a = put("tmp_a", [P, 2, T], at=X + 68 * K)
        tmp_b = put("tmp_b", [P, 2, T], at=X + 72 * K)
        sq = put("sq", [P, 2, T], at=X + 76 * K)
        sum1 = put("sum1", [P, T], at=X + 80 * K)
        sum2 = put("sum2", [P, T], at=X + 82 * K)
        spec = put("spec", [P, 5, HYW], at=X + 84 * K)
        assert X + 94 * K <= nc.sbuf_usable_end
        window = put("window", [P, 4, HYW], at=X + 24 * K)
        fw3 = put("fw3", [FHID + 1, 2 * HYW], at=X + 32 * K)
        fw1 = put("fw1", [EMB, FHID], at=X + 36 * K)
        fw2 = put("fw2", [FHID, FHID], at=X + 36 * K + 256)
        feats = put("feats", [EMB, SEQ], at=X + 37 * K)
        farg = put("farg", [FHID, 2, SEQ], at=X + 38 * K)
        fh = put("fh", [FHID + 1, 2, SEQ], at=X + 40 * K)
        taps = put("taps", [P, 4, HYW], at=X + 42 * K)
        tmix = put("tmix", [P, 4, HYW], at=X + 50 * K)
        dft0 = put("dft0", [P, 2, NFREQ], at=X + 58 * K)
        tsq = put("tsq", [P, 4, HYW], at=X + 62 * K)
        qk = put("qk", [P, 4, T], at=X)
        attm = put("attm", [P, TC, 2, GH, GCH], at=X)
        ga = put("ga", [P, 4, T], at=X + 8 * K)
        cv = put("cv", [P, 2, 2, T], at=X + 8 * K)
        kstt = put("kstt", [P, TC, 2, 2, P], at=X + 8 * K)
        o_sb = put("o_sb", [P, GH, T], at=X + 8 * K)
        gm = put("gm", [P, 4, T], at=X + 16 * K)
        cum = put("cum", [P, 4, T], at=X + 24 * K)
        ds = put("ds_sb", [P, NCH, 2, 2, P], at=X + 16 * K)
        gs = put("gs", [P, GH, T], at=X + 16 * K)
        go = put("go", [P, GH, T], at=X + 24 * K)
        qin = put("qin", [P, 4, T], at=X + 32 * K)
        kin = put("kin", [P, 4, T], at=X + 40 * K)
        kst = put("kst", [P, 4, T], at=X + 48 * K)
        state = put("state", [P, NCH, 2, 2, P], at=X + 40 * K)
        osqr = put("osqr", [P, GH, T], at=X + 40 * K)
        odiag = put("odiag", [P, GH, T], at=X + 48 * K)
        v = put("v", [P, TC, GH * GDV], at=X + 56 * K)
        zf = put("zf", [P, YC, T], at=X + 64 * K)
        part2 = put("part2", [P, YC, T], at=X + 72 * K)
        low = put("low", [2 * RANK, T], at=X + 80 * K)
        rst = put("rst", [P, T], at=X + 82 * K)
        bound = put("bound", [P, 2, 2, GCH], at=X + 94 * K)
        gu = put("gu", [2 * RANK, 2, 2 * P], at=X + 56 * K)
        dft = put("dft_sb", [P, 2, NFREQ], at=X)
        idft = put("idft_sb", [P, 4, SEQ], at=X + 4 * K)
        zt = put("zt", [P, TC, HYW], at=X + 32 * K)
        prod = put("prod", [P, 4, HYW], at=X + 40 * K)
        yspec = put("yspec", [P, 4, 2, HYW], at=X + 48 * K)
        yt = put("yt", [P, 2, T], at=X + 8 * K)
        kg = put("kg", [P, KVH, T], at=X)
        krt = put("krt", [P, KVH, SEQ], at=X + 4 * K)
        ksqr = put("ksqr", [P, KVH, T], at=X + 6 * K)
        kd = put("kd", [P, KVH, T], at=X + 10 * K)
        kT = put("kT", [P, KVH, T], at=X + 14 * K)
        vo = put("vo", [P, TC, KVH * HD], at=X + 18 * K)
        rope = put("rope", [P, 2 * SEQ + P], at=X + 22 * K)
        qg = put("qg", [P, QH, SEQ], at=X + 26 * K)
        qsqr = put("qsqr", [P, QH, SEQ], at=X + 34 * K)
        qrt = put("qrt", [P, 2, 2, SEQ], at=X + 42 * K)
        pr = put("pr", [P, 2, T], at=X + 46 * K)
        prn = put("prn", [P, 2, T], at=X + 50 * K)
        pt = put("pt", [P, 2, TC, 2, P], at=X + 54 * K)
        assert X + 95 * K <= nc.sbuf_usable_end

        bank = [ctx.enter_context(nc.psum_tensor(f"bank{i}", [P, T], F32)) for i in range(8)]

        def pcol(name, i=0, rows=P):
            return par[0:rows, COL[name] + i:COL[name] + i + 1]

        def jbank(j):
            return bank[j % 4]

        def wait_for(eng, pair, more=0):
            name, value = pair
            eng.wait_ge(s[name], value + more)

        def job_ready(eng, j, more=0):
            wait_for(eng, plan.ready[j], more)

        def bank_read(eng, j, more=0):
            if j >= 4:
                wait_for(eng, plan.free[j - 4], more)

        def z_count(n, c, half=1):
            return plan.base[("z", n, half, c)]

        def chunk_of(m):
            return m % HH

        def unit_source(n, i=0):
            kind, at, cols = plan.units[n]
            if kind == "w1":
                layer, f, j, g = at
                return w1_d[layer, f, j + 2 * i, g]
            if kind == "w2":
                layer, f, half, oc, piece = at
                lo = piece * UW2[0] * P
                return w2_d[layer, f, half, oc][:, lo:lo + cols]
            if kind == "e_low":
                return ew_d[0]
            if kind == "e_qk":
                return ew_d[1 + at[0]]
            if kind == "e_hy":
                return ew_d[5 + at[0]]
            if kind == "e_g":
                return ew_d[5 + 3 * YC + at[0]]
            if kind == "e_v":
                return ev_d[at[0]]
            if kind == "e_out":
                return eo_d[at[0]]
            if kind == "o_k":
                return ow_d[at[0]]
            if kind == "o_q":
                return ow_d[KVH + at[0]]
            if kind == "o_v":
                return ov_d[at[0]]
            return oo_d[at[0]]

        E_U, E_J = plan.base[("e_low", 0)]
        O_U, O_J = plan.base[("o_k", 0)]

        def first_job(name):
            return plan.base[(name, 0)][1]

        def first_unit(name):
            return plan.base[(name, 0)][0]

        def hidden(t, j, i, nt):
            if isinstance(i, int):
                return t[:, j, 0:nt]
            return t[:, bass.ds(j + 2 * i, 1), 0:nt].rearrange("p a t -> p (a t)")

        block = ctx.enter_context(nc.Block())


        @block.sync
        def _(sp):
            pos = [0]

            def load_unit(n, i=0):
                cols = plan.units[n][2]
                if n >= RING:
                    sp.wait_ge(s["lo_ready"], n - RING + 1 + 4 * i)
                sp.dma_start(raw[:, n % RING, 0:cols], unit_source(n, i)).then_inc(raw_in[n % RING], 16)

            def load_to(n):
                while pos[0] < min(n, NU):
                    load_unit(pos[0])
                    pos[0] += 1

            def load_ada(a, k, piece, i=0):
                if a is None:
                    return
                layer, slot = ADA_ORDER[a]
                q = PIECES * a + 2 * k + piece
                if q >= 2:
                    sp.wait_ge(s["ada_used"], q - 1 + 2 * i)
                sp.dma_start(ada[:, piece, :], ada_d[layer, slot, k + i][:, piece * ADA_PIECE:(piece + 1) * ADA_PIECE])\
                    .then_inc(ada_in[piece], 16)

            for k in range(KC):
                for piece in range(2):
                    load_ada(0, k, piece)
                if k == 1:
                    load_to(RING)
            for fi, (_, _, _, _, adas) in enumerate(FFNS):
                for half in range(2):
                    a = ADA_ORDER.index(adas[half]) if adas[half] else None
                    n0, _ = plan.base[("w1", fi, half)]
                    load_to(n0 + 4)
                    load_ada(a, 0, 0)
                    load_to(n0 + 6)
                    load_ada(a, 0, 1)
                    with sp.Fori(0, 4) as i:
                        for jj in range(2):
                            load_unit(n0 + 6 + 2 * jj, i)
                            load_unit(n0 + 7 + 2 * jj, i)
                            load_ada(a, 1, jj, i)
                    pos[0] = n0 + 22
                    load_to(n0 + 24)
                    load_ada(a, 5, 0)
                    load_ada(a, 5, 1)
                    for oc in range(KC):
                        load_to(n0 + 22 + 2 * oc + 4)
                        if oc % 2 == 0:
                            load_ada(a, 6 + oc // 4, oc // 2 % 2)
                if fi == 0 or fi == 2:
                    load_to(plan.base[("w1", fi + 1, 0)][0])

        @block.gpsimd
        def _(pool):
            g = nc.gpsimd
            g.memset(ident[:], 0.0).then_inc(s["ones_made"], 1)
            pool.wait_ge(s["ones_made"], 1)
            g.affine_select(out=ident[:], in_=ident[:], compare_op=ALU.not_equal, fill=1.0, base=0,
                            pattern=[[-1, P]], channel_multiplier=1).then_inc(s["ones_made"], 1)
            g.memset(ones[:], 1.0).then_inc(s["ones_made"], 1)
            g.memset(fh[:], 1.0).then_inc(s["ones_made"], 1)
            g.memset(acc[:], 0.0).then_inc(s["acc_zeroed"], 1)

            def add_squares(n):
                nt = T if n < 4 else SEQ
                for c in range(1, KC):
                    pool.wait_ge(s["sq_ready"], KC * n + c + 1)
                    if c > 1:
                        pool.wait_ge(s["s2_added"], (KC - 1) * n + c - 1)
                    g.tensor_tensor(sum2[:, 0:nt], sum2[:, 0:nt], sq[:, c % 2, 0:nt],
                                    ALU.add).then_inc(s["s2_added"], 1)

            def zero_acc(a):
                pool.wait_ge(s["mods_summed"], a)
                g.memset(acc[:], 0.0).then_inc(s["acc_zeroed"], 1)

            zero_acc(1)
            zero_acc(2)
            add_squares(0)
            pool.wait_ge(s["a_ready"], 2 * KC)
            pool.dma_start(bound[:], bound_d).then_inc(s["gla_in"], 16)
            pool.dma_start(gu[:], gu_d).then_inc(s["gla_in"], 16)
            g.memset(rst[:], 1.0).then_inc(s["rst_made"], 1)
            pool.wait_ge(s["rst_made"], 1)
            g.memset(rst[:].rearrange("p (c t) -> p c t", t=GCH)[:, :, 0:1], 0.0).then_inc(s["rst_made"], 1)
            pool.wait_ge(s["o_done"], GH)
            pool.dma_start(dft[:], dft_d).then_inc(s["dft_in"], 16)
            pool.dma_start(idft[:], idft_d).then_inc(s["dft_in"], 16)
            add_squares(1)
            pool.wait_ge(s["a_ready"], 3 * KC)
            zero_acc(3)
            zero_acc(4)
            add_squares(2)
            zero_acc(5)
            add_squares(3)
            pool.wait_ge(s["a_ready"], 5 * KC)
            pool.dma_start(rope[:], rope_d).then_inc(s["odd_in"], 16)
            add_squares(4)
            add_squares(5)

        @block.scalar
        def _(act):
            A = nc.scalar
            pos, links = [0], [0]

            act.dma_start(par[:], par_d).then_inc(s["par_in"], 16)
            for t, d in ((feats, feats_d), (fw1, fw1_d), (fw2, fw2_d), (fw3, fw3_d), (window, window_d),
                         (dft0, dft_d)):
                act.dma_start(t[:], d).then_inc(s["filter_in"], 16)
            act.dma_start(hz[:], x_t).then_inc(s["x_in"], 16)

            def link(ins):
                links[0] += 1
                ins.then_inc(s["act_link"], 1)
                act.wait_ge(s["act_link"], links[0])

            def split_hi(n, i=0):
                cols = plan.units[n][2]
                act.wait_ge(raw_in[n % RING], 16 * (n // RING + 1) + 16 * i)
                if n >= RING:
                    act.wait_ge(s["w_used"], n - RING + 1 + 4 * i)
                A.copy(w_hi[:, n % RING, 0:cols], raw[:, n % RING, 0:cols]).then_inc(s["hi_ready"], 1)

            def split_to(n):
                while pos[0] < min(n, NU):
                    split_hi(pos[0])
                    pos[0] += 1

            def apply_ln(n):
                nt = T if n < 5 else SEQ
                nz = T if n < 4 else SEQ
                act.wait_ge(s["mod_cols"], n + 1)
                for c in range(KC):
                    if n > 0:
                        act.wait_ge(s["t_ready"], KC * (n - 1) + c + 1)
                    t = tmp_a[:, c % 2, :] if n > 0 else hz[:, c, :]
                    if c >= 2:
                        act.wait_ge(s["a_ready"], KC * n + c - 1)
                    for w in range(nt // SEQ):
                        cols = slice(w * SEQ, (w + 1) * SEQ)
                        ins = A.activation(tmp_b[:, c % 2, cols], t[:, cols], ACT.Identity,
                                           bias=acol[:, n, w, 1, c:c + 1], scale=acol[:, n, w, 0, c:c + 1])
                    link(ins)
                    A.activation(hz[:, c, 0:nz], t[:, 0:nz], ACT.Identity, bias=hcol[:, n, 1, c:c + 1],
                                 scale=hcol[:, n, 0, c:c + 1])
                    A.copy(a_hi[:, c, 0:nt], tmp_b[:, c % 2, 0:nt]).then_inc(s["ahi_ready"], 1)

            def square_z(n, c):
                nt = T if n < 4 else SEQ
                act.wait_ge(s["z_ready"], z_count(n, c))
                if c >= 3:
                    act.wait_ge(s["s2_added"], (KC - 1) * n + c - 2)
                A.activation(sum2[:, 0:nt] if c == 0 else sq[:, c % 2, 0:nt], hz[:, c, 0:nt],
                             ACT.Square).then_inc(s["sq_ready"], 1)

            def ffn(fi):
                nt = FFNS[fi][3]

                def hidden_step(n, m, j, i=0):
                    act.wait_ge(s["w_used"], n + 1 + 4 * i)
                    A.activation(tmp_a[:, m % 2, 0:nt], jbank(j0 + n - n0)[:, 0:nt], ACT.Silu)\
                        .then_inc(s["silu_ready"], 1)
                    act.wait_ge(s["hraw_ready"], m + 1 + 2 * i)
                    A.copy(hidden(h_hi, j, i, nt), tmp_b[:, m % 2, 0:nt]).then_inc(s["hhi_ready"], 1)

                for half in range(2):
                    n0, j0 = plan.base[("w1", fi, half)]
                    m0 = (2 * fi + half) * HH
                    for j in range(2):
                        split_to(n0 + 2 * j + 4)
                        hidden_step(n0 + 2 * j, m0 + j, j)
                    with act.Fori(0, 4) as i:
                        for j in (2, 3):
                            split_hi(n0 + 2 * j + 2, i)
                            split_hi(n0 + 2 * j + 3, i)
                            hidden_step(n0 + 2 * j, m0 + j, j, i)
                    pos[0] = n0 + 22
                    split_to(n0 + 24)
                    hidden_step(n0 + 20, m0 + 10, 10)
                    for oc in range(KC):
                        split_to(n0 + 22 + 2 * oc + 4)
                        if half == 1:
                            square_z(SUB_OF_FFN[fi], oc)

            def hyena_filter():
                for layer in range(2):
                    act.wait_ge(s["filter_h_read"], layer + 1)
                    if layer == 1:
                        act.wait_ge(s["ones_made"], 4)
                    else:
                        act.wait_ge(s["ones_made"], 4)
                    A.activation(fh[0:FHID, layer, :], farg[:, layer, :], ACT.Sin).then_inc(s["filter_sin"], 1)
                for i in range(4):
                    act.wait_ge(s["taps_read"], i + 1)
                    A.activation(tsq[:, i, :], taps[:, i, :], ACT.Square).then_inc(s["taps_squared"], 1)
                j0 = first_job("spectrum")
                for i in range(4):
                    job_ready(act, j0 + i)
                    if i == 0:
                        A.copy(spec[:, 4, :], jbank(j0)[:])
                    A.copy(spec[:, i, :], jbank(j0 + i)[:]).then_inc(s["spectrum_read"], 1)

            def even_mixer():
                for e in range(4):
                    split_to(E_U + e + 4)
                    job_ready(act, first_job("e_qk") + e)
                    A.copy(qk[:, e, :], jbank(first_job("e_qk") + e)[:]).then_inc(s["qk_read"], 1)
                split_to(first_unit("e_v") + 6)
                for e in range(4):
                    j = first_job("gate_pre") + e
                    job_ready(act, j)
                    A.activation(ga[:, e, :], jbank(j)[:], ACT.Abs, bias=pcol("gate_b", e)).then_inc(s["gate_abs"], 1)
                act.wait_ge(s["gate_abs"], 4)
                for e in range(4):
                    ins = A.activation(ga[:, e, :], ga[:, e, :], ACT.Exp, scale=-1.0)
                link(ins)
                for e in range(4):
                    A.activation(ga[:, e, :], ga[:, e, :], ACT.Ln, bias=1.0).then_inc(s["gate_ln"], 1)
                for e in range(4):
                    act.wait_ge(s["gate_rest"], e + 1)
                    A.activation(qin[:, e, :], cum[:, e, :], ACT.Exp, scale=1.0 / TAU)
                    A.activation(kin[:, e, :], cum[:, e, :], ACT.Exp, scale=-1.0 / TAU)
                    last = (GCH - 1) * (1 - e // 2)
                    A.activation(dec[:, e // 2, e % 2, :], cum[:, e, last::GCH], ACT.Exp, scale=1.0 / TAU)
                    A.activation(kst[:, e, :], kst[:, e, :], ACT.Exp, scale=1.0 / TAU).then_inc(s["gate_exp"], 1)
                for c in range(YC):
                    for part in range(3):
                        e = 3 * c + part
                        split_to(first_unit("e_hy") + e + 4)
                        j = first_job("e_hy") + e
                        job_ready(act, j)
                        if c >= 2 and part == 0:
                            act.wait_ge(s["zf_ready"], c - 1)
                        dst = part2[:, c, :] if part == 2 else cv[:, part, c % 2, :]
                        A.activation(dst, jbank(j)[:], ACT.Identity, bias=pcol("conv_b", YC * part + c),
                                     scale=pcol("conv_w", 3 * YC + YC * part + c)).then_inc(s["hy_mid"], 1)
                act.wait_ge(s["zf_ready"], YC)
                for t in range(TC):
                    j = first_job("kst_turned") + t
                    job_ready(act, j)
                    A.copy(kstt[:, t].rearrange("p a b c -> p (a b c)"), jbank(j)[:]).then_inc(s["kst_read"], 1)
                for cc in range(NCH):
                    j = first_job("ds") + cc
                    job_ready(act, j)
                    A.copy(ds[:, cc].rearrange("p a b c -> p (a b c)"), jbank(j)[:]).then_inc(s["ds_read"], 1)
                act.wait_ge(s["state_ready"], 7)
                for h in range(GH):
                    split_to(first_unit("e_g") + h + 4)
                    j = first_job("e_g") + h
                    job_ready(act, j)
                    A.activation(gs[:, h, :], jbank(j)[:], ACT.Silu).then_inc(s["g_read"], 1)
                for h in range(GH):
                    act.wait_ge(s["o_done"], h + 1)
                    A.copy(o_sb[:, h, :], bank[4 + h][:]).then_inc(s["o_copied"], 1)
                for h in range(GH):
                    A.activation(osqr[:, h, :], bank[4 + h][:], ACT.Square).then_inc(s["o_sq"], 1)
                for h in range(GH):
                    act.wait_ge(s["gla_out"], h + 1)
                    A.copy(a_hi[:, YC + h, :], go[:, h, :]).then_inc(s["cat_hi"], 1)
                for t in range(TC):
                    j = first_job("z_turned") + t
                    job_ready(act, j)
                    A.copy(zt[:, t, :], jbank(j)[:]).then_inc(s["zt_read"], 1)
                for c in range(YC):
                    act.wait_ge(s["cat"], c + 1)
                    A.copy(a_hi[:, c, :], yt[:, c % 2, :]).then_inc(s["cat_hi"], 1)
                for c in range(KC):
                    split_to(first_unit("e_out") + c + 4)
                    square_z(1, c)

            def odd_mixer():
                for g in range(KVH):
                    split_to(O_U + g + 4)
                    j = O_J + g
                    job_ready(act, j)
                    A.activation(kg[:, g, :], jbank(j)[:], ACT.Identity, scale=pcol("k_norm"))
                    A.activation(ksqr[:, g, :], jbank(j)[:], ACT.Square).then_inc(s["k_read"], 1)
                for h in range(QH):
                    split_to(first_unit("o_q") + h + 4)
                    j = first_job("o_q") + h
                    job_ready(act, j)
                    A.activation(qg[:, h, :], jbank(j)[:, 0:SEQ], ACT.Identity, scale=pcol("q_norm"))
                    A.activation(qsqr[:, h, :], jbank(j)[:, 0:SEQ], ACT.Square).then_inc(s["q_read"], 1)

                def p_exp(i):
                    act.wait_ge(s["smax"], i + 1)
                    if i >= 2:
                        act.wait_ge(s["p_ready"], i - 1)
                    A.activation(pr[:, i % 2, :], jbank(plan.base[("scores", i)])[:], ACT.Exp,
                                 bias=att_stat[:, 1, i:i + 1], scale=att_stat[:, 0, i:i + 1],
                                 accum_out=att_stat[:, 2, i:i + 1]).then_inc(s["scores_read"], 1)

                p_exp(0)
                for i in range(2 * QH):
                    if i + 1 < 2 * QH:
                        p_exp(i + 1)
                    j = plan.base[("turned", i)]
                    job_ready(act, j)
                    h, qb = divmod(i, 2)
                    if h >= 2:
                        act.wait_ge(s["attn_o"], h - 1)
                    A.copy(pt[:, h % 2, :, qb, :], jbank(j)[:].rearrange("p (c q) -> p c q", c=TC))\
                        .then_inc(s["pt_read"], 1)
                    if qb == 1:
                        act.wait_ge(s["attn_o"], h + 1)
                        A.copy(a_hi[:, h, 0:SEQ], jbank(plan.base[("attn_o", h)])[:, 0:SEQ]).then_inc(s["attn_hi"], 1)
                for c in range(KC):
                    split_to(first_unit("o_out") + c + 4)
                    square_z(4, c)

            act.wait_ge(s["par_in"], 16)
            A.activation(scol[:].rearrange("p a b -> p (a b)"), par[:, COL["c"]:COL["c"] + 2 * KC],
                         ACT.Silu).then_inc(s["silu_c"], 1)
            hyena_filter()
            split_to(RING)
            act.wait_ge(s["x_in"], 16)
            apply_ln(0)
            ffn(0)
            split_to(E_U + 4)
            apply_ln(1)
            even_mixer()
            split_to(plan.base[("w1", 1, 0)][0] + 4)
            apply_ln(2)
            ffn(1)
            split_to(plan.base[("w1", 2, 0)][0] + 4)
            apply_ln(3)
            ffn(2)
            split_to(O_U + 4)
            apply_ln(4)
            odd_mixer()
            split_to(plan.base[("w1", 3, 0)][0] + 4)
            apply_ln(5)
            ffn(3)
            for c in range(KC):
                act.wait_ge(s["t_ready"], 5 * KC + c + 1)
                A.activation(hz[:, c, 0:SEQ], tmp_a[:, c % 2, 0:SEQ], ACT.Identity,
                             bias=pcol("ln_b", 5 * KC + c), scale=pcol("ln_g", 5 * KC + c)).then_inc(s["out_ready"], 1)
                act.wait_ge(s["out_ready"], c + 1)
                act.dma_start(out[c * P:(c + 1) * P, :], hz[:, c, 0:SEQ]).then_inc(s["out_stored"], 16)
            act.wait_ge(s["out_stored"], 16 * KC)

        @block.vector
        def _(dve):
            V = nc.vector
            pos, links = [0], [0]

            def link(ins):
                links[0] += 1
                ins.then_inc(s["dve_link"], 1)
                dve.wait_ge(s["dve_link"], links[0])

            def split_lo(n, i=0):
                cols = plan.units[n][2]
                dve.wait_ge(s["hi_ready"], n + 1 + 4 * i)
                V.tensor_tensor(w_lo[:, n % RING, 0:cols], raw[:, n % RING, 0:cols],
                                w_hi[:, n % RING, 0:cols].bitcast(F32), ALU.subtract).then_inc(s["lo_ready"], 1)

            def split_to(n):
                while pos[0] < min(n, NU):
                    split_lo(pos[0])
                    pos[0] += 1

            def add_ada(a, k, piece, i=0):
                if a is None:
                    return
                q = PIECES * a + 2 * k + piece
                if k == 0 and piece == 0:
                    dve.wait_ge(s["acc_zeroed"], a + 1)
                dve.wait_ge(ada_in[piece], 16 * (KC * a + k + 1) + 16 * i)
                if q >= 2:
                    dve.wait_ge(s["ada_used"], q - 1 + 2 * i)
                cols = slice(piece * ADA_PIECE, (piece + 1) * ADA_PIECE)
                for w in range(2 if a < 5 else 1):
                    scalar = scol[:, w, k:k + 1] if isinstance(i, int) else scol[:, w, bass.ds(k + i, 1)]
                    ins = V.scalar_tensor_tensor(acc[:, w, cols], ada[:, piece, :], scalar, acc[:, w, cols],
                                                 ALU.mult, ALU.add)
                ins.then_inc(s["ada_used"], 1)

            def take_mods(a):
                nw = 2 if a < 5 else 1
                j = plan.base[("mod", a)][1]
                job_ready(dve, j)
                for w in range(nw):
                    ins = V.tensor_tensor(mods[:, w, :], jbank(j)[:, w * 3 * KC:(w + 1) * 3 * KC],
                                          par[:, COL["ada_b"] + a * 3 * KC:COL["ada_b"] + (a + 1) * 3 * KC], ALU.add)
                ins.then_inc(s["mods_read"], 1)
                dve.wait_ge(s["mods_read"], a + 1)
                for w in range(nw):
                    ins = V.tensor_scalar(mods[:, w, KC:2 * KC], mods[:, w, KC:2 * KC], 1.0, None, ALU.add)
                    V.tensor_scalar(acol[:, a, w, 2, :], mods[:, w, 2 * KC:3 * KC], 1.0 if a in (1, 4) else 0.5,
                                    None, ALU.mult)
                link(V.memset(hcol[:, a, 0, :], ALPHA))
                if a == 0:
                    V.memset(hcol[:, a, 1, :], 0.0)
                    for w in range(nw):
                        V.tensor_copy(acol[:, a, w, 0, :], mods[:, w, KC:2 * KC])
                        ins = V.tensor_copy(acol[:, a, w, 1, :], mods[:, w, 0:KC])
                else:
                    gain = par[:, COL["ln_g"] + (a - 1) * KC:COL["ln_g"] + a * KC]
                    bias = par[:, COL["ln_b"] + (a - 1) * KC:COL["ln_b"] + a * KC]
                    V.tensor_scalar(hcol[:, a, 0, :], gain, ALPHA, None, ALU.mult)
                    V.tensor_scalar(hcol[:, a, 1, :], bias, ALPHA, None, ALU.mult)
                    for w in range(nw):
                        V.tensor_tensor(acol[:, a, w, 0, :], mods[:, w, KC:2 * KC], gain, ALU.mult)
                        link(V.tensor_tensor(acol[:, a, w, 1, :], mods[:, w, KC:2 * KC], bias, ALU.mult))
                        ins = V.tensor_tensor(acol[:, a, w, 1, :], acol[:, a, w, 1, :], mods[:, w, 0:KC], ALU.add)
                ins.then_inc(s["mod_cols"], 1)

            def rsqrt(y, x, tmp):
                link(V.tensor_scalar(tmp.bitcast(I32), x.bitcast(I32), 1, None, ALU.logical_shift_right))
                link(V.tensor_scalar(y.bitcast(I32), tmp.bitcast(I32), -1, MAGIC, ALU.mult, ALU.add))
                for _ in range(3):
                    link(V.tensor_tensor(tmp, y, y, ALU.mult))
                    link(V.scalar_tensor_tensor(tmp, tmp, -0.5, x, ALU.mult, ALU.mult))
                    link(V.scalar_tensor_tensor(y, tmp, 1.5, y, ALU.add, ALU.mult))

            def sum_z(n, c, j, half=1):
                nt = T if n < 4 else SEQ
                job_ready(dve, j)
                if half == 1 and n in SUB_OF_FFN:
                    dve.wait_ge(s["z_ready"], z_count(n, c, 0))
                for w in range(nt // SEQ):
                    cols = slice(w * SEQ, (w + 1) * SEQ)
                    ins = V.scalar_tensor_tensor(hz[:, c, cols], jbank(j)[:, cols], acol[:, n, w, 2, c:c + 1],
                                                 hz[:, c, cols], ALU.mult, ALU.add)
                ins.then_inc(s["z_ready"], 1)
                if half == 0:
                    return
                dve.wait_ge(s["z_ready"], z_count(n, c))
                if c == 0:
                    V.tensor_copy(sum1[:, 0:nt], hz[:, c, 0:nt]).then_inc(s["s1_added"], 1)
                else:
                    dve.wait_ge(s["s1_added"], KC * n + c)
                    V.tensor_tensor(sum1[:, 0:nt], sum1[:, 0:nt], hz[:, c, 0:nt], ALU.add).then_inc(s["s1_added"], 1)

            def normalise(n, split_after):
                nt = T if n < 4 else SEQ
                tc = nt // P
                mean, var, r, nmr, tmp = (stat[:, i, 0:tc] for i in range(5))
                dve.wait_ge(s["stat_sums"], n + 1)
                V.tensor_scalar(mean, bank[4][:, 0:tc], 1.0 / D, None, ALU.mult)
                link(V.tensor_scalar(var, bank[4][:, TC:TC + tc], 1.0 / D, None, ALU.mult))
                link(V.tensor_tensor(tmp, mean, mean, ALU.mult))
                link(V.tensor_tensor(var, var, tmp, ALU.subtract))
                link(V.tensor_scalar(var, var, 0.0, LN_EPS, ALU.max, ALU.add))
                rsqrt(r, var, tmp)
                link(V.scalar_tensor_tensor(nmr, mean, -1.0, r, ALU.mult, ALU.mult))
                for which, col in ((0, r), (1, nmr)):
                    for t in range(tc):
                        ins = V.tensor_scalar(tmp_a[:, which, t * P:(t + 1) * P], ident[:], col[:, t:t + 1],
                                              None, ALU.mult)
                ins.then_inc(s["diag_ready"], 1)
                dve.wait_ge(s["stat_bcast"], n + 1)

                def lower(c):
                    na = T if n + 1 < 5 else SEQ
                    dve.wait_ge(s["ahi_ready"], KC * (n + 1) + c + 1)
                    V.tensor_tensor(a_lo[:, c, 0:na], tmp_b[:, c % 2, 0:na], a_hi[:, c, 0:na].bitcast(F32),
                                    ALU.subtract).then_inc(s["a_ready"], 1)

                for c in range(KC):
                    if n == 5 and c >= 2:
                        dve.wait_ge(s["out_ready"], c - 1)
                    link(V.tensor_tensor(tmp_a[:, c % 2, 0:nt], hz[:, c, 0:nt], bank[5][:, 0:nt], ALU.mult))
                    V.tensor_tensor(tmp_a[:, c % 2, 0:nt], tmp_a[:, c % 2, 0:nt], bank[6][:, 0:nt],
                                    ALU.add).then_inc(s["t_ready"], 1)
                    if n < 5 and c >= 1:
                        lower(c - 1)
                if n < 5:
                    lower(KC - 1)

            def ffn(fi):
                _, _, _, nt, adas = FFNS[fi]

                def hidden_step(n, m, j, i=0):
                    dve.wait_ge(s["silu_ready"], m + 1 + 2 * i)
                    dve.wait_ge(s["w_used"], n + 2 + 4 * i)
                    V.tensor_tensor(tmp_b[:, m % 2, 0:nt], tmp_a[:, m % 2, 0:nt], jbank(j0 + n - n0 + 1)[:, 0:nt],
                                    ALU.mult).then_inc(s["hraw_ready"], 1)
                    dve.wait_ge(s["hhi_ready"], m + 1 + 2 * i)
                    V.tensor_tensor(hidden(h_lo, j, i, nt), tmp_b[:, m % 2, 0:nt],
                                    hidden(h_hi, j, i, nt).bitcast(F32), ALU.subtract).then_inc(s["h_ready"], 1)

                for half in range(2):
                    a = ADA_ORDER.index(adas[half]) if adas[half] else None
                    n0, j0 = plan.base[("w1", fi, half)]
                    m0 = (2 * fi + half) * HH
                    for j in range(2):
                        split_to(n0 + 2 * j + 4)
                        hidden_step(n0 + 2 * j, m0 + j, j)
                        add_ada(a, 0, j)
                    with dve.Fori(0, 4) as i:
                        for j in (2, 3):
                            split_lo(n0 + 2 * j + 2, i)
                            split_lo(n0 + 2 * j + 3, i)
                            hidden_step(n0 + 2 * j, m0 + j, j, i)
                            add_ada(a, 1, j - 2, i)
                    pos[0] = n0 + 22
                    split_to(n0 + 24)
                    hidden_step(n0 + 20, m0 + 10, 10)
                    add_ada(a, 5, 0)
                    add_ada(a, 5, 1)
                    j1 = plan.base[("w2", fi, half)][1]
                    for oc in range(KC):
                        split_to(n0 + 22 + 2 * oc + 4)
                        sum_z(SUB_OF_FFN[fi], oc, j1 + oc, half)
                        if oc % 2 == 0:
                            add_ada(a, 6 + oc // 4, oc // 2 % 2)
                    if a is not None:
                        take_mods(a)

            def hyena_filter():
                dve.wait_ge(s["par_in"], 16)
                arg, turns, rest = (taps[0:FHID, i, 0:SEQ] for i in range(3))
                for layer in range(2):
                    j = first_job("filter_h") + layer
                    job_ready(dve, j)
                    b, fr = (("f_b1", "f_fr1"), ("f_b2", "f_fr2"))[layer]
                    link(V.tensor_scalar(arg, jbank(j)[0:FHID, 0:SEQ], pcol(b, 0, FHID), pcol(fr, 0, FHID),
                                         ALU.add, ALU.mult))
                    link(V.tensor_scalar(turns, arg, 1.0 / (2.0 * np.pi), ROUND, ALU.mult, ALU.add))
                    link(V.tensor_scalar(turns, turns, ROUND, None, ALU.subtract))
                    link(V.scalar_tensor_tensor(rest, turns, -TWO_PI_HI, arg, ALU.mult, ALU.add))
                    link(V.scalar_tensor_tensor(rest, turns, -TWO_PI_MID, rest, ALU.mult, ALU.add))
                    V.tensor_scalar(farg[:, layer, :], rest, PI_LOW, -PI_LOW, ALU.min, ALU.max)\
                        .then_inc(s["filter_h_read"], 1)
                j0 = first_job("filter_taps")
                for i in range(4):
                    job_ready(dve, j0 + i)
                    V.tensor_tensor(taps[:, i, :], jbank(j0 + i)[:], window[:, i, :], ALU.mult)\
                        .then_inc(s["taps_read"], 1)
                dve.wait_ge(s["taps_read"], 4)
                for i, op in ((0, ALU.add), (1, ALU.add), (2, ALU.subtract), (3, ALU.subtract)):
                    V.tensor_tensor(tmix[:, i, :], taps[:, i % 2, :], taps[:, 2 + i % 2, :], op)\
                        .then_inc(s["taps_mixed"], 1)
                dve.wait_ge(s["spectrum_read"], 4)
                V.memset(spec[0:1, 2, :], 0.0)
                j = first_job("nyquist")
                job_ready(dve, j)
                V.tensor_copy(spec[0:1, 4, :], jbank(j)[0:1, :]).then_inc(s["nyquist_read"], 1)
                j = first_job("tap_norm")
                job_ready(dve, j)
                V.tensor_scalar(stat[:, 0, 0:YC], jbank(j)[:, 0:YC], RMS_EPS, None, ALU.add)\
                    .then_inc(s["tap_norm_read"], 1)
                dve.wait_ge(s["tap_norm_read"], 1)
                rsqrt(kscale[:], stat[:, 0, 0:YC], stat[:, 1, 0:YC])

            def even_mixer():
                split_to(E_U + 4)
                job_ready(dve, E_J)
                V.tensor_copy(low[:], jbank(E_J)[0:2 * RANK, :]).then_inc(s["low_read"], 1)
                split_to(first_unit("e_v") + 6)
                for e in range(4):
                    j = first_job("gate_pre") + e
                    dve.wait_ge(s["gate_abs"], e + 1)
                    V.tensor_scalar(gm[:, e, :], jbank(j)[:], pcol("gate_b", e), 0.0, ALU.add, ALU.min)\
                        .then_inc(s["gate_read"], 1)
                dve.wait_ge(s["w_used"], first_unit("e_v") + 4)
                for t in range(TC):
                    V.tensor_copy(v[:, t, :], bank[4 + t][:]).then_inc(s["v_read"], 1)
                dve.wait_ge(s["rst_made"], 2)
                for e in range(4):
                    dve.wait_ge(s["gate_ln"], e + 1)
                    dve.wait_ge(s["gate_read"], e + 1)
                    link(V.tensor_tensor(gm[:, e, :], gm[:, e, :], ga[:, e, :], ALU.subtract))
                    if e < 2:
                        ins = V.tensor_tensor_scan(cum[:, e, :], rst[:], gm[:, e, :], 0.0, ALU.mult, ALU.add)
                    else:
                        ins = V.tensor_tensor_scan(cum[:, e, ::-1], rst[:], gm[:, e, ::-1], 0.0, ALU.mult, ALU.add)
                    link(ins)
                    last = (GCH - 1) * (1 - e // 2)
                    by_chunk = cum[:, e, :].rearrange("p (c t) -> p c t", t=GCH)
                    V.tensor_tensor(kst[:, e, :].rearrange("p (c t) -> p c t", t=GCH),
                                    by_chunk[:, :, last:last + 1].to_broadcast([P, NCH, GCH]), by_chunk,
                                    ALU.subtract).then_inc(s["gate_rest"], 1)
                dve.wait_ge(s["qk_read"], 4)
                for e in range(4):
                    dve.wait_ge(s["gate_exp"], e + 1)
                    q, k = qk[:, e % 2, :], qk[:, 2 + e % 2, :]
                    V.scalar_tensor_tensor(qin[:, e, :], q, GDK ** -0.5, qin[:, e, :], ALU.mult, ALU.mult)
                    V.tensor_tensor(kin[:, e, :], k, kin[:, e, :], ALU.mult)
                    V.tensor_tensor(kst[:, e, :], k, kst[:, e, :], ALU.mult).then_inc(s["gla_ops"], 1)
                for c in range(YC):
                    for part in range(3):
                        e = 3 * c + part
                        split_to(first_unit("e_hy") + e + 4)
                        j = first_job("e_hy") + e
                        dve.wait_ge(s["hy_mid"], e + 1)
                        dst = (part2[:, c, :] if part == 2 else cv[:, part, c % 2, :]).rearrange(
                            "p (w t) -> p w t", w=2)
                        u = jbank(j)[:].rearrange("p (w t) -> p w t", w=2)
                        link(V.scalar_tensor_tensor(dst[:, :, 1:SEQ], u[:, :, 0:SEQ - 1],
                                                    pcol("conv_w", YC * part + c), dst[:, :, 1:SEQ],
                                                    ALU.mult, ALU.add))
                        V.scalar_tensor_tensor(dst[:, :, 0:SEQ - 1], u[:, :, 1:SEQ],
                                               pcol("conv_w", 6 * YC + YC * part + c), dst[:, :, 0:SEQ - 1],
                                               ALU.mult, ALU.add).then_inc(s["hy_read"], 1)
                        if part == 1:
                            dve.wait_ge(s["hy_read"], e + 1)
                            V.tensor_tensor(zf[:, c, :], cv[:, 0, c % 2, :], cv[:, 1, c % 2, :], ALU.mult)\
                                .then_inc(s["zf_ready"], 1)
                dve.wait_ge(s["gla_in"], 32)
                for t in range(TC):
                    j = first_job("att") + t
                    job_ready(dve, j)
                    u = jbank(j)[:].rearrange("p (d h c) -> p d h c", d=2, h=GH)
                    lim = [bound[:, i].rearrange("p d (h c) -> p d h c", h=1).to_broadcast([P, 2, GH, GCH])
                           for i in range(2)]
                    V.tensor_tensor(attm[:, t], u, lim[0], ALU.min).then_inc(s["att_read"], 1)
                    dve.wait_ge(s["att_read"], t + 1)
                    V.tensor_tensor(attm[:, t], attm[:, t], lim[1], ALU.max).then_inc(s["att_masked"], 1)
                dve.wait_ge(s["att"], TC)
                dve.wait_ge(s["kst_turned"], TC)
                dve.wait_ge(s["ds_read"], NCH)
                order = ([4, 5, 6, 7, 0, 1, 2, 3], [7, 6, 5, 4, 3, 2, 1, 0])
                for step in range(NCH - 1):
                    if step:
                        dve.wait_ge(s["state_ready"], step)
                    for d in range(2):
                        now, nxt = order[d][step], order[d][step + 1]
                        for hp in range(2):
                            if step == 0:
                                ins = V.tensor_copy(state[:, nxt, d, hp, :], ds[:, now, d, hp, :])
                            else:
                                ins = V.scalar_tensor_tensor(state[:, nxt, d, hp, :], state[:, now, d, hp, :],
                                                             dec[:, d, hp, now:now + 1], ds[:, now, d, hp, :],
                                                             ALU.mult, ALU.add)
                    ins.then_inc(s["state_ready"], 1)
                split_to(first_unit("e_g") + 7)
                j = first_job("osq")
                job_ready(dve, j)
                V.tensor_scalar(stat[:, 0, :], jbank(j)[:, 0:16], 1.0 / GDV, RMS_EPS, ALU.mult, ALU.add)\
                    .then_inc(s["osq_read"], 1)
                dve.wait_ge(s["osq_read"], 1)
                rsqrt(stat[:, 1, :], stat[:, 0, :], stat[:, 2, :])
                for h in range(GH):
                    for t in range(TC):
                        ins = V.tensor_scalar(odiag[:, h, t * P:(t + 1) * P], ident[:],
                                              stat[:, 1, h * TC + t:h * TC + t + 1], None, ALU.mult)
                    ins.then_inc(s["odiag_ready"], 1)
                for h in range(GH):
                    j = first_job("orms") + h
                    job_ready(dve, j)
                    dve.wait_ge(s["o_copied"], h + 1)
                    dve.wait_ge(s["g_read"], h + 1)
                    V.tensor_tensor(go[:, h, :], o_sb[:, h, :], jbank(j)[:], ALU.mult).then_inc(s["orms_read"], 1)
                    dve.wait_ge(s["orms_read"], h + 1)
                    V.scalar_tensor_tensor(go[:, h, :], go[:, h, :], pcol("gla_g"), gs[:, h, :],
                                           ALU.mult, ALU.mult).then_inc(s["gla_out"], 1)
                for h in range(GH):
                    dve.wait_ge(s["cat_hi"], h + 1)
                    V.tensor_tensor(a_lo[:, YC + h, :], go[:, h, :], a_hi[:, YC + h, :].bitcast(F32),
                                    ALU.subtract).then_inc(s["cat_ready"], 1)
                for i in range(4):
                    w, r = divmod(i, 2)
                    j = first_job("dft") + 2 * i
                    job_ready(dve, j)
                    if i:
                        dve.wait_ge(s["spec_out"], i)
                    V.tensor_tensor(prod[:, 0, :], jbank(j)[:], spec[:, r, :], ALU.mult)
                    V.tensor_tensor(prod[:, 1, :], jbank(j)[:], spec[:, 2 + r, :], ALU.mult).then_inc(s["dft_read"], 1)
                    job_ready(dve, j + 1)
                    V.tensor_tensor(prod[:, 2, :], jbank(j + 1)[:], spec[:, 2 + r, :], ALU.mult)
                    V.tensor_tensor(prod[:, 3, :], jbank(j + 1)[:], spec[:, 4 if r == 0 else 1, :], ALU.mult)\
                        .then_inc(s["dft_read"], 1)
                    dve.wait_ge(s["dft_read"], 2 * i + 2)
                    V.tensor_tensor(yspec[:, r, w, :], prod[:, 0, :], prod[:, 2, :], ALU.subtract)
                    V.tensor_tensor(yspec[:, 2 + r, w, :], prod[:, 1, :], prod[:, 3, :], ALU.add)\
                        .then_inc(s["spec_out"], 1)
                for c in range(YC):
                    j = first_job("idft") + c
                    if c >= 2:
                        dve.wait_ge(s["cat_hi"], GH + c - 1)
                    link(V.tensor_scalar(yt[:, c % 2, :], zf[:, c, :], pcol("skip", c), None, ALU.mult))
                    job_ready(dve, j)
                    V.scalar_tensor_tensor(yt[:, c % 2, :], jbank(j)[:], kscale[:, c:c + 1], yt[:, c % 2, :],
                                           ALU.mult, ALU.add).then_inc(s["idft_read"], 1)
                    dve.wait_ge(s["idft_read"], c + 1)
                    V.tensor_tensor(yt[:, c % 2, :], yt[:, c % 2, :], part2[:, c, :], ALU.mult).then_inc(s["cat"], 1)
                    dve.wait_ge(s["cat_hi"], GH + c + 1)
                    V.tensor_tensor(a_lo[:, c, :], yt[:, c % 2, :], a_hi[:, c, :].bitcast(F32),
                                    ALU.subtract).then_inc(s["cat_ready"], 1)
                for c in range(KC):
                    split_to(first_unit("e_out") + c + 4)
                    sum_z(1, c, first_job("e_out") + c)

            def odd_mixer():
                cos, sin = rope[:, 0:SEQ], rope[:, SEQ:2 * SEQ]

                def both(x):
                    return x.rearrange("p (a t) -> p a t", a=1).to_broadcast([P, 2, SEQ])

                def rotate(x, turned, tmp, read, done):
                    V.tensor_tensor(tmp, turned, both(sin), ALU.mult).then_inc(s[read[0]], 1)
                    link(V.tensor_tensor(x, x, both(cos), ALU.mult))
                    ins = V.tensor_tensor(x, x, tmp, ALU.add)
                    if done:
                        ins.then_inc(s[done], 1)
                    return ins

                split_to(first_unit("o_v") + 5)
                dve.wait_ge(s["odd_in"], 16)
                dve.wait_ge(s["w_used"], first_unit("o_v") + 2)
                for t in range(TC):
                    V.tensor_copy(vo[:, t, :], bank[4 + t][:, 0:KVH * HD]).then_inc(s["ov_read"], 1)
                j = first_job("krot")
                job_ready(dve, j)
                link(rotate(kg[:, :, 0:SEQ], jbank(j)[:].rearrange("p (a t) -> p a t", a=2), krt[:],
                            ("krot_read",), None))
                j = first_job("ksq")
                job_ready(dve, j)
                nk = KVH * TC
                V.tensor_scalar(stat[:, 0, 0:nk], jbank(j)[:, 0:nk], 1.0 / HD, RMS_EPS, ALU.mult, ALU.add)\
                    .then_inc(s["ksq_read"], 1)
                dve.wait_ge(s["ksq_read"], 1)
                rsqrt(stat[:, 1, 0:nk], stat[:, 0, 0:nk], stat[:, 2, 0:nk])
                for g in range(KVH):
                    for t in range(TC):
                        ins = V.tensor_scalar(kd[:, g, t * P:(t + 1) * P], ident[:],
                                              stat[:, 1, g * TC + t:g * TC + t + 1], None, ALU.mult)
                    ins.then_inc(s["kdiag_ready"], 1)
                for g in range(KVH):
                    j = first_job("krms") + g
                    job_ready(dve, j)
                    V.tensor_tensor(kT[:, g, :], kg[:, g, :], jbank(j)[:], ALU.mult).then_inc(s["krms_read"], 1)
                for h in range(QH):
                    split_to(first_unit("o_q") + h + 4)
                for i in range(QH // 2):
                    j = first_job("qrot") + i
                    job_ready(dve, j)
                    rotate(qg[:, 2 * i:2 * i + 2, :], jbank(j)[:].rearrange("p (a t) -> p a t", a=2), qrt[:, i % 2],
                           ("qrot_read",), "q_ready")
                j = first_job("qsq")
                job_ready(dve, j)
                V.tensor_scalar(stat[:, 0, :], jbank(j)[:, 0:16], 1.0 / HD, RMS_EPS, ALU.mult, ALU.add)\
                    .then_inc(s["qsq_read"], 1)
                dve.wait_ge(s["qsq_read"], 1)
                rsqrt(stat[:, 1, :], stat[:, 0, :], stat[:, 2, :])
                V.tensor_scalar(att_stat[:, 3, :], stat[:, 1, :], -(HD ** -0.5), None, ALU.mult)
                link(V.tensor_scalar(att_stat[:, 0, :], stat[:, 1, :], HD ** -0.5, None, ALU.mult))

                def row_max(i):
                    job = plan.base[("scores", i)]
                    job_ready(dve, job)
                    link(V.tensor_reduce(stat[:, 3, i:i + 1], jbank(job)[:], AX_X, ALU.max))
                    V.tensor_tensor(att_stat[:, 1, i:i + 1], stat[:, 3, i:i + 1], att_stat[:, 3, i:i + 1],
                                    ALU.mult).then_inc(s["smax"], 1)

                row_max(0)
                for i in range(2 * QH):
                    dve.wait_ge(s["scores_read"], i + 1)
                    link(V.reciprocal(stat[:, 4, i:i + 1], att_stat[:, 2, i:i + 1]))
                    if i >= 2:
                        dve.wait_ge(s["p_turned"], i - 1)
                    V.tensor_scalar(prn[:, i % 2, :], pr[:, i % 2, :], stat[:, 4, i:i + 1], None, ALU.mult)\
                        .then_inc(s["p_ready"], 1)
                    if i + 1 < 2 * QH:
                        row_max(i + 1)
                    if i % 2 == 1:
                        h = i // 2
                        dve.wait_ge(s["attn_hi"], h + 1)
                        V.tensor_tensor(a_lo[:, h, 0:SEQ], jbank(plan.base[("attn_o", h)])[:, 0:SEQ],
                                        a_hi[:, h, 0:SEQ].bitcast(F32), ALU.subtract).then_inc(s["attn_o_read"], 1)
                for c in range(KC):
                    split_to(first_unit("o_out") + c + 4)
                    sum_z(4, c, first_job("o_out") + c)

            dve.wait_ge(s["ones_made"], 4)
            hyena_filter()
            dve.wait_ge(s["silu_c"], 1)
            for k in range(KC):
                for piece in range(2):
                    add_ada(0, k, piece)
            split_to(RING)
            take_mods(0)
            for c in range(KC):
                dve.wait_ge(s["ahi_ready"], c + 1)
                V.tensor_tensor(a_lo[:, c, :], tmp_b[:, c % 2, :], a_hi[:, c, :].bitcast(F32),
                                ALU.subtract).then_inc(s["a_ready"], 1)
            ffn(0)
            split_to(E_U + 4)
            normalise(0, None)
            even_mixer()
            split_to(plan.base[("w1", 1, 0)][0] + 4)
            normalise(1, None)
            ffn(1)
            split_to(plan.base[("w1", 2, 0)][0] + 4)
            normalise(2, None)
            ffn(2)
            split_to(O_U + 4)
            normalise(3, None)
            odd_mixer()
            split_to(plan.base[("w1", 3, 0)][0] + 4)
            normalise(4, None)
            ffn(3)
            normalise(5, None)

        @block.tensor
        def _(pe):
            def split_product(dst, w_at, x_at, first, last):
                pe.matmul(dst, w_at(0), x_at(0), start=first, stop=False)
                pe.matmul(dst, w_at(1), x_at(0), start=False, stop=False)
                return pe.matmul(dst, w_at(0), x_at(1), start=False, stop=last)

            def w_tile(n, k, width=P):
                return lambda part: (w_hi, w_lo)[part][:, n % RING, k * width:(k + 1) * width]

            def tokens(pair, k, nt):
                return lambda part: pair[part][:, k, 0:nt]

            A_IN, H_IN = (a_hi, a_lo), (h_hi, h_lo)

            def unit_split(n, i=0):
                pe.wait_ge(s["lo_ready"], n + 1 + 4 * i)

            def project(n, j, nt, i=0, order=None, each=None):
                unit_split(n, i)
                order = order or range(KC)
                for at, k in enumerate(order):
                    if each:
                        each(at, k)
                    ins = split_product(jbank(j)[:, 0:nt], w_tile(n, k), tokens(A_IN, k, nt), at == 0, at == KC - 1)
                ins.then_inc(s["w_used"], 1)

            def sum_mods(a):
                j = plan.base[("mod", a)][1]
                bank_read(pe, j)
                pe.wait_ge(s["ada_used"], PIECES * (a + 1))
                for w in range(2 if a < 5 else 1):
                    for c in range(3 * KC):
                        ins = pe.matmul(jbank(j)[:, w * 3 * KC + c:w * 3 * KC + c + 1], acc[:, w, c * P:(c + 1) * P],
                                        ones[:, 0:1], start=True, stop=True)
                ins.then_inc(s["mods_summed"], 1)

            def layer_norm(n):
                nt = T if n < 4 else SEQ
                pe.wait_ge(s["s1_added"], KC * (n + 1))
                pe.wait_ge(s["s2_added"], (KC - 1) * (n + 1))
                for col, t in ((0, sum1), (TC, sum2)):
                    for b in range(nt // P):
                        ins = pe.matmul(bank[4][:, col + b:col + b + 1], t[:, b * P:(b + 1) * P], ones[:, 0:1],
                                        start=True, stop=True)
                ins.then_inc(s["stat_sums"], 1)
                pe.wait_ge(s["diag_ready"], n + 1)
                pe.matmul(bank[5][:, 0:nt], ones[:], tmp_a[:, 0, 0:nt], start=True, stop=True)
                pe.matmul(bank[6][:, 0:nt], ones[:], tmp_a[:, 1, 0:nt], start=True, stop=True)\
                    .then_inc(s["stat_bcast"], 1)

            def ffn(fi):
                _, _, _, nt, adas = FFNS[fi]
                n_sub = SUB_OF_FFN[fi]
                for half in range(2):
                    n0, j0 = plan.base[("w1", fi, half)]
                    m0 = (2 * fi + half) * HH
                    if half == 0:
                        for u in range(4):
                            unit_split(n0 + u)
                            bank_read(pe, j0 + u)
                        for k in range(KC):
                            pe.wait_ge(s["a_ready"], KC * n_sub + k + 1)
                            for u in range(4):
                                ins = split_product(jbank(j0 + u)[:, 0:nt], w_tile(n0 + u, k), tokens(A_IN, k, nt),
                                                    k == 0, k == KC - 1)
                                if k == KC - 1:
                                    ins.then_inc(s["w_used"], 1)
                    else:
                        for u in range(4):
                            bank_read(pe, j0 + u)
                            project(n0 + u, j0 + u, nt)
                    with pe.Fori(0, 4) as i:
                        for u in range(4, 8):
                            if u % 2 == 0:
                                pe.wait_ge(s["hraw_ready"], m0 + u // 2 - 1 + 2 * i)
                            project(n0 + u, j0 + u, nt, i)
                    for u in (20, 21):
                        bank_read(pe, j0 + u)
                        project(n0 + u, j0 + u, nt)
                    n1, j1 = plan.base[("w2", fi, half)]
                    for oc in range(KC):
                        bank_read(pe, j1 + oc)
                        if oc == 0:
                            pe.wait_ge(s["h_ready"], m0 + HH - 1)
                        for piece in range(2):
                            n = n1 + 2 * oc + piece
                            unit_split(n)
                            for k in range(UW2[piece]):
                                j = piece * UW2[0] + k
                                if oc == 0 and j == HH - 1:
                                    pe.wait_ge(s["h_ready"], m0 + HH)
                                ins = split_product(jbank(j1 + oc)[:, 0:nt], w_tile(n, k), tokens(H_IN, j, nt),
                                                    j == 0, j == HH - 1)
                            ins.then_inc(s["w_used"], 1)
                    if adas[half]:
                        sum_mods(ADA_ORDER.index(adas[half]))

            def hyena_filter():
                pe.wait_ge(s["filter_in"], 96)
                pe.wait_ge(s["ones_made"], 4)
                j = first_job("filter_h")
                pe.matmul(jbank(j)[0:FHID, 0:SEQ], fw1[:], feats[:], start=True, stop=True).then_inc(s["filter_h"], 1)
                pe.wait_ge(s["filter_sin"], 1)
                pe.matmul(jbank(j + 1)[0:FHID, 0:SEQ], fw2[:], fh[0:FHID, 0, :], start=True, stop=True)\
                    .then_inc(s["filter_h"], 1)
                pe.wait_ge(s["filter_sin"], 2)
                j = first_job("filter_taps")
                for i in range(4):
                    bank_read(pe, j + i)
                    pe.matmul(jbank(j + i)[:], fh[:, 1, (i % 2) * P:(i % 2 + 1) * P],
                              fw3[:, (i // 2) * HYW:(i // 2 + 1) * HYW], start=True, stop=True)\
                        .then_inc(s["filter_taps"], 1)
                pe.wait_ge(s["taps_mixed"], 4)
                j = first_job("spectrum")
                for i in range(4):
                    bank_read(pe, j + i)
                    for b in range(2):
                        ins = pe.matmul(jbank(j + i)[:], dft0[:, b, i * P:(i + 1) * P], tmix[:, (i // 2) * 2 + b, :],
                                        start=(b == 0), stop=(b == 1))
                    ins.then_inc(s["spectrum"], 1)
                j = first_job("nyquist")
                bank_read(pe, j)
                for b in range(2):
                    ins = pe.matmul(jbank(j)[0:1, :], dft0[:, b, SEQ:SEQ + 1], tmix[:, b, :],
                                    start=(b == 0), stop=(b == 1))
                ins.then_inc(s["nyquist"], 1)
                j = first_job("tap_norm")
                bank_read(pe, j)
                pe.wait_ge(s["taps_squared"], 4)
                for c in range(YC):
                    for i in range(4):
                        ins = pe.matmul(jbank(j)[:, c:c + 1], tsq[:, i, c * P:(c + 1) * P], ones[:, 0:1],
                                        start=(i == 0), stop=(i == 3))
                ins.then_inc(s["tap_norm"], 1)

            def a_chunk(n_sub):
                return lambda at, k: pe.wait_ge(s["a_ready"], KC * n_sub + k + 1)

            def even_mixer():
                bank_read(pe, E_J)
                project(E_U, E_J, T, each=a_chunk(1))
                for e in range(4):
                    bank_read(pe, first_job("e_qk") + e)
                    project(first_unit("e_qk") + e, first_job("e_qk") + e, T)
                for m in range(4):
                    n = first_unit("e_v") + m
                    unit_split(n)
                    for kk in range(2):
                        k = 2 * m + kk
                        for t in range(TC):
                            ins = split_product(bank[4 + t][:], lambda part: A_IN[part][:, k, t * P:(t + 1) * P],
                                                w_tile(n, kk, GH * GDV), k == 0, k == KC - 1)
                    ins.then_inc(s["w_used"], 1)
                pe.wait_ge(s["low_read"], 1)
                pe.wait_ge(s["gla_in"], 32)
                for e in range(4):
                    j = first_job("gate_pre") + e
                    bank_read(pe, j)
                    pe.matmul(jbank(j)[:], gu[:, e // 2, (e % 2) * P:(e % 2 + 1) * P], low[:], start=True, stop=True)\
                        .then_inc(s["gate_pre"], 1)
                for e in range(3 * YC):
                    bank_read(pe, first_job("e_hy") + e)
                    project(first_unit("e_hy") + e, first_job("e_hy") + e, T)
                pe.wait_ge(s["gla_ops"], 4)
                for t in range(TC):
                    bank_read(pe, first_job("att") + t)
                for odd in range(2):
                    if odd:
                        pe.wait_ge(s["att_even"], 1)
                    for t in range(TC):
                        j = first_job("att") + t
                        for e in range(odd, 2 * GH, 2):
                            d, h = divmod(e, GH)
                            rows = slice(odd * GDK, (odd + 1) * GDK)
                            for b in range(2):
                                cols = slice((2 * t + b) * GCH, (2 * t + b + 1) * GCH)
                                ins = pe.matmul(jbank(j)[b * GCH:(b + 1) * GCH, e * GCH:(e + 1) * GCH],
                                                kin[rows, 2 * d + h // 2, cols], qin[rows, 2 * d + h // 2, cols],
                                                start=True, stop=True)
                        if odd:
                            ins.then_inc(s["att"], 1)
                        elif t == TC - 1:
                            ins.then_inc(s["att_even"], 1)
                for t in range(TC):
                    j = first_job("kst_turned") + t
                    bank_read(pe, j)
                    for e in range(4):
                        ins = pe.transpose(jbank(j)[:, e * P:(e + 1) * P], kst[:, e, t * P:(t + 1) * P], ident[:])
                    ins.then_inc(s["kst_turned"], 1)
                pe.wait_ge(s["v_read"], TC)
                for cc in range(NCH):
                    j = first_job("ds") + cc
                    t, b = divmod(cc, 2)
                    bank_read(pe, j)
                    pe.wait_ge(s["kst_read"], t + 1)
                    rows = slice(b * GCH, (b + 1) * GCH)
                    for d in range(2):
                        for h in range(GH):
                            at = (2 * d + h // 2) * P
                            ins = pe.matmul(jbank(j)[(h % 2) * GDK:(h % 2 + 1) * GDK, at:at + P],
                                            kstt[rows, t, d, h // 2, (h % 2) * GDK:(h % 2 + 1) * GDK],
                                            v[rows, t, h * GDV:(h + 1) * GDV], start=True, stop=True)
                    ins.then_inc(s["ds"], 1)
                for h in range(GH):
                    bank_read(pe, first_job("e_g") + h)
                    project(first_unit("e_g") + h, first_job("e_g") + h, T)
                pe.wait_ge(s["att_masked"], TC)
                pe.wait_ge(s["state_ready"], NCH - 1)
                for top in range(2):
                    if top:
                        pe.wait_ge(s["o_lower"], 1)
                    rows = slice(top * GCH, (top + 1) * GCH)
                    for h in range(GH):
                        terms = []
                        for cc in range(NCH):
                            t, b = divmod(cc, 2)
                            cols = slice(cc * GCH, (cc + 1) * GCH)
                            if b == top:
                                terms += [(cols, v[rows, t, h * GDV:(h + 1) * GDV], attm[rows, t, d, h, :])
                                          for d in range(2)]
                            if h % 2 == top:
                                terms += [(cols, state[rows, cc, d, h // 2, :], qin[rows, 2 * d + h // 2, cols])
                                          for d in range(2) if cc != (NLAT, NCH - 1)[d]]
                        for at, (cols, lhs, rhs) in enumerate(terms):
                            ins = pe.matmul(bank[4 + h][:, cols], lhs, rhs, start=(top == 0 and at == 0),
                                            stop=(top == 1 and at == len(terms) - 1), skip_group_check=True)
                        if top:
                            ins.then_inc(s["o_done"], 1)
                        elif h == GH - 1:
                            ins.then_inc(s["o_lower"], 1)
                j = first_job("osq")
                bank_read(pe, j)
                for h in range(GH):
                    pe.wait_ge(s["o_sq"], h + 1)
                    for t in range(TC):
                        ins = pe.matmul(jbank(j)[:, h * TC + t:h * TC + t + 1], osqr[:, h, t * P:(t + 1) * P],
                                        ones[:, 0:1], start=True, stop=True)
                ins.then_inc(s["osq"], 1)
                for h in range(GH):
                    j = first_job("orms") + h
                    bank_read(pe, j)
                    pe.wait_ge(s["odiag_ready"], h + 1)
                    pe.matmul(jbank(j)[:], ones[:], odiag[:, h, :], start=True, stop=True).then_inc(s["orms"], 1)
                for t in range(TC):
                    j = first_job("z_turned") + t
                    bank_read(pe, j)
                    for c in range(YC):
                        ins = pe.transpose(jbank(j)[:, c * P:(c + 1) * P], zf[:, c, t * P:(t + 1) * P], ident[:])
                    ins.then_inc(s["z_turned"], 1)
                pe.wait_ge(s["zt_read"], TC)
                pe.wait_ge(s["dft_in"], 32)
                for i in range(8):
                    w, r, part = i // 4, i // 2 % 2, i % 2
                    j = first_job("dft") + i
                    bank_read(pe, j)
                    for b in range(2):
                        ins = pe.matmul(jbank(j)[:], dft[:, b, (2 * part + r) * P:(2 * part + r + 1) * P],
                                        zt[:, 2 * w + b, :], start=(b == 0), stop=(b == 1))
                    ins.then_inc(s["dft"], 1)
                pe.wait_ge(s["spec_out"], 4)
                for c in range(YC):
                    j = first_job("idft") + c
                    bank_read(pe, j)
                    for w in range(2):
                        for f in range(4):
                            ins = pe.matmul(jbank(j)[:, w * SEQ:(w + 1) * SEQ], yspec[:, f, w, c * P:(c + 1) * P],
                                            idft[:, f, :], start=(f == 0), stop=(f == 3))
                    ins.then_inc(s["idft"], 1)
                order = list(range(YC, KC)) + list(range(YC))
                for c in range(KC):
                    bank_read(pe, first_job("e_out") + c)
                    project(first_unit("e_out") + c, first_job("e_out") + c, T, order=order,
                            each=(lambda at, k: pe.wait_ge(s["cat_ready"], at + 1)) if c == 0 else None)

            def odd_mixer():
                turn = rope[:, 2 * SEQ:2 * SEQ + P]
                for g in range(KVH):
                    bank_read(pe, O_J + g)
                    project(O_U + g, O_J + g, T, each=a_chunk(4) if g == 0 else None)
                for m in range(2):
                    n = first_unit("o_v") + m
                    unit_split(n)
                    for kk in range(4):
                        k = 4 * m + kk
                        for t in range(TC):
                            ins = split_product(bank[4 + t][:, 0:KVH * HD],
                                                lambda part: A_IN[part][:, k, t * P:(t + 1) * P],
                                                w_tile(n, kk, KVH * HD), k == 0, k == KC - 1)
                    ins.then_inc(s["w_used"], 1)
                pe.wait_ge(s["k_read"], KVH)
                pe.wait_ge(s["odd_in"], 16)
                j = first_job("krot")
                bank_read(pe, j)
                for g in range(KVH):
                    ins = pe.matmul(jbank(j)[:, g * SEQ:(g + 1) * SEQ], turn, kg[:, g, 0:SEQ], start=True, stop=True)
                ins.then_inc(s["krot"], 1)
                j = first_job("ksq")
                bank_read(pe, j)
                for g in range(KVH):
                    for t in range(TC):
                        ins = pe.matmul(jbank(j)[:, g * TC + t:g * TC + t + 1], ksqr[:, g, t * P:(t + 1) * P],
                                        ones[:, 0:1], start=True, stop=True)
                ins.then_inc(s["ksq"], 1)
                for g in range(KVH):
                    j = first_job("krms") + g
                    bank_read(pe, j)
                    pe.wait_ge(s["kdiag_ready"], g + 1)
                    pe.matmul(jbank(j)[:], ones[:], kd[:, g, :], start=True, stop=True).then_inc(s["krms"], 1)
                for h in range(QH):
                    bank_read(pe, first_job("o_q") + h)
                    project(first_unit("o_q") + h, first_job("o_q") + h, SEQ)
                for i in range(QH // 2):
                    j = first_job("qrot") + i
                    bank_read(pe, j)
                    pe.wait_ge(s["q_read"], 2 * i + 2)
                    pe.matmul(jbank(j)[:], turn, qg[:, 2 * i:2 * i + 2, :].rearrange("p a t -> p (a t)"),
                              start=True, stop=True).then_inc(s["qrot"], 1)
                j = first_job("qsq")
                bank_read(pe, j)
                for i in range(2 * QH):
                    h, qb = divmod(i, 2)
                    ins = pe.matmul(jbank(j)[:, i:i + 1], qsqr[:, h, qb * P:(qb + 1) * P], ones[:, 0:1],
                                    start=True, stop=True)
                ins.then_inc(s["qsq"], 1)
                pe.wait_ge(s["krms_read"], KVH)

                def scores(i):
                    h, qb = divmod(i, 2)
                    j = plan.base[("scores", i)]
                    bank_read(pe, j)
                    pe.wait_ge(s["q_ready"], h // 2 + 1)
                    pe.matmul(jbank(j)[:], qg[:, h, qb * P:(qb + 1) * P], kT[:, h // (QH // KVH), :],
                              start=True, stop=True).then_inc(s["scores"], 1)

                scores(0)
                for i in range(2 * QH):
                    h, qb = divmod(i, 2)
                    if i + 1 < 2 * QH:
                        scores(i + 1)
                    j = plan.base[("turned", i)]
                    bank_read(pe, j)
                    pe.wait_ge(s["p_ready"], i + 1)
                    for t in range(TC):
                        ins = pe.transpose(jbank(j)[:, t * P:(t + 1) * P], prn[:, i % 2, t * P:(t + 1) * P], ident[:])
                    ins.then_inc(s["p_turned"], 1)
                    if qb == 1:
                        j = plan.base[("attn_o", h)]
                        bank_read(pe, j)
                        pe.wait_ge(s["pt_read"], i + 1)
                        g = h // (QH // KVH)
                        for t in range(TC):
                            ins = pe.matmul(jbank(j)[:, 0:SEQ], vo[:, t, g * HD:(g + 1) * HD],
                                            pt[:, h % 2, t, :, :].rearrange("p a q -> p (a q)"),
                                            start=(t == 0), stop=(t == TC - 1))
                        ins.then_inc(s["attn_o"], 1)
                for c in range(KC):
                    bank_read(pe, first_job("o_out") + c)
                    project(first_unit("o_out") + c, first_job("o_out") + c, SEQ,
                            each=(lambda at, k: pe.wait_ge(s["attn_o_read"], k + 1)) if c == 0 else None)

            hyena_filter()
            sum_mods(0)
            ffn(0)
            layer_norm(0)
            even_mixer()
            layer_norm(1)
            ffn(1)
            layer_norm(2)
            ffn(2)
            layer_norm(3)
            odd_mixer()
            layer_norm(4)
            ffn(3)
            layer_norm(5)


def shape_tables():
    f = np.float64
    n = np.arange(SEQ, dtype=f)
    t = np.linspace(0.0, 1.0, SEQ)
    bands = np.linspace(1e-4, BANDS - 1, BANDS)
    ang = 2.0 * np.pi * n[:, None] * bands / SEQ
    feats = np.concatenate([t[:, None], np.cos(ang), -np.sin(ang)], 1).T
    deltas = np.abs(np.linspace(np.log(1e-2) / 1.5, np.log(1e-2) / 0.3, HYW))
    decay = np.exp(-t[:, None] * deltas).reshape(2, P, HYW)
    back = decay.copy()
    back[0, 0] = 0.0
    window = np.stack([decay[0], decay[1], back[0], back[1]], 1)
    fr = np.arange(SEQ, dtype=f)
    turn = 2.0 * np.pi * np.outer(n, fr) / NFREQ
    cos, sin = np.cos(turn), np.sin(turn)
    nyq = np.where(n % 2 == 0, 1.0, -1.0)
    fwd_sin, inv_sin = sin.copy(), 2.0 * sin
    fwd_sin[:, 0] = nyq
    inv_sin[:, 0] = nyq
    inv_cos = 2.0 * cos
    inv_cos[:, 0] = 1.0
    dft = np.concatenate([cos, fwd_sin], 1).reshape(2, P, NFREQ).transpose(1, 0, 2)
    inv = (np.concatenate([inv_cos, inv_sin], 1) / NFREQ).T.reshape(4, P, SEQ).transpose(1, 0, 2)
    key = np.arange(P)[:, None] % GCH
    q = np.arange(GCH)[None, :]
    keep = np.stack([key <= q, key >= q], 1)
    bound = np.stack([np.where(keep, BIG, 0.0), np.where(keep, -BIG, 0.0)], 1)
    pairs = HD // 4
    inv_freq = 10000.0 ** (-np.arange(pairs, dtype=f) / pairs)
    row, col = n // GRID_W, n % GRID_W
    angles = np.concatenate([np.outer(inv_freq, row)] * 2 + [np.outer(inv_freq, col)] * 2, 0)
    exchange = np.zeros((HD, HD))
    for b in (0, 2 * pairs):
        for r in range(pairs):
            exchange[b + pairs + r, b + r] = -1.0
            exchange[b + r, b + pairs + r] = 1.0
    rope = np.concatenate([np.cos(angles), np.sin(angles), exchange], 1)
    return [np.ascontiguousarray(a, dtype=np.float32) for a in (feats, window, dft, inv, bound, rope)]


def lay_out(i):
    cols = [
        i["ada_b"].reshape(-1, P), i["ln_g"].reshape(-1, P), i["ln_b"].reshape(-1, P),
        i["c"].reshape(-1, P), i["c_ctx"].reshape(-1, P),
        i["hyena_conv_w"].reshape(-1, P), i["hyena_conv_b"].reshape(-1, P), i["hyena_skip"].reshape(-1, P),
        i["gla_gate_b"].reshape(-1, P), i["gla_norm_g"].reshape(-1, P),
        i["attn_q_norm"].reshape(-1, P), i["attn_k_norm"].reshape(-1, P),
    ]
    cols += [np.concatenate([i[n], i[n]], 1) for n in ("hyena_f_b1", "hyena_f_fr1", "hyena_f_b2", "hyena_f_fr2")]
    par = np.concatenate(cols, 0).T
    x = np.concatenate([i["x"][0], i["ctx"][0]], 0).T.reshape(KC, P, T).transpose(1, 0, 2)

    def chunks(w):
        return w.reshape(KC, P, -1, P).transpose(2, 1, 0, 3).reshape(-1, P, KC * P)

    def rows(w, per):
        return w.reshape(KC // per, per, P, -1).transpose(0, 2, 1, 3).reshape(KC // per, P, -1)

    w1 = i["ffn_w1"].reshape(DEPTH, 2, KC, P, 2, HC, P).transpose(0, 1, 5, 4, 3, 2, 6).reshape(
        DEPTH, 2, HC, 2, P, KC * P)
    w2 = i["ffn_w2"].reshape(DEPTH, 2, 2, HH, P, KC, P).transpose(0, 1, 2, 5, 4, 3, 6).reshape(
        DEPTH, 2, 2, KC, P, HH * P)
    ada = i["ada_w"].reshape(DEPTH, KC, P, 3, 3 * D).transpose(0, 3, 1, 2, 4)
    w = i["even_w_in"][0]
    at = np.cumsum([0, 3 * HYW, GH * GDK, GH * GDK, GH * GDV, GH * GDV, 2 * RANK])
    hy, q, k, v, g, low = (w[:, a:b] for a, b in zip(at[:-1], at[1:]))
    low = np.concatenate([low, np.zeros((D, P - 2 * RANK), low.dtype)], 1)
    hy = hy.reshape(D, 3, YC, P).transpose(0, 2, 1, 3).reshape(D, -1)
    ew = chunks(np.concatenate([low, q, k, hy, g], 1))
    o = i["attn_w_in"][0]
    gu = np.zeros((2 * RANK, 2, 2 * P), np.float32)
    gu[0:RANK, 0], gu[RANK:, 1] = i["gla_gate_up"][0]
    fw3 = np.concatenate([i["hyena_f_w3"][0], i["hyena_f_b3"]], 0)
    feats, window, dft, inv, bound, rope = shape_tables()
    return [x, par, w1, w2, ada, ew, rows(v, 2), chunks(i["even_w_out"][0]),
            chunks(np.concatenate([o[:, QH * HD:(QH + KVH) * HD], o[:, :QH * HD]], 1)),
            rows(o[:, (QH + KVH) * HD:], 4), chunks(i["attn_w_out"][0]), gu,
            i["hyena_f_w1"][0], i["hyena_f_w2"][0], fw3, feats, window, dft, inv, bound, rope]


def kernel(**inputs):
    import concourse.bacc as _bacc
    from concourse.bass_utils import run_bass_kernel_spmd as _run

    nc = _bacc.Bacc("TRN2", target_bir_lowering=False, num_devices=1)
    arrays, args = {}, []
    for n, a in enumerate(lay_out({k: np.asarray(v) for k, v in inputs.items()})):
        a = np.ascontiguousarray(a)
        arrays[f"in_{n}_dram"] = a
        args.append(nc.dram_tensor(f"in_{n}_dram", a.shape, mybir.dt.from_np(a.dtype), kind="ExternalInput").ap())
    args.append(nc.dram_tensor("out_dram", (D, SEQ), F32, kind="ExternalOutput").ap())
    hybrid_trunk(nc, *args)
    r = _run(nc, [arrays], core_ids=[0])
    return np.ascontiguousarray(r.results[0]["out_dram"].T).reshape(1, SEQ, D)
```

```python
from contextlib import ExitStack

import numpy as np

import concourse.bass as bass
from concourse import mybir

ALU = mybir.AluOpType
ACT = mybir.ActivationFunctionType
F32 = mybir.dt.float32
F32R = mybir.dt.float32r
I32 = mybir.dt.int32
AX_X = mybir.AxisListType.X

P = 128
D = 1024
KC = D // P
SEQ = 256
CTX = 256
T = SEQ + CTX
TC = T // P
DEPTH = 2
FFN = ((8 * D // 3 + 255) // 256) * 256
HC = FFN // P
HH = HC // 2
ALPHA = (2.0 * DEPTH) ** 0.25
LN_EPS = 1e-5
RMS_EPS = 1e-6

HYW = D // 2
YC = HYW // P
NFREQ = 2 * SEQ
BANDS, FHID = 16, 64
EMB = 1 + 2 * BANDS

GH, GDV, GDK = 4, 128, 64
GCH = 64
NCH = T // GCH
RANK = 16
TAU = 16.0
NLAT = SEQ // GCH

HD, QH, KVH = 128, 8, 2
GRID_W = 64

RING = 4
UCOL = 1024
UW2 = (6, 5)
ADA_PIECE = 3 * D // 2
PIECES = 2 * KC
MAGIC = 0x5F3759DF
ROUND = 12582912.0
TWO_PI_HI, TWO_PI_MID = 6.28125, 0.0019353071795864769
PI_LOW = 3.1415925
BIG = float(np.finfo(np.float32).max)


def column_map():
    at, n = {}, 0
    for name, k in (
        ("ada_b", DEPTH * 9 * KC), ("ln_g", DEPTH * 3 * KC), ("ln_b", DEPTH * 3 * KC), ("c", 2 * KC),
        ("conv_w", 3 * 3 * YC), ("conv_b", 3 * YC), ("skip", YC), ("gate_b", 4), ("gla_g", 1),
        ("q_norm", 1), ("k_norm", 1), ("f_b1", 1), ("f_fr1", 1), ("f_b2", 1), ("f_fr2", 1),
    ):
        at[name] = n
        n += k
    return at, n


COL, NCOL = column_map()

FFNS = [
    (0, 0, 0, T, [(0, 1), (0, 2)]),
    (0, 1, 2, T, [(1, 0), (1, 1)]),
    (1, 0, 0, T, [(1, 2), None]),
    (1, 1, 2, SEQ, [None, None]),
]
ADA_ORDER = [(0, 0), (0, 1), (0, 2), (1, 0), (1, 1), (1, 2)]
SUB_OF_FFN = (0, 2, 3, 5)


ADA_FIRST = ((4, 1), (5, 1))
ADA_BODY = ((0, 0, 0), (0, 1, 1), (4, 0, 0))
ADA_LAST = ((6, 1), (7, 1))


def ada_before(a):
    return 0 if a == 0 else KC + PIECES * (a - 1)


def ada_loads(a, buf):
    return 0 if a == 0 else KC // 2 + (10, 6)[buf] * (a - 1)


def turned_before(a):
    return 0 if a == 0 else 2 + 4 * (a - 1)


class Plan:

    def __init__(self):
        self.units = []
        self.ready = []
        self.free = []
        self.base = {}
        self.count = {}

    def bump(self, name, n=1):
        self.count[name] = self.count.get(name, 0) + n
        return self.count[name]

    def unit(self, *u):
        self.units.append(u)
        return len(self.units)

    def job(self, ready, free):
        self.ready.append(ready)
        self.free.append(free)
        return len(self.ready) - 1

    def mark(self, name):
        self.base[name] = (len(self.units), len(self.ready))


def make_plan():
    p = Plan()

    def ffn(fi):
        layer, f = FFNS[fi][:2]
        for half in range(2):
            p.mark(("w1", fi, half))
            for j in range(HH):
                m = (fi * 2 + half) * HH + j
                for g in range(2):
                    n = p.unit("w1", (layer, f, half * HH + j, g), UCOL)
                    p.job(("w_used", n), ("hraw_ready", m + 1))
            p.mark(("w2", fi, half))
            for oc in range(KC):
                for piece in range(2):
                    n = p.unit("w2", (layer, f, half, oc, piece), UW2[piece] * P)
                p.base[("z", SUB_OF_FFN[fi], half, oc)] = p.bump("z_ready")
                p.job(("w_used", n), ("z_ready", p.count["z_ready"]))

    def proj(name, n, free):
        p.mark((name, 0))
        for e in range(n):
            if free == "z_ready":
                p.base[("z", 1 if name == "e_out" else 4, 1, e)] = p.count["z_ready"] + 1
            u = p.unit(name, (e,), UCOL)
            p.job(("w_used", u), (free, p.bump(free)))

    def jobs(name, n, free):
        p.mark((name, 0))
        for _ in range(n):
            p.job((name, p.bump(name)), (free, p.bump(free)))

    jobs("filter_h", 2, "filter_h_read")
    jobs("filter_taps", 4, "taps_read")
    jobs("spectrum", 4, "spectrum_read")
    jobs("nyquist", 1, "nyquist_read")
    jobs("tap_norm", 1, "tap_norm_read")
    ffn(0)
    proj("e_low", 1, "low_read")
    proj("e_qk", 4, "qk_read")
    p.mark(("e_v", 0))
    for m in range(4):
        p.unit("e_v", (m,), UCOL)
    jobs("gate_pre", 4, "gate_read")
    proj("e_hy", 3 * YC, "hy_read")
    jobs("att", TC, "att_read")
    jobs("kst_turned", TC, "kst_read")
    jobs("ds", NCH, "ds_read")
    proj("e_g", GH, "g_read")
    jobs("osq", 1, "osq_read")
    jobs("orms", GH, "orms_read")
    jobs("z_turned", TC, "zt_read")
    jobs("dft", 8, "dft_read")
    jobs("idft", YC, "idft_read")
    proj("e_out", KC, "z_ready")
    ffn(1)
    ffn(2)
    proj("o_k", KVH, "k_read")
    proj("o_q", QH, "q_read")
    p.mark(("o_v", 0))
    for m in range(2):
        p.unit("o_v", (m,), UCOL)
    jobs("krot", 1, "krot_read")
    jobs("ksq", 1, "ksq_read")
    jobs("qrot", QH // 2, "qrot_read")
    jobs("qsq", 1, "qsq_read")
    jobs("krms", KVH, "krms_read")
    p.mark(("attn", 0))
    for step in range(2 * QH + 1):
        if step < 2 * QH:
            p.base[("turned", step)] = p.job(("p_turned", p.bump("p_turned")), ("pt_read", p.bump("pt_read")))
        if step >= 2 and step % 2 == 0:
            p.base[("attn_o", step // 2 - 1)] = p.job(("attn_o", p.bump("attn_o")), ("attn_o_read", p.bump("attn_o_read")))
    proj("o_out", KC, "z_ready")
    ffn(3)
    return p


SEMAPHORES = (
    "x_in", "par_in", "filter_in", "taps_in", "window_in", "dft0_in", "gla_in", "dft_in", "odd_in", "ones_made", "fold_made", "rst_made", "silu_c",
    "hi_ready", "lo_ready", "w_used",
    "ada_used", "ada_product", "ada_turned", "acc_zeroed", "mods_summed", "mods_read", "mod_cols",
    "silu_ready", "hraw_ready", "hhi_ready", "h_ready",
    "mean_ready", "mean_diag", "mean_bcast", "z_ready", "s1_added", "sq_ready", "s2_added", "stat_sums", "diag_ready", "stat_bcast",
    "t_ready", "ahi_ready", "ah_ready", "a_ready", "out_ready", "out_stored", "dve_link", "act_link",
    "filter_h", "filter_h_read", "filter_sin", "filter_taps", "taps_read", "taps_mixed", "taps_squared",
    "spectrum", "spectrum_read", "nyquist", "nyquist_read", "tap_norm", "tap_norm_read",
    "low_read", "qk_read", "v_read", "gate_pre", "gate_read", "gate_abs", "gate_ln", "gate_cum",
    "gate_rest", "gate_exp", "gla_ops", "hy_mid", "hy_read", "zf_ready", "att_even", "att", "att_read", "att_masked",
    "kst_turned", "kst_read", "ds", "ds_read", "state_ready", "g_read", "o_lower", "o_done", "o_copied", "o_sq",
    "osq", "osq_read", "odiag_ready", "orms", "orms_read", "gla_out", "z_turned", "zt_read",
    "dft", "dft_read", "spec_out", "idft", "idft_read", "cat", "cat_hi", "cat_ready",
    "k_read", "ov_read", "krot", "krot_read", "ksq", "ksq_read", "kdiag_ready", "krms", "krms_read",
    "q_read", "qrot", "qrot_read", "q_ready", "qsq", "qsq_read", "scores", "scores_read", "smax",
    "p_ready", "p_turned", "pt_read", "attn_o", "attn_o_read", "attn_hi",
)


def hybrid_trunk(nc, x_t, par_d, w1_d, w2_d, ada_d, ew_d, ev_d, eo_d, ow_d, ov_d, oo_d, gu_d,
                 fw1_d, fw2_d, fw3_d, feats_d, window_d, dft_d, idft_d, bound_d, rope_d, out):
    plan = make_plan()
    NU = len(plan.units)

    with ExitStack() as ctx:
        s = {n: ctx.enter_context(nc.semaphore(n)) for n in SEMAPHORES}
        raw_in = [ctx.enter_context(nc.semaphore(f"raw_in{i}")) for i in range(RING)]
        ada_in = [ctx.enter_context(nc.semaphore(f"ada_in{i}")) for i in range(4)]

        top = [(nc.sbuf_base + 63) // 64 * 64]

        def put(name, shape, dt=F32, at=None):
            size = int(np.prod(shape[1:])) * 4
            if at is None:
                at = top[0]
                top[0] += (size + 31) // 32 * 32
            return nc.alloc_sbuf_tensor_at(name, shape, dt, offset=at)

        ident = put("ident", [P, P])
        ones = put("ones", [P, P])
        par = put("par", [P, NCOL])
        mods = put("mods", [P, 2, 3 * KC])
        acol = put("acol", [P, 6, 2, 3, KC])
        hcol = put("hcol", [P, 6, 2, KC])
        stat = put("stat", [P, 6, 16])
        att_stat = put("att_stat", [P, 4, 2 * QH])
        fold = nc.alloc_sbuf_tensor_at("fold", [P, 32], F32, offset=top[0] - 4 * 4 * 2 * QH)
        dec = put("dec", [P, 2, 2, NCH])
        kscale = put("kscale", [P, YC])
        scol = put("scol", [P, 2, KC])
        hz = put("hz", [P, KC, T])
        a_hi = put("a_hi", [P, KC, T], F32R)
        a_lo = put("a_lo", [P, KC, T], F32R)
        raw = put("raw", [P, RING, UCOL])
        w_hi = put("w_hi", [P, RING, UCOL], F32R)
        w_lo = put("w_lo", [P, RING, UCOL], F32R)
        ada = put("ada", [P, 2, ADA_PIECE])
        X = top[0]
        K = 1024
        acc = put("acc", [P, 2, 3 * D], at=X)
        h_hi = put("h_hi", [P, HH, T], F32R, at=X + 24 * K)
        h_lo = put("h_lo", [P, HH, T], F32R, at=X + 46 * K)
        tmp_a = put("tmp_a", [P, 2, T], at=X + 68 * K)
        tmp_b = put("tmp_b", [P, 2, T], at=X + 72 * K)
        sq = put("sq", [P, 2, T], at=X + 76 * K)
        sum1 = put("sum1", [P, T], at=X + 80 * K)
        sum2 = put("sum2", [P, T], at=X + 82 * K)
        spec = put("spec", [P, 5, HYW], at=X + 84 * K)
        assert X + 94 * K <= nc.sbuf_usable_end
        turned = put("turned", [P, 2, 3 * KC * 4], at=X + 94 * K)
        ada0 = put("ada0", [P, 2, ADA_PIECE], at=X + 70 * K)
        window = put("window", [P, 4, HYW], at=X + 24 * K)
        fw3 = put("fw3", [FHID + 1, 2 * HYW], at=X + 32 * K)
        fw1 = put("fw1", [EMB, FHID], at=X + 36 * K)
        fw2 = put("fw2", [FHID, FHID], at=X + 36 * K + 256)
        feats = put("feats", [EMB, SEQ], at=X + 37 * K)
        farg = put("farg", [FHID, 2, SEQ], at=X + 38 * K)
        fh = put("fh", [FHID + 1, 2, SEQ], at=X + 40 * K)
        taps = put("taps", [P, 4, HYW], at=X + 42 * K)
        tmix = put("tmix", [P, 4, HYW], at=X + 50 * K)
        dft0 = put("dft0", [P, 2, NFREQ], at=X + 58 * K)
        tsq = put("tsq", [P, 4, HYW], at=X + 62 * K)
        qk = put("qk", [P, 4, T], at=X)
        attm = put("attm", [P, TC, 2, GH, GCH], at=X)
        ga = put("ga", [P, 4, T], at=X + 8 * K)
        cv = put("cv", [P, 2, 2, T], at=X + 8 * K)
        kstt = put("kstt", [P, TC, 2, 2, P], at=X + 8 * K)
        o_sb = put("o_sb", [P, GH, T], at=X + 8 * K)
        gm = put("gm", [P, 4, T], at=X + 16 * K)
        cum = put("cum", [P, 4, T], at=X + 24 * K)
        ds = put("ds_sb", [P, NCH, 2, 2, P], at=X + 16 * K)
        gs = put("gs", [P, GH, T], at=X + 16 * K)
        go = put("go", [P, GH, T], at=X + 24 * K)
        qin = put("qin", [P, 4, T], at=X + 32 * K)
        kin = put("kin", [P, 4, T], at=X + 40 * K)
        kst = put("kst", [P, 4, T], at=X + 48 * K)
        state = put("state", [P, NCH, 2, 2, P], at=X + 40 * K)
        osqr = put("osqr", [P, GH, T], at=X + 40 * K)
        odiag = put("odiag", [P, GH, T], at=X + 48 * K)
        v = put("v", [P, TC, GH * GDV], at=X + 56 * K)
        zf = put("zf", [P, YC, T], at=X + 64 * K)
        part2 = put("part2", [P, YC, T], at=X + 72 * K)
        low = put("low", [2 * RANK, T], at=X + 80 * K)
        rst = put("rst", [P, T], at=X + 82 * K)
        bound = put("bound", [P, 2, 2, GCH], at=X + 94 * K)
        gu = put("gu", [2 * RANK, 2, 2 * P], at=X + 56 * K)
        dft = put("dft_sb", [P, 2, NFREQ], at=X)
        idft = put("idft_sb", [P, 4, SEQ], at=X + 4 * K)
        zt = put("zt", [P, TC, HYW], at=X + 32 * K)
        prod = put("prod", [P, 4, HYW], at=X + 40 * K)
        yspec = put("yspec", [P, 4, 2, HYW], at=X + 48 * K)
        yt = put("yt", [P, 2, T], at=X + 8 * K)
        kg = put("kg", [P, KVH, T], at=X)
        krt = put("krt", [P, KVH, SEQ], at=X + 4 * K)
        ksqr = put("ksqr", [P, KVH, T], at=X + 6 * K)
        kd = put("kd", [P, KVH, T], at=X + 10 * K)
        kT = put("kT", [P, KVH, T], at=X + 14 * K)
        vo = put("vo", [P, TC, KVH * HD], at=X + 18 * K)
        rope = put("rope", [P, 2 * SEQ + P], at=X + 22 * K)
        qg = put("qg", [P, QH, SEQ], at=X + 26 * K)
        qsqr = put("qsqr", [P, QH, SEQ], at=X + 34 * K)
        qrt = put("qrt", [P, 2, 2, SEQ], at=X + 42 * K)
        pr = put("pr", [P, 4, T], at=X + 62 * K)
        prn = put("prn", [P, 3, T], at=X + 70 * K)
        pt = put("pt", [P, 2, TC, 2, P], at=X + 54 * K)
        assert X + 95 * K <= nc.sbuf_usable_end

        bank = [ctx.enter_context(nc.psum_tensor(f"bank{i}", [P, T], F32)) for i in range(8)]

        def pcol(name, i=0, rows=P):
            return par[0:rows, COL[name] + i:COL[name] + i + 1]

        def jbank(j):
            return bank[j % 4]

        def wait_for(eng, pair, more=0):
            name, value = pair
            eng.wait_ge(s[name], value + more)

        def job_ready(eng, j, more=0):
            wait_for(eng, plan.ready[j], more)

        def bank_read(eng, j, more=0):
            if j >= 4:
                wait_for(eng, plan.free[j - 4], more)

        def z_count(n, c, half=1):
            return plan.base[("z", n, half, c)]

        def chunk_of(m):
            return m % HH

        def unit_source(n, i=0):
            kind, at, cols = plan.units[n]
            if kind == "w1":
                layer, f, j, g = at
                return w1_d[layer, f, j + 2 * i, g]
            if kind == "w2":
                layer, f, half, oc, piece = at
                lo = piece * UW2[0] * P
                return w2_d[layer, f, half, oc][:, lo:lo + cols]
            if kind == "e_low":
                return ew_d[0]
            if kind == "e_qk":
                return ew_d[1 + at[0]]
            if kind == "e_hy":
                return ew_d[5 + at[0]]
            if kind == "e_g":
                return ew_d[5 + 3 * YC + at[0]]
            if kind == "e_v":
                return ev_d[at[0]]
            if kind == "e_out":
                return eo_d[at[0]]
            if kind == "o_k":
                return ow_d[at[0]]
            if kind == "o_q":
                return ow_d[KVH + at[0]]
            if kind == "o_v":
                return ov_d[at[0]]
            return oo_d[at[0]]

        E_U, E_J = plan.base[("e_low", 0)]
        O_U, O_J = plan.base[("o_k", 0)]

        def first_job(name):
            return plan.base[(name, 0)][1]

        def first_unit(name):
            return plan.base[(name, 0)][0]

        def hidden(t, j, i, nt):
            if isinstance(i, int):
                return t[:, j, 0:nt]
            return t[:, bass.ds(j + 2 * i, 1), 0:nt].rearrange("p a t -> p (a t)")

        block = ctx.enter_context(nc.Block())


        @block.sync
        def _(sp):
            pos = [0]

            def load_unit(n, i=0):
                cols = plan.units[n][2]
                if n >= RING:
                    sp.wait_ge(s["lo_ready"], n - RING + 1 + 4 * i)
                sp.dma_start(raw[:, n % RING, 0:cols], unit_source(n, i)).then_inc(raw_in[n % RING], 16)

            def load_to(n):
                while pos[0] < min(n, NU):
                    load_unit(pos[0])
                    pos[0] += 1

            def load_ada(a, k, half, buf, after, i=0):
                if a is None:
                    return
                if after is not None:
                    sp.wait_ge(s["ada_used"], after)
                layer, slot = ADA_ORDER[a]
                dst = ada if buf < 2 else ada0
                sp.dma_start(dst[:, buf % 2, :], ada_d[layer, slot, k + i][:, half * ADA_PIECE:(half + 1) * ADA_PIECE])\
                    .then_inc(ada_in[buf], 16)

            for k in range(KC):
                for half in range(2):
                    if k >= 2 and half == 1:
                        sp.wait_ge(s["ada_product"], k - 1)
                    load_ada(0, k, half, 2 * (k % 2) + half, k - 1 if k >= 2 and half == 0 else None)
                if k == 3:
                    sp.dma_start(hz[:], x_t).then_inc(s["x_in"], 16)
                    load_to(1)
            load_to(RING)
            for fi, (_, _, _, _, adas) in enumerate(FFNS):
                for half in range(2):
                    a = ADA_ORDER.index(adas[half]) if adas[half] else None
                    n0, _ = plan.base[("w1", fi, half)]
                    used = ada_before(a) if a else 0
                    if a:
                        sp.wait_ge(s["ada_turned"], turned_before(a))
                        if a == 1:
                            sp.wait_ge(s["ada_product"], KC)
                    for j in range(2):
                        load_to(n0 + 4 + 2 * j)
                        load_ada(a, *ADA_FIRST[j], j, None)
                    with sp.Fori(0, 4) as i:
                        for jj in range(2):
                            load_unit(n0 + 6 + 2 * jj, i)
                            load_unit(n0 + 7 + 2 * jj, i)
                            for k, ah, buf in ADA_BODY[2 * jj:2 * jj + 2 - jj]:
                                load_ada(a, k, ah, buf, used + 2 + jj + 3 * i, i)
                    pos[0] = n0 + 22
                    load_to(n0 + 24)
                    for j in range(2):
                        load_ada(a, *ADA_LAST[j], j, used + 14)
                    load_to(n0 + 22 + 2 * KC + 2)
                if fi == 0 or fi == 2:
                    load_to(plan.base[("w1", fi + 1, 0)][0])

        @block.gpsimd
        def _(pool):
            g = nc.gpsimd
            g.memset(ident[:], 0.0).then_inc(s["ones_made"], 1)
            pool.wait_ge(s["ones_made"], 1)
            g.affine_select(out=ident[:], in_=ident[:], compare_op=ALU.not_equal, fill=1.0, base=0,
                            pattern=[[-1, P]], channel_multiplier=1).then_inc(s["ones_made"], 1)
            g.memset(ones[:], 1.0).then_inc(s["ones_made"], 1)
            g.memset(fh[:], 1.0).then_inc(s["ones_made"], 1)
            g.memset(acc[:, :, 0:ADA_PIECE], 0.0).then_inc(s["acc_zeroed"], 1)

            def add_squares(n):
                nt = T if n < 4 else SEQ
                for c in range(1, KC - 1):
                    pool.wait_ge(s["sq_ready"], KC * n + c + 1)
                    if c > 1:
                        pool.wait_ge(s["s2_added"], (KC - 2) * n + c - 1)
                    g.tensor_tensor(sum2[:, 0:nt], sum2[:, 0:nt], sq[:, c % 2, 0:nt],
                                    ALU.add).then_inc(s["s2_added"], 1)

            def zero_acc(a):
                pool.wait_ge(s["ada_turned"], turned_before(a))
                g.memset(acc[:], 0.0).then_inc(s["acc_zeroed"], 1)

            zero_acc(1)
            zero_acc(2)
            add_squares(0)
            pool.wait_ge(s["a_ready"], 2 * KC)
            pool.dma_start(bound[:], bound_d).then_inc(s["gla_in"], 16)
            pool.dma_start(gu[:], gu_d).then_inc(s["gla_in"], 16)
            g.memset(rst[:], 1.0).then_inc(s["rst_made"], 1)
            pool.wait_ge(s["rst_made"], 1)
            g.memset(rst[:].rearrange("p (c t) -> p c t", t=GCH)[:, :, 0:1], 0.0).then_inc(s["rst_made"], 1)
            pool.wait_ge(s["o_done"], GH)
            pool.dma_start(dft[:], dft_d).then_inc(s["dft_in"], 16)
            pool.dma_start(idft[:], idft_d).then_inc(s["dft_in"], 16)
            add_squares(1)
            pool.wait_ge(s["a_ready"], 3 * KC)
            zero_acc(3)
            zero_acc(4)
            add_squares(2)
            zero_acc(5)
            add_squares(3)
            pool.wait_ge(s["a_ready"], 5 * KC)
            pool.dma_start(rope[:], rope_d).then_inc(s["odd_in"], 16)
            add_squares(4)
            add_squares(5)

        @block.scalar
        def _(act):
            A = nc.scalar
            pos, links = [0], [0]

            act.dma_start(par[:], par_d).then_inc(s["par_in"], 16)
            for t, d in ((feats, feats_d), (fw1, fw1_d), (fw2, fw2_d)):
                act.dma_start(t[:], d).then_inc(s["filter_in"], 16)
            act.dma_start(fw3[:], fw3_d).then_inc(s["taps_in"], 16)
            act.dma_start(window[:], window_d).then_inc(s["window_in"], 16)
            act.dma_start(dft0[:], dft_d).then_inc(s["dft0_in"], 16)

            def link(ins):
                links[0] += 1
                ins.then_inc(s["act_link"], 1)
                act.wait_ge(s["act_link"], links[0])

            def split_hi(n, i=0):
                cols = plan.units[n][2]
                act.wait_ge(raw_in[n % RING], 16 * (n // RING + 1) + 16 * i)
                if n >= RING:
                    act.wait_ge(s["w_used"], n - RING + 1 + 4 * i)
                A.copy(w_hi[:, n % RING, 0:cols], raw[:, n % RING, 0:cols]).then_inc(s["hi_ready"], 1)

            def split_to(n):
                while pos[0] < min(n, NU):
                    split_hi(pos[0])
                    pos[0] += 1

            def apply_ln(n):
                nt = T if n < 5 else SEQ
                nz = T if n < 4 else SEQ
                act.wait_ge(s["mod_cols"], n + 1)
                for c in range(KC):
                    if n > 0:
                        act.wait_ge(s["t_ready"], KC * (n - 1) + c + 1)
                    t = tmp_a[:, c % 2, :] if n > 0 else hz[:, c, :]
                    if c >= 2:
                        act.wait_ge(s["a_ready"], KC * n + c - 1)
                    for w in range(nt // SEQ):
                        cols = slice(w * SEQ, (w + 1) * SEQ)
                        ins = A.activation(tmp_b[:, c % 2, cols], t[:, cols], ACT.Identity,
                                           bias=acol[:, n, w, 1, c:c + 1], scale=acol[:, n, w, 0, c:c + 1])
                    link(ins)
                    A.copy(a_hi[:, c, 0:nt], tmp_b[:, c % 2, 0:nt]).then_inc(s["ahi_ready"], 1)
                    A.activation(hz[:, c, 0:nz], t[:, 0:nz], ACT.Identity, bias=hcol[:, n, 1, c:c + 1],
                                 scale=hcol[:, n, 0, c:c + 1]).then_inc(s["ah_ready"], 1)

            def spread_mean(n):
                act.wait_ge(s["mean_ready"], n + 1)
                for t in range((T if n < 4 else SEQ) // P):
                    ins = A.activation(sq[:, 1, t * P:(t + 1) * P], ident[:], ACT.Copy, scale=stat[:, 0, t:t + 1])
                ins.then_inc(s["mean_diag"], 1)

            def square_z(n, c):
                nt = T if n < 4 else SEQ
                act.wait_ge(s["z_ready"], z_count(n, c))
                if c >= 3:
                    act.wait_ge(s["s2_added"], (KC - 2) * n + c - 2)
                A.activation(sum2[:, 0:nt] if c == 0 else sq[:, c % 2, 0:nt], hz[:, c, 0:nt],
                             ACT.Square).then_inc(s["sq_ready"], 1)

            def ffn(fi):
                nt = FFNS[fi][3]

                def hidden_step(n, m, j, i=0):
                    act.wait_ge(s["w_used"], n + 1 + 4 * i)
                    A.activation(tmp_a[:, m % 2, 0:nt], jbank(j0 + n - n0)[:, 0:nt], ACT.Silu)\
                        .then_inc(s["silu_ready"], 1)
                    act.wait_ge(s["hraw_ready"], m + 1 + 2 * i)
                    A.copy(hidden(h_hi, j, i, nt), tmp_b[:, m % 2, 0:nt]).then_inc(s["hhi_ready"], 1)

                for half in range(2):
                    n0, j0 = plan.base[("w1", fi, half)]
                    m0 = (2 * fi + half) * HH
                    for j in range(2):
                        split_to(n0 + 2 * j + 4)
                        hidden_step(n0 + 2 * j, m0 + j, j)
                    with act.Fori(0, 4) as i:
                        for j in (2, 3):
                            split_hi(n0 + 2 * j + 2, i)
                            split_hi(n0 + 2 * j + 3, i)
                            hidden_step(n0 + 2 * j, m0 + j, j, i)
                    pos[0] = n0 + 22
                    split_to(n0 + 24)
                    hidden_step(n0 + 20, m0 + 10, 10)
                    for oc in range(KC):
                        split_to(n0 + 22 + 2 * oc + 4)
                        if half == 1:
                            square_z(SUB_OF_FFN[fi], oc)

            def hyena_filter():
                for layer in range(2):
                    act.wait_ge(s["filter_h_read"], layer + 1)
                    act.wait_ge(s["ones_made"], 4)
                    A.activation(fh[0:FHID, layer, :], farg[:, layer, :], ACT.Sin).then_inc(s["filter_sin"], 1)
                for i in range(4):
                    act.wait_ge(s["taps_read"], i + 1)
                    A.activation(tsq[:, i, :], taps[:, i, :], ACT.Square).then_inc(s["taps_squared"], 1)
                j0 = first_job("spectrum")
                for i in range(4):
                    job_ready(act, j0 + i)
                    if i == 0:
                        A.copy(spec[:, 4, :], jbank(j0)[:])
                    A.copy(spec[:, i, :], jbank(j0 + i)[:]).then_inc(s["spectrum_read"], 1)

            def even_mixer():
                for e in range(4):
                    split_to(E_U + e + 4)
                    job_ready(act, first_job("e_qk") + e)
                    A.copy(qk[:, e, :], jbank(first_job("e_qk") + e)[:]).then_inc(s["qk_read"], 1)
                split_to(first_unit("e_v") + 6)
                for e in range(4):
                    j = first_job("gate_pre") + e
                    job_ready(act, j)
                    A.activation(ga[:, e, :], jbank(j)[:], ACT.Abs, bias=pcol("gate_b", e)).then_inc(s["gate_abs"], 1)
                act.wait_ge(s["gate_abs"], 4)
                for e in range(4):
                    ins = A.activation(ga[:, e, :], ga[:, e, :], ACT.Exp, scale=-1.0)
                link(ins)
                for e in range(4):
                    A.activation(ga[:, e, :], ga[:, e, :], ACT.Ln, bias=1.0).then_inc(s["gate_ln"], 1)
                for e in range(4):
                    act.wait_ge(s["gate_rest"], e + 1)
                    A.activation(qin[:, e, :], cum[:, e, :], ACT.Exp, scale=1.0 / TAU)
                    A.activation(kin[:, e, :], cum[:, e, :], ACT.Exp, scale=-1.0 / TAU)
                    last = (GCH - 1) * (1 - e // 2)
                    A.activation(dec[:, e // 2, e % 2, :], cum[:, e, last::GCH], ACT.Exp, scale=1.0 / TAU)
                    A.activation(kst[:, e, :], kst[:, e, :], ACT.Exp, scale=1.0 / TAU).then_inc(s["gate_exp"], 1)
                for c in range(YC):
                    for part in range(3):
                        e = 3 * c + part
                        split_to(first_unit("e_hy") + e + 4)
                        j = first_job("e_hy") + e
                        job_ready(act, j)
                        if c >= 2 and part == 0:
                            act.wait_ge(s["zf_ready"], c - 1)
                        dst = part2[:, c, :] if part == 2 else cv[:, part, c % 2, :]
                        A.activation(dst, jbank(j)[:], ACT.Identity, bias=pcol("conv_b", YC * part + c),
                                     scale=pcol("conv_w", 3 * YC + YC * part + c)).then_inc(s["hy_mid"], 1)
                act.wait_ge(s["zf_ready"], YC)
                for t in range(TC):
                    j = first_job("kst_turned") + t
                    job_ready(act, j)
                    A.copy(kstt[:, t].rearrange("p a b c -> p (a b c)"), jbank(j)[:]).then_inc(s["kst_read"], 1)
                for cc in range(NCH):
                    j = first_job("ds") + cc
                    job_ready(act, j)
                    A.copy(ds[:, cc].rearrange("p a b c -> p (a b c)"), jbank(j)[:]).then_inc(s["ds_read"], 1)
                act.wait_ge(s["state_ready"], 7)
                for h in range(GH):
                    split_to(first_unit("e_g") + h + 4)
                    j = first_job("e_g") + h
                    job_ready(act, j)
                    A.activation(gs[:, h, :], jbank(j)[:], ACT.Silu).then_inc(s["g_read"], 1)
                for h in range(GH):
                    act.wait_ge(s["o_done"], h + 1)
                    A.copy(o_sb[:, h, :], bank[4 + h][:]).then_inc(s["o_copied"], 1)
                for h in range(GH):
                    A.activation(osqr[:, h, :], bank[4 + h][:], ACT.Square).then_inc(s["o_sq"], 1)
                for h in range(GH):
                    act.wait_ge(s["gla_out"], h + 1)
                    A.copy(a_hi[:, YC + h, :], go[:, h, :]).then_inc(s["cat_hi"], 1)
                for t in range(TC):
                    j = first_job("z_turned") + t
                    job_ready(act, j)
                    A.copy(zt[:, t, :], jbank(j)[:]).then_inc(s["zt_read"], 1)
                for c in range(YC):
                    act.wait_ge(s["cat"], c + 1)
                    A.copy(a_hi[:, c, :], yt[:, c % 2, :]).then_inc(s["cat_hi"], 1)
                for c in range(KC):
                    split_to(first_unit("e_out") + c + 4)
                    square_z(1, c)

            def odd_mixer():
                for g in range(KVH):
                    split_to(O_U + g + 4)
                    j = O_J + g
                    job_ready(act, j)
                    A.activation(kg[:, g, :], jbank(j)[:], ACT.Identity, scale=pcol("k_norm"))
                    A.activation(ksqr[:, g, :], jbank(j)[:], ACT.Square).then_inc(s["k_read"], 1)
                for h in range(QH):
                    split_to(first_unit("o_q") + h + 4)
                    j = first_job("o_q") + h
                    job_ready(act, j)
                    A.activation(qg[:, h, :], jbank(j)[:, 0:SEQ], ACT.Identity, scale=pcol("q_norm"))
                    A.activation(qsqr[:, h, :], jbank(j)[:, 0:SEQ], ACT.Square).then_inc(s["q_read"], 1)

                split_to(first_unit("o_v") + 5)

                def p_exp(i):
                    act.wait_ge(s["smax"], i + 1)
                    if i >= 4:
                        act.wait_ge(s["p_ready"], i - 3)
                    A.activation(pr[:, i % 4, :], bank[4 + i % 4][:], ACT.Exp,
                                 bias=att_stat[:, 1, i:i + 1], scale=att_stat[:, 0, i:i + 1],
                                 accum_out=att_stat[:, 2, i:i + 1]).then_inc(s["scores_read"], 1)

                def take_o(h):
                    act.wait_ge(s["attn_o"], h + 1)
                    A.copy(a_hi[:, h, 0:SEQ], jbank(plan.base[("attn_o", h)])[:, 0:SEQ]).then_inc(s["attn_hi"], 1)

                p_exp(0)
                p_exp(1)
                for i in range(2 * QH):
                    if i + 2 < 2 * QH:
                        p_exp(i + 2)
                    j = plan.base[("turned", i)]
                    job_ready(act, j)
                    h, qb = divmod(i, 2)
                    if h >= 2:
                        act.wait_ge(s["attn_o"], h - 1)
                    A.copy(pt[:, h % 2, :, qb, :], jbank(j)[:].rearrange("p (c q) -> p c q", c=TC))\
                        .then_inc(s["pt_read"], 1)
                    if i % 2 == 1 and i >= 3:
                        take_o(i // 2 - 1)
                take_o(QH - 1)
                for c in range(KC):
                    split_to(first_unit("o_out") + c + 4)
                    square_z(4, c)

            act.wait_ge(s["par_in"], 16)
            A.activation(scol[:].rearrange("p a b -> p (a b)"), par[:, COL["c"]:COL["c"] + 2 * KC],
                         ACT.Silu).then_inc(s["silu_c"], 1)
            hyena_filter()
            split_to(RING)
            act.wait_ge(s["x_in"], 16)
            apply_ln(0)
            ffn(0)
            split_to(E_U + 4)
            spread_mean(0)
            apply_ln(1)
            even_mixer()
            split_to(plan.base[("w1", 1, 0)][0] + 4)
            spread_mean(1)
            apply_ln(2)
            ffn(1)
            split_to(plan.base[("w1", 2, 0)][0] + 4)
            spread_mean(2)
            apply_ln(3)
            ffn(2)
            split_to(O_U + 4)
            spread_mean(3)
            apply_ln(4)
            odd_mixer()
            split_to(plan.base[("w1", 3, 0)][0] + 4)
            spread_mean(4)
            apply_ln(5)
            ffn(3)
            spread_mean(5)
            for c in range(KC):
                act.wait_ge(s["t_ready"], 5 * KC + c + 1)
                A.activation(hz[:, c, 0:SEQ], tmp_a[:, c % 2, 0:SEQ], ACT.Identity,
                             bias=pcol("ln_b", 5 * KC + c), scale=pcol("ln_g", 5 * KC + c)).then_inc(s["out_ready"], 1)
                act.wait_ge(s["out_ready"], c + 1)
                act.dma_start(out[c * P:(c + 1) * P, :], hz[:, c, 0:SEQ]).then_inc(s["out_stored"], 16)
            act.wait_ge(s["out_stored"], 16 * KC)

        @block.vector
        def _(dve):
            V = nc.vector
            pos, links = [0], [0]

            def link(ins):
                links[0] += 1
                ins.then_inc(s["dve_link"], 1)
                dve.wait_ge(s["dve_link"], links[0])

            def split_lo(n, i=0):
                cols = plan.units[n][2]
                dve.wait_ge(s["hi_ready"], n + 1 + 4 * i)
                V.tensor_tensor(w_lo[:, n % RING, 0:cols], raw[:, n % RING, 0:cols],
                                w_hi[:, n % RING, 0:cols].bitcast(F32), ALU.subtract).then_inc(s["lo_ready"], 1)

            def split_to(n):
                while pos[0] < min(n, NU):
                    split_lo(pos[0])
                    pos[0] += 1

            def add_ada(a, k, half, buf, before, loads, i=0):
                if a is None:
                    return
                if isinstance(before, int) and before == ada_before(a):
                    dve.wait_ge(s["acc_zeroed"], a + 1)
                else:
                    dve.wait_ge(s["ada_used"], before)
                dve.wait_ge(ada_in[buf], loads)
                cols = slice(half * ADA_PIECE, (half + 1) * ADA_PIECE)
                src = ada if buf < 2 else ada0
                for w in range(2 if a < 5 else 1):
                    scalar = scol[:, w, k:k + 1] if isinstance(i, int) else scol[:, w, bass.ds(k + i, 1)]
                    ins = V.scalar_tensor_tensor(acc[:, w, cols], src[:, buf % 2, :], scalar, acc[:, w, cols],
                                                 ALU.mult, ALU.add)
                ins.then_inc(s["ada_used"], 1)

            def turn_ada(a, x):
                if a is None or (a in (0, 5) and x >= 2):
                    return
                w, half = (x, 0) if a == 0 else divmod(x, 2)
                dve.wait_ge(s["ada_used"], ada_before(a + 1))
                if a == 0:
                    dve.wait_ge(s["ada_product"], KC)
                if x >= 2:
                    dve.wait_ge(s["ada_turned"], turned_before(a) + x - 1)
                room = ada[:, x % 2, :]
                link(V.transpose(room, acc[:, w, half * ADA_PIECE:(half + 1) * ADA_PIECE]))
                n = ADA_PIECE // 32
                V.tensor_reduce(turned[:, w, half * n:(half + 1) * n], room.rearrange("p (b j) -> p b j", j=32),
                                AX_X, ALU.add).then_inc(s["ada_turned"], 1)

            def take_mods(a):
                nw = 2 if a < 5 else 1
                dve.wait_ge(s["mods_summed"], a + 1)
                half = 3 * KC // 2
                for w in range(nw):
                    for x in range(2):
                        at = w * 3 * KC + x * half
                        bias = COL["ada_b"] + a * 3 * KC + x * half
                        ins = V.tensor_tensor(mods[:, w, x * half:(x + 1) * half],
                                              bank[6 if a == 0 and x == 1 else 7][:, at:at + half],
                                              par[:, bias:bias + half], ALU.add)
                ins.then_inc(s["mods_read"], 1)
                dve.wait_ge(s["mods_read"], a + 1)
                for w in range(nw):
                    ins = V.tensor_scalar(mods[:, w, KC:2 * KC], mods[:, w, KC:2 * KC], 1.0, None, ALU.add)
                    V.tensor_scalar(acol[:, a, w, 2, :], mods[:, w, 2 * KC:3 * KC], 1.0 if a in (1, 4) else 0.5,
                                    None, ALU.mult)
                link(V.memset(hcol[:, a, 0, :], ALPHA))
                if a == 0:
                    V.memset(hcol[:, a, 1, :], 0.0)
                    for w in range(nw):
                        V.tensor_copy(acol[:, a, w, 0, :], mods[:, w, KC:2 * KC])
                        ins = V.tensor_copy(acol[:, a, w, 1, :], mods[:, w, 0:KC])
                else:
                    gain = par[:, COL["ln_g"] + (a - 1) * KC:COL["ln_g"] + a * KC]
                    bias = par[:, COL["ln_b"] + (a - 1) * KC:COL["ln_b"] + a * KC]
                    V.tensor_scalar(hcol[:, a, 0, :], gain, ALPHA, None, ALU.mult)
                    V.tensor_scalar(hcol[:, a, 1, :], bias, ALPHA, None, ALU.mult)
                    for w in range(nw):
                        V.tensor_tensor(acol[:, a, w, 0, :], mods[:, w, KC:2 * KC], gain, ALU.mult)
                        link(V.tensor_tensor(acol[:, a, w, 1, :], mods[:, w, KC:2 * KC], bias, ALU.mult))
                        ins = V.tensor_tensor(acol[:, a, w, 1, :], acol[:, a, w, 1, :], mods[:, w, 0:KC], ALU.add)
                ins.then_inc(s["mod_cols"], 1)

            def rsqrt(y, x, tmp):
                link(V.tensor_scalar(tmp.bitcast(I32), x.bitcast(I32), 1, None, ALU.logical_shift_right))
                link(V.tensor_scalar(y.bitcast(I32), tmp.bitcast(I32), -1, MAGIC, ALU.mult, ALU.add))
                for _ in range(3):
                    link(V.tensor_tensor(tmp, y, y, ALU.mult))
                    link(V.scalar_tensor_tensor(tmp, tmp, -0.5, x, ALU.mult, ALU.mult))
                    link(V.scalar_tensor_tensor(y, tmp, 1.5, y, ALU.add, ALU.mult))

            def sum_z(n, c, j, half=1):
                nt = T if n < 4 else SEQ
                job_ready(dve, j)
                if c == 0:
                    dve.wait_ge(s["ah_ready"], KC * (n + 1))
                if half == 1 and n in SUB_OF_FFN:
                    dve.wait_ge(s["z_ready"], z_count(n, c, 0))
                for w in range(nt // SEQ):
                    cols = slice(w * SEQ, (w + 1) * SEQ)
                    ins = V.scalar_tensor_tensor(hz[:, c, cols], jbank(j)[:, cols], acol[:, n, w, 2, c:c + 1],
                                                 hz[:, c, cols], ALU.mult, ALU.add)
                ins.then_inc(s["z_ready"], 1)
                if half == 0:
                    return
                if c == KC - 1:
                    return
                dve.wait_ge(s["z_ready"], z_count(n, c))
                if c == 0:
                    V.tensor_copy(sum1[:, 0:nt], hz[:, c, 0:nt]).then_inc(s["s1_added"], 1)
                else:
                    dve.wait_ge(s["s1_added"], (KC - 1) * n + c)
                    V.tensor_tensor(sum1[:, 0:nt], sum1[:, 0:nt], hz[:, c, 0:nt], ALU.add).then_inc(s["s1_added"], 1)

            def normalise(n):
                nt = T if n < 4 else SEQ
                tc = nt // P
                mean, var, r, tmp = (stat[:, i, 0:tc] for i in range(4))
                dve.wait_ge(s["stat_sums"], n + 1)
                V.tensor_scalar(mean, bank[4][:, 0:tc], 1.0 / D, None, ALU.mult).then_inc(s["mean_ready"], 1)
                dve.wait_ge(s["mean_ready"], n + 1)
                link(V.scalar_tensor_tensor(tmp, mean, -1.0, mean, ALU.mult, ALU.mult))
                link(V.scalar_tensor_tensor(var, bank[4][:, TC:TC + tc], 1.0 / D, tmp, ALU.mult, ALU.add))
                link(V.tensor_scalar(var, var, 0.0, LN_EPS, ALU.max, ALU.add))
                rsqrt(r, var, tmp)
                for t in range(tc):
                    ins = V.tensor_scalar(sq[:, 0, t * P:(t + 1) * P], ident[:], r[:, t:t + 1], None, ALU.mult)
                ins.then_inc(s["diag_ready"], 1)
                dve.wait_ge(s["mean_bcast"], n + 1)

                def centre(c):
                    if n == 5 and c >= 2:
                        dve.wait_ge(s["out_ready"], c - 1)
                    elif c >= 2:
                        dve.wait_ge(s["ah_ready"], KC * (n + 1) + c - 1)
                    return V.tensor_tensor(tmp_a[:, c % 2, 0:nt], hz[:, c, 0:nt], bank[6][:, 0:nt], ALU.subtract)

                centre(0)
                link(centre(1))
                dve.wait_ge(s["stat_bcast"], n + 1)

                def lower(c):
                    na = T if n + 1 < 5 else SEQ
                    dve.wait_ge(s["ahi_ready"], KC * (n + 1) + c + 1)
                    V.tensor_tensor(a_lo[:, c, 0:na], tmp_b[:, c % 2, 0:na], a_hi[:, c, 0:na].bitcast(F32),
                                    ALU.subtract).then_inc(s["a_ready"], 1)

                for c in range(KC):
                    if c >= 2:
                        link(centre(c))
                    V.tensor_tensor(tmp_a[:, c % 2, 0:nt], tmp_a[:, c % 2, 0:nt], bank[5][:, 0:nt],
                                    ALU.mult).then_inc(s["t_ready"], 1)
                    if n < 5 and c >= 1:
                        lower(c - 1)
                if n < 5:
                    lower(KC - 1)

            def ffn(fi):
                _, _, _, nt, adas = FFNS[fi]

                def hidden_step(n, m, j, i=0):
                    dve.wait_ge(s["silu_ready"], m + 1 + 2 * i)
                    dve.wait_ge(s["w_used"], n + 2 + 4 * i)
                    V.tensor_tensor(tmp_b[:, m % 2, 0:nt], tmp_a[:, m % 2, 0:nt], jbank(j0 + n - n0 + 1)[:, 0:nt],
                                    ALU.mult).then_inc(s["hraw_ready"], 1)
                    dve.wait_ge(s["hhi_ready"], m + 1 + 2 * i)
                    V.tensor_tensor(hidden(h_lo, j, i, nt), tmp_b[:, m % 2, 0:nt],
                                    hidden(h_hi, j, i, nt).bitcast(F32), ALU.subtract).then_inc(s["h_ready"], 1)

                for half in range(2):
                    a = ADA_ORDER.index(adas[half]) if adas[half] else None
                    n0, j0 = plan.base[("w1", fi, half)]
                    m0 = (2 * fi + half) * HH
                    used = ada_before(a) if a else 0
                    for j in range(2):
                        split_to(n0 + 2 * j + 4)
                        hidden_step(n0 + 2 * j, m0 + j, j)
                        if a:
                            add_ada(a, *ADA_FIRST[j], j, used + j, 16 * (ada_loads(a, j) + 1))
                    with dve.Fori(0, 4) as i:
                        for j in (2, 3):
                            split_lo(n0 + 2 * j + 2, i)
                            split_lo(n0 + 2 * j + 3, i)
                            hidden_step(n0 + 2 * j, m0 + j, j, i)
                            for x in ((0,), (1, 2))[j - 2] if a else ():
                                k, ah, buf = ADA_BODY[x]
                                loads = ada_loads(a, buf) + (2, 2, 3)[x]
                                add_ada(a, k, ah, buf, used + 2 + x + 3 * i, 16 * loads + 16 * (2, 1, 2)[x] * i, i)
                    pos[0] = n0 + 22
                    split_to(n0 + 24)
                    hidden_step(n0 + 20, m0 + 10, 10)
                    if a:
                        add_ada(a, *ADA_LAST[0], 0, used + 14, 16 * ada_loads(a + 1, 0))
                    j1 = plan.base[("w2", fi, half)][1]
                    for oc in range(KC):
                        split_to(n0 + 22 + 2 * oc + 4)
                        sum_z(SUB_OF_FFN[fi], oc, j1 + oc, half)
                        if a and oc == 0:
                            add_ada(a, *ADA_LAST[1], 1, used + 15, 16 * ada_loads(a + 1, 1))
                        if a and 1 <= oc <= 4:
                            turn_ada(a, oc - 1)
                        if a and oc == 6:
                            take_mods(a)

            def filter_and_slot_0():
                def rows(k):
                    add_ada(0, k, 0, 2 * (k % 2), k, 16 * (k // 2 + 1))

                dve.wait_ge(s["par_in"], 16)
                dve.wait_ge(s["silu_c"], 1)
                rows(0)
                arg, turns, rest = (taps[0:FHID, i, 0:SEQ] for i in range(3))
                for layer in range(2):
                    j = first_job("filter_h") + layer
                    job_ready(dve, j)
                    b, fr = (("f_b1", "f_fr1"), ("f_b2", "f_fr2"))[layer]
                    link(V.tensor_scalar(arg, jbank(j)[0:FHID, 0:SEQ], pcol(b, 0, FHID), pcol(fr, 0, FHID),
                                         ALU.add, ALU.mult))
                    link(V.tensor_scalar(turns, arg, 1.0 / (2.0 * np.pi), ROUND, ALU.mult, ALU.add))
                    link(V.tensor_scalar(turns, turns, ROUND, None, ALU.subtract))
                    link(V.scalar_tensor_tensor(rest, turns, -TWO_PI_HI, arg, ALU.mult, ALU.add))
                    link(V.scalar_tensor_tensor(rest, turns, -TWO_PI_MID, rest, ALU.mult, ALU.add))
                    V.tensor_scalar(farg[:, layer, :], rest, PI_LOW, -PI_LOW, ALU.min, ALU.max)\
                        .then_inc(s["filter_h_read"], 1)
                    rows(layer + 1)
                j0 = first_job("filter_taps")
                dve.wait_ge(s["window_in"], 16)
                for i in range(4):
                    job_ready(dve, j0 + i)
                    V.tensor_tensor(taps[:, i, :], jbank(j0 + i)[:], window[:, i, :], ALU.mult)\
                        .then_inc(s["taps_read"], 1)
                dve.wait_ge(s["taps_read"], 4)
                for i, op in ((0, ALU.add), (1, ALU.add), (2, ALU.subtract), (3, ALU.subtract)):
                    V.tensor_tensor(tmix[:, i, :], taps[:, i % 2, :], taps[:, 2 + i % 2, :], op)\
                        .then_inc(s["taps_mixed"], 1)
                for k in range(3, KC):
                    rows(k)
                split_to(RING)
                for x in range(2):
                    turn_ada(0, x)
                dve.wait_ge(s["spectrum_read"], 4)
                V.memset(spec[0:1, 2, :], 0.0)
                j = first_job("nyquist")
                job_ready(dve, j)
                V.tensor_copy(spec[0:1, 4, :], jbank(j)[0:1, :]).then_inc(s["nyquist_read"], 1)
                j = first_job("tap_norm")
                job_ready(dve, j)
                V.tensor_scalar(stat[:, 0, 0:YC], jbank(j)[:, 0:YC], RMS_EPS, None, ALU.add)\
                    .then_inc(s["tap_norm_read"], 1)
                dve.wait_ge(s["tap_norm_read"], 1)
                rsqrt(kscale[:], stat[:, 0, 0:YC], stat[:, 1, 0:YC])

            def even_mixer():
                split_to(E_U + 4)
                job_ready(dve, E_J)
                V.tensor_copy(low[:], jbank(E_J)[0:2 * RANK, :]).then_inc(s["low_read"], 1)
                split_to(first_unit("e_v") + 6)
                for e in range(4):
                    j = first_job("gate_pre") + e
                    dve.wait_ge(s["gate_abs"], e + 1)
                    V.tensor_scalar(gm[:, e, :], jbank(j)[:], pcol("gate_b", e), 0.0, ALU.add, ALU.min)\
                        .then_inc(s["gate_read"], 1)
                dve.wait_ge(s["w_used"], first_unit("e_v") + 4)
                for t in range(TC):
                    V.tensor_copy(v[:, t, :], bank[4 + t][:]).then_inc(s["v_read"], 1)
                dve.wait_ge(s["rst_made"], 2)
                for e in range(4):
                    dve.wait_ge(s["gate_ln"], e + 1)
                    dve.wait_ge(s["gate_read"], e + 1)
                    link(V.tensor_tensor(gm[:, e, :], gm[:, e, :], ga[:, e, :], ALU.subtract))
                    if e < 2:
                        ins = V.tensor_tensor_scan(cum[:, e, :], rst[:], gm[:, e, :], 0.0, ALU.mult, ALU.add)
                    else:
                        ins = V.tensor_tensor_scan(cum[:, e, ::-1], rst[:], gm[:, e, ::-1], 0.0, ALU.mult, ALU.add)
                    link(ins)
                    last = (GCH - 1) * (1 - e // 2)
                    by_chunk = cum[:, e, :].rearrange("p (c t) -> p c t", t=GCH)
                    V.tensor_tensor(kst[:, e, :].rearrange("p (c t) -> p c t", t=GCH),
                                    by_chunk[:, :, last:last + 1].to_broadcast([P, NCH, GCH]), by_chunk,
                                    ALU.subtract).then_inc(s["gate_rest"], 1)
                dve.wait_ge(s["qk_read"], 4)
                for e in range(4):
                    dve.wait_ge(s["gate_exp"], e + 1)
                    q, k = qk[:, e % 2, :], qk[:, 2 + e % 2, :]
                    V.scalar_tensor_tensor(qin[:, e, :], q, GDK ** -0.5, qin[:, e, :], ALU.mult, ALU.mult)
                    V.tensor_tensor(kin[:, e, :], k, kin[:, e, :], ALU.mult)
                    V.tensor_tensor(kst[:, e, :], k, kst[:, e, :], ALU.mult).then_inc(s["gla_ops"], 1)
                for c in range(YC):
                    for part in range(3):
                        e = 3 * c + part
                        split_to(first_unit("e_hy") + e + 4)
                        j = first_job("e_hy") + e
                        dve.wait_ge(s["hy_mid"], e + 1)
                        dst = (part2[:, c, :] if part == 2 else cv[:, part, c % 2, :]).rearrange(
                            "p (w t) -> p w t", w=2)
                        u = jbank(j)[:].rearrange("p (w t) -> p w t", w=2)
                        link(V.scalar_tensor_tensor(dst[:, :, 1:SEQ], u[:, :, 0:SEQ - 1],
                                                    pcol("conv_w", YC * part + c), dst[:, :, 1:SEQ],
                                                    ALU.mult, ALU.add))
                        V.scalar_tensor_tensor(dst[:, :, 0:SEQ - 1], u[:, :, 1:SEQ],
                                               pcol("conv_w", 6 * YC + YC * part + c), dst[:, :, 0:SEQ - 1],
                                               ALU.mult, ALU.add).then_inc(s["hy_read"], 1)
                        if part == 1:
                            dve.wait_ge(s["hy_read"], e + 1)
                            V.tensor_tensor(zf[:, c, :], cv[:, 0, c % 2, :], cv[:, 1, c % 2, :], ALU.mult)\
                                .then_inc(s["zf_ready"], 1)
                dve.wait_ge(s["gla_in"], 32)
                for t in range(TC):
                    j = first_job("att") + t
                    job_ready(dve, j)
                    u = jbank(j)[:].rearrange("p (d h c) -> p d h c", d=2, h=GH)
                    lim = [bound[:, i].rearrange("p d (h c) -> p d h c", h=1).to_broadcast([P, 2, GH, GCH])
                           for i in range(2)]
                    V.tensor_tensor(attm[:, t], u, lim[0], ALU.min).then_inc(s["att_read"], 1)
                    dve.wait_ge(s["att_read"], t + 1)
                    V.tensor_tensor(attm[:, t], attm[:, t], lim[1], ALU.max).then_inc(s["att_masked"], 1)
                dve.wait_ge(s["att"], TC)
                dve.wait_ge(s["kst_turned"], TC)
                dve.wait_ge(s["ds_read"], NCH)
                order = ([4, 5, 6, 7, 0, 1, 2, 3], [7, 6, 5, 4, 3, 2, 1, 0])
                for step in range(NCH - 1):
                    if step:
                        dve.wait_ge(s["state_ready"], step)
                    for d in range(2):
                        now, nxt = order[d][step], order[d][step + 1]
                        for hp in range(2):
                            if step == 0:
                                ins = V.tensor_copy(state[:, nxt, d, hp, :], ds[:, now, d, hp, :])
                            else:
                                ins = V.scalar_tensor_tensor(state[:, nxt, d, hp, :], state[:, now, d, hp, :],
                                                             dec[:, d, hp, now:now + 1], ds[:, now, d, hp, :],
                                                             ALU.mult, ALU.add)
                    ins.then_inc(s["state_ready"], 1)
                split_to(first_unit("e_g") + 7)
                j = first_job("osq")
                job_ready(dve, j)
                V.tensor_scalar(stat[:, 0, :], jbank(j)[:, 0:16], 1.0 / GDV, RMS_EPS, ALU.mult, ALU.add)\
                    .then_inc(s["osq_read"], 1)
                dve.wait_ge(s["osq_read"], 1)
                rsqrt(stat[:, 1, :], stat[:, 0, :], stat[:, 2, :])
                for h in range(GH):
                    for t in range(TC):
                        ins = V.tensor_scalar(odiag[:, h, t * P:(t + 1) * P], ident[:],
                                              stat[:, 1, h * TC + t:h * TC + t + 1], None, ALU.mult)
                    ins.then_inc(s["odiag_ready"], 1)
                for h in range(GH):
                    j = first_job("orms") + h
                    job_ready(dve, j)
                    dve.wait_ge(s["o_copied"], h + 1)
                    dve.wait_ge(s["g_read"], h + 1)
                    V.tensor_tensor(go[:, h, :], o_sb[:, h, :], jbank(j)[:], ALU.mult).then_inc(s["orms_read"], 1)
                    dve.wait_ge(s["orms_read"], h + 1)
                    V.scalar_tensor_tensor(go[:, h, :], go[:, h, :], pcol("gla_g"), gs[:, h, :],
                                           ALU.mult, ALU.mult).then_inc(s["gla_out"], 1)
                for h in range(GH):
                    dve.wait_ge(s["cat_hi"], h + 1)
                    V.tensor_tensor(a_lo[:, YC + h, :], go[:, h, :], a_hi[:, YC + h, :].bitcast(F32),
                                    ALU.subtract).then_inc(s["cat_ready"], 1)
                for i in range(4):
                    w, r = divmod(i, 2)
                    j = first_job("dft") + 2 * i
                    job_ready(dve, j)
                    if i:
                        dve.wait_ge(s["spec_out"], i)
                    V.tensor_tensor(prod[:, 0, :], jbank(j)[:], spec[:, r, :], ALU.mult)
                    V.tensor_tensor(prod[:, 1, :], jbank(j)[:], spec[:, 2 + r, :], ALU.mult).then_inc(s["dft_read"], 1)
                    job_ready(dve, j + 1)
                    V.tensor_tensor(prod[:, 2, :], jbank(j + 1)[:], spec[:, 2 + r, :], ALU.mult)
                    V.tensor_tensor(prod[:, 3, :], jbank(j + 1)[:], spec[:, 4 if r == 0 else 1, :], ALU.mult)\
                        .then_inc(s["dft_read"], 1)
                    dve.wait_ge(s["dft_read"], 2 * i + 2)
                    V.tensor_tensor(yspec[:, r, w, :], prod[:, 0, :], prod[:, 2, :], ALU.subtract)
                    V.tensor_tensor(yspec[:, 2 + r, w, :], prod[:, 1, :], prod[:, 3, :], ALU.add)\
                        .then_inc(s["spec_out"], 1)
                for c in range(YC):
                    j = first_job("idft") + c
                    if c >= 2:
                        dve.wait_ge(s["cat_hi"], GH + c - 1)
                    link(V.tensor_scalar(yt[:, c % 2, :], zf[:, c, :], pcol("skip", c), None, ALU.mult))
                    job_ready(dve, j)
                    V.scalar_tensor_tensor(yt[:, c % 2, :], jbank(j)[:], kscale[:, c:c + 1], yt[:, c % 2, :],
                                           ALU.mult, ALU.add).then_inc(s["idft_read"], 1)
                    dve.wait_ge(s["idft_read"], c + 1)
                    V.tensor_tensor(yt[:, c % 2, :], yt[:, c % 2, :], part2[:, c, :], ALU.mult).then_inc(s["cat"], 1)
                    dve.wait_ge(s["cat_hi"], GH + c + 1)
                    V.tensor_tensor(a_lo[:, c, :], yt[:, c % 2, :], a_hi[:, c, :].bitcast(F32),
                                    ALU.subtract).then_inc(s["cat_ready"], 1)
                for c in range(KC):
                    split_to(first_unit("e_out") + c + 4)
                    sum_z(1, c, first_job("e_out") + c)

            def odd_mixer():
                cos, sin = rope[:, 0:SEQ], rope[:, SEQ:2 * SEQ]

                def both(x):
                    return x.rearrange("p (a t) -> p a t", a=1).to_broadcast([P, 2, SEQ])

                def rotate(x, turned, tmp, read, done):
                    V.tensor_tensor(tmp, turned, both(sin), ALU.mult).then_inc(s[read[0]], 1)
                    link(V.tensor_tensor(x, x, both(cos), ALU.mult))
                    ins = V.tensor_tensor(x, x, tmp, ALU.add)
                    if done:
                        ins.then_inc(s[done], 1)
                    return ins

                for e in range(KVH + QH + 2):
                    split_to(O_U + e + 4)
                dve.wait_ge(s["odd_in"], 16)
                dve.wait_ge(s["w_used"], first_unit("o_v") + 2)
                for t in range(TC):
                    V.tensor_copy(vo[:, t, :], bank[4 + t][:, 0:KVH * HD]).then_inc(s["ov_read"], 1)
                j = first_job("krot")
                job_ready(dve, j)
                link(rotate(kg[:, :, 0:SEQ], jbank(j)[:].rearrange("p (a t) -> p a t", a=2), krt[:],
                            ("krot_read",), None))
                j = first_job("ksq")
                job_ready(dve, j)
                nk = KVH * TC
                V.tensor_scalar(stat[:, 0, 0:nk], jbank(j)[:, 0:nk], 1.0 / HD, RMS_EPS, ALU.mult, ALU.add)\
                    .then_inc(s["ksq_read"], 1)
                dve.wait_ge(s["ksq_read"], 1)
                rsqrt(stat[:, 1, 0:nk], stat[:, 0, 0:nk], stat[:, 2, 0:nk])
                for g in range(KVH):
                    for t in range(TC):
                        ins = V.tensor_scalar(kd[:, g, t * P:(t + 1) * P], ident[:],
                                              stat[:, 1, g * TC + t:g * TC + t + 1], None, ALU.mult)
                    ins.then_inc(s["kdiag_ready"], 1)
                for i in range(QH // 2):
                    j = first_job("qrot") + i
                    job_ready(dve, j)
                    rotate(qg[:, 2 * i:2 * i + 2, :], jbank(j)[:].rearrange("p (a t) -> p a t", a=2), qrt[:, i % 2],
                           ("qrot_read",), "q_ready")
                j = first_job("qsq")
                job_ready(dve, j)
                V.tensor_scalar(stat[:, 0, :], jbank(j)[:, 0:16], 1.0 / HD, RMS_EPS, ALU.mult, ALU.add)\
                    .then_inc(s["qsq_read"], 1)
                dve.wait_ge(s["qsq_read"], 1)
                rsqrt(stat[:, 1, :], stat[:, 0, :], stat[:, 2, :])
                V.tensor_scalar(att_stat[:, 3, :], stat[:, 1, :], -(HD ** -0.5), None, ALU.mult)
                link(V.tensor_scalar(att_stat[:, 0, :], stat[:, 1, :], HD ** -0.5, None, ALU.mult))

                for g in range(KVH):
                    j = first_job("krms") + g
                    job_ready(dve, j)
                    V.tensor_tensor(kT[:, g, :], kg[:, g, :], jbank(j)[:], ALU.mult).then_inc(s["krms_read"], 1)

                def row_max(i):
                    dve.wait_ge(s["scores"], i + 1)
                    link(V.tensor_reduce(stat[:, 3, i:i + 1], bank[4 + i % 4][:], AX_X, ALU.max))
                    V.tensor_tensor(att_stat[:, 1, i:i + 1], stat[:, 3, i:i + 1], att_stat[:, 3, i:i + 1],
                                    ALU.mult).then_inc(s["smax"], 1)

                def lower_o(h):
                    dve.wait_ge(s["attn_hi"], h + 1)
                    V.tensor_tensor(a_lo[:, h, 0:SEQ], jbank(plan.base[("attn_o", h)])[:, 0:SEQ],
                                    a_hi[:, h, 0:SEQ].bitcast(F32), ALU.subtract).then_inc(s["attn_o_read"], 1)

                for i in range(3):
                    row_max(i)
                for i in range(2 * QH):
                    dve.wait_ge(s["scores_read"], i + 1)
                    link(V.reciprocal(stat[:, 4, i:i + 1], att_stat[:, 2, i:i + 1]))
                    if i >= 3:
                        dve.wait_ge(s["p_turned"], i - 2)
                    V.tensor_scalar(prn[:, i % 3, :], pr[:, i % 4, :], stat[:, 4, i:i + 1], None, ALU.mult)\
                        .then_inc(s["p_ready"], 1)
                    if i + 3 < 2 * QH:
                        row_max(i + 3)
                    if i % 2 == 0 and i >= 4:
                        lower_o(i // 2 - 2)
                for h in range(QH - 2, QH):
                    lower_o(h)
                for c in range(KC):
                    split_to(first_unit("o_out") + c + 4)
                    sum_z(4, c, first_job("o_out") + c)

            dve.wait_ge(s["ones_made"], 4)
            for q in range(4):
                V.tensor_copy(fold[32 * q:32 * (q + 1), :], ident[32 * q:32 * (q + 1), 32 * q:32 * (q + 1)])\
                    .then_inc(s["fold_made"], 1)
            filter_and_slot_0()
            take_mods(0)
            for c in range(KC):
                dve.wait_ge(s["ahi_ready"], c + 1)
                V.tensor_tensor(a_lo[:, c, :], tmp_b[:, c % 2, :], a_hi[:, c, :].bitcast(F32),
                                ALU.subtract).then_inc(s["a_ready"], 1)
            ffn(0)
            split_to(E_U + 4)
            normalise(0)
            even_mixer()
            split_to(plan.base[("w1", 1, 0)][0] + 4)
            normalise(1)
            ffn(1)
            split_to(plan.base[("w1", 2, 0)][0] + 4)
            normalise(2)
            ffn(2)
            split_to(O_U + 4)
            normalise(3)
            odd_mixer()
            split_to(plan.base[("w1", 3, 0)][0] + 4)
            normalise(4)
            ffn(3)
            normalise(5)

        @block.tensor
        def _(pe):
            def split_product(dst, w_at, x_at, first, last):
                pe.matmul(dst, w_at(0), x_at(0), start=first, stop=False)
                pe.matmul(dst, w_at(1), x_at(0), start=False, stop=False)
                return pe.matmul(dst, w_at(0), x_at(1), start=False, stop=last)

            def w_tile(n, k, width=P):
                return lambda part: (w_hi, w_lo)[part][:, n % RING, k * width:(k + 1) * width]

            def tokens(pair, k, nt):
                return lambda part: pair[part][:, k, 0:nt]

            A_IN, H_IN = (a_hi, a_lo), (h_hi, h_lo)

            def unit_split(n, i=0):
                pe.wait_ge(s["lo_ready"], n + 1 + 4 * i)

            def project(n, j, nt, i=0, order=None, each=None):
                unit_split(n, i)
                order = order or range(KC)
                for at, k in enumerate(order):
                    if each:
                        each(at, k)
                    ins = split_product(jbank(j)[:, 0:nt], w_tile(n, k), tokens(A_IN, k, nt), at == 0, at == KC - 1)
                ins.then_inc(s["w_used"], 1)

            def sum_mods(a):
                nw = 2 if a < 5 else 1
                pe.wait_ge(s["fold_made"], 4)
                pe.wait_ge(s["ada_turned"], turned_before(a) + (2 if a in (0, 5) else 4))
                for q in range(4):
                    for w in range(nw):
                        n = 3 * KC // 2 if a == 0 else 3 * KC
                        ins = pe.matmul(bank[7][32 * q:32 * (q + 1), w * 3 * KC:w * 3 * KC + n], fold[:],
                                        turned[:, w, q:4 * n:4], start=True, stop=True)
                ins.then_inc(s["mods_summed"], 1)

            def ada_rows(k):
                buf = 2 * (k % 2) + 1
                pe.wait_ge(ada_in[buf], 16 * (k // 2 + 1))
                if k == 0:
                    pe.wait_ge(s["silu_c"], 1)
                half = 3 * KC // 2
                src = ada if buf < 2 else ada0
                for c in range(half):
                    ins = pe.matmul(bank[6][:, half + c:6 * KC:3 * KC], src[:, 1, c * P:(c + 1) * P], scol[:, :, k],
                                    start=(k == c == 0), stop=(k == KC - 1), skip_group_check=True)
                ins.then_inc(s["ada_product"], 1)

            def layer_norm(n):
                nt = T if n < 4 else SEQ
                for last in range(2):
                    for col, t in ((0, hz[:, KC - 1, :] if last else sum1[:]), (TC, sq[:, 1, :] if last else sum2[:])):
                        if last:
                            pe.wait_ge(*((s["z_ready"], z_count(n, KC - 1)) if col == 0
                                         else (s["sq_ready"], KC * (n + 1))))
                        else:
                            pe.wait_ge(*((s["s1_added"], (KC - 1) * (n + 1)) if col == 0
                                         else (s["s2_added"], (KC - 2) * (n + 1))))
                        for b in range(nt // P):
                            ins = pe.matmul(bank[4][:, col + b:col + b + 1], t[:, b * P:(b + 1) * P], ones[:, 0:1],
                                            start=(last == col == b == 0), stop=(last == 1), skip_group_check=True)
                ins.then_inc(s["stat_sums"], 1)
                pe.wait_ge(s["mean_diag"], n + 1)
                pe.matmul(bank[6][:, 0:nt], ones[:], sq[:, 1, 0:nt], start=True, stop=True)\
                    .then_inc(s["mean_bcast"], 1)
                pe.wait_ge(s["diag_ready"], n + 1)
                pe.matmul(bank[5][:, 0:nt], ones[:], sq[:, 0, 0:nt], start=True, stop=True)\
                    .then_inc(s["stat_bcast"], 1)

            def first_four(n_sub, n0, j0, nts):
                for u in range(4):
                    unit_split(n0 + u)
                    bank_read(pe, j0 + u)
                side = KC - 2
                steps = [(k, u) for k in range(side) for u in range(4)]
                steps += [(k, u) for u in range(4) for k in range(side, KC)]
                made = 0
                for k, u in steps:
                    if k + 1 > made:
                        made = k + 1
                        pe.wait_ge(s["a_ready"], KC * n_sub + made)
                    ins = split_product(jbank(j0 + u)[:, 0:nts[u]], w_tile(n0 + u, k), tokens(A_IN, k, nts[u]),
                                        k == 0, k == KC - 1)
                    if k == KC - 1:
                        ins.then_inc(s["w_used"], 1)

            def ffn(fi):
                _, _, _, nt, adas = FFNS[fi]
                n_sub = SUB_OF_FFN[fi]
                for half in range(2):
                    n0, j0 = plan.base[("w1", fi, half)]
                    m0 = (2 * fi + half) * HH
                    if half == 0:
                        first_four(n_sub, n0, j0, [nt] * 4)
                    else:
                        for u in range(4):
                            bank_read(pe, j0 + u)
                            project(n0 + u, j0 + u, nt)
                    with pe.Fori(0, 4) as i:
                        for u in range(4, 8):
                            if u % 2 == 0:
                                pe.wait_ge(s["hraw_ready"], m0 + u // 2 - 1 + 2 * i)
                            project(n0 + u, j0 + u, nt, i)
                    for u in (20, 21):
                        bank_read(pe, j0 + u)
                        project(n0 + u, j0 + u, nt)
                    n1, j1 = plan.base[("w2", fi, half)]
                    for oc in range(KC):
                        if oc == 6 and adas[half]:
                            sum_mods(ADA_ORDER.index(adas[half]))
                        bank_read(pe, j1 + oc)
                        if oc == 0:
                            pe.wait_ge(s["h_ready"], m0 + HH - 1)
                        for piece in range(2):
                            n = n1 + 2 * oc + piece
                            unit_split(n)
                            for k in range(UW2[piece]):
                                j = piece * UW2[0] + k
                                if oc == 0 and j == HH - 1:
                                    pe.wait_ge(s["h_ready"], m0 + HH)
                                ins = split_product(jbank(j1 + oc)[:, 0:nt], w_tile(n, k), tokens(H_IN, j, nt),
                                                    j == 0, j == HH - 1)
                            ins.then_inc(s["w_used"], 1)

            def filter_and_slot_0():
                pe.wait_ge(s["filter_in"], 48)
                pe.wait_ge(s["ones_made"], 4)
                j = first_job("filter_h")
                pe.matmul(jbank(j)[0:FHID, 0:SEQ], fw1[:], feats[:], start=True, stop=True).then_inc(s["filter_h"], 1)
                ada_rows(0)
                pe.wait_ge(s["filter_sin"], 1)
                pe.matmul(jbank(j + 1)[0:FHID, 0:SEQ], fw2[:], fh[0:FHID, 0, :], start=True, stop=True)\
                    .then_inc(s["filter_h"], 1)
                ada_rows(1)
                pe.wait_ge(s["filter_sin"], 2)
                pe.wait_ge(s["taps_in"], 16)
                j = first_job("filter_taps")
                for i in range(4):
                    bank_read(pe, j + i)
                    pe.matmul(jbank(j + i)[:], fh[:, 1, (i % 2) * P:(i % 2 + 1) * P],
                              fw3[:, (i // 2) * HYW:(i // 2 + 1) * HYW], start=True, stop=True)\
                        .then_inc(s["filter_taps"], 1)
                ada_rows(2)
                ada_rows(3)
                pe.wait_ge(s["taps_mixed"], 4)
                pe.wait_ge(s["dft0_in"], 16)
                j = first_job("spectrum")
                for i in range(4):
                    bank_read(pe, j + i)
                    for b in range(2):
                        ins = pe.matmul(jbank(j + i)[:], dft0[:, b, i * P:(i + 1) * P], tmix[:, (i // 2) * 2 + b, :],
                                        start=(b == 0), stop=(b == 1))
                    ins.then_inc(s["spectrum"], 1)
                    ada_rows(4 + i)
                j = first_job("nyquist")
                bank_read(pe, j)
                for b in range(2):
                    ins = pe.matmul(jbank(j)[0:1, :], dft0[:, b, SEQ:SEQ + 1], tmix[:, b, :],
                                    start=(b == 0), stop=(b == 1))
                ins.then_inc(s["nyquist"], 1)
                j = first_job("tap_norm")
                bank_read(pe, j)
                pe.wait_ge(s["taps_squared"], 4)
                for c in range(YC):
                    for i in range(4):
                        ins = pe.matmul(jbank(j)[:, c:c + 1], tsq[:, i, c * P:(c + 1) * P], ones[:, 0:1],
                                        start=(i == 0), stop=(i == 3))
                ins.then_inc(s["tap_norm"], 1)

            def even_mixer():
                first_four(1, E_U, E_J, [T] * 4)
                for e in range(3, 4):
                    bank_read(pe, first_job("e_qk") + e)
                    project(first_unit("e_qk") + e, first_job("e_qk") + e, T)
                for m in range(4):
                    n = first_unit("e_v") + m
                    unit_split(n)
                    for kk in range(2):
                        k = 2 * m + kk
                        for t in range(TC):
                            ins = split_product(bank[4 + t][:], lambda part: A_IN[part][:, k, t * P:(t + 1) * P],
                                                w_tile(n, kk, GH * GDV), k == 0, k == KC - 1)
                    ins.then_inc(s["w_used"], 1)
                pe.wait_ge(s["low_read"], 1)
                pe.wait_ge(s["gla_in"], 32)
                for e in range(4):
                    j = first_job("gate_pre") + e
                    bank_read(pe, j)
                    pe.matmul(jbank(j)[:], gu[:, e // 2, (e % 2) * P:(e % 2 + 1) * P], low[:], start=True, stop=True)\
                        .then_inc(s["gate_pre"], 1)
                for e in range(3 * YC):
                    bank_read(pe, first_job("e_hy") + e)
                    project(first_unit("e_hy") + e, first_job("e_hy") + e, T)
                pe.wait_ge(s["gla_ops"], 4)
                for t in range(TC):
                    bank_read(pe, first_job("att") + t)
                for odd in range(2):
                    if odd:
                        pe.wait_ge(s["att_even"], 1)
                    for t in range(TC):
                        j = first_job("att") + t
                        for e in range(odd, 2 * GH, 2):
                            d, h = divmod(e, GH)
                            rows = slice(odd * GDK, (odd + 1) * GDK)
                            for b in range(2):
                                cols = slice((2 * t + b) * GCH, (2 * t + b + 1) * GCH)
                                ins = pe.matmul(jbank(j)[b * GCH:(b + 1) * GCH, e * GCH:(e + 1) * GCH],
                                                kin[rows, 2 * d + h // 2, cols], qin[rows, 2 * d + h // 2, cols],
                                                start=True, stop=True)
                        if odd:
                            ins.then_inc(s["att"], 1)
                        elif t == TC - 1:
                            ins.then_inc(s["att_even"], 1)
                for t in range(TC):
                    j = first_job("kst_turned") + t
                    bank_read(pe, j)
                    for e in range(4):
                        ins = pe.transpose(jbank(j)[:, e * P:(e + 1) * P], kst[:, e, t * P:(t + 1) * P], ident[:])
                    ins.then_inc(s["kst_turned"], 1)
                pe.wait_ge(s["v_read"], TC)
                for cc in range(NCH):
                    j = first_job("ds") + cc
                    t, b = divmod(cc, 2)
                    bank_read(pe, j)
                    pe.wait_ge(s["kst_read"], t + 1)
                    rows = slice(b * GCH, (b + 1) * GCH)
                    for d in range(2):
                        for h in range(GH):
                            at = (2 * d + h // 2) * P
                            ins = pe.matmul(jbank(j)[(h % 2) * GDK:(h % 2 + 1) * GDK, at:at + P],
                                            kstt[rows, t, d, h // 2, (h % 2) * GDK:(h % 2 + 1) * GDK],
                                            v[rows, t, h * GDV:(h + 1) * GDV], start=True, stop=True)
                    ins.then_inc(s["ds"], 1)
                for h in range(GH):
                    bank_read(pe, first_job("e_g") + h)
                    project(first_unit("e_g") + h, first_job("e_g") + h, T)
                pe.wait_ge(s["att_masked"], TC)
                pe.wait_ge(s["state_ready"], NCH - 1)
                for top in range(2):
                    if top:
                        pe.wait_ge(s["o_lower"], 1)
                    rows = slice(top * GCH, (top + 1) * GCH)
                    for h in range(GH):
                        terms = []
                        for cc in range(NCH):
                            t, b = divmod(cc, 2)
                            cols = slice(cc * GCH, (cc + 1) * GCH)
                            if b == top:
                                terms += [(cols, v[rows, t, h * GDV:(h + 1) * GDV], attm[rows, t, d, h, :])
                                          for d in range(2)]
                            if h % 2 == top:
                                terms += [(cols, state[rows, cc, d, h // 2, :], qin[rows, 2 * d + h // 2, cols])
                                          for d in range(2) if cc != (NLAT, NCH - 1)[d]]
                        for at, (cols, lhs, rhs) in enumerate(terms):
                            ins = pe.matmul(bank[4 + h][:, cols], lhs, rhs, start=(top == 0 and at == 0),
                                            stop=(top == 1 and at == len(terms) - 1), skip_group_check=True)
                        if top:
                            ins.then_inc(s["o_done"], 1)
                        elif h == GH - 1:
                            ins.then_inc(s["o_lower"], 1)
                j = first_job("osq")
                bank_read(pe, j)
                for h in range(GH):
                    pe.wait_ge(s["o_sq"], h + 1)
                    for t in range(TC):
                        ins = pe.matmul(jbank(j)[:, h * TC + t:h * TC + t + 1], osqr[:, h, t * P:(t + 1) * P],
                                        ones[:, 0:1], start=True, stop=True)
                ins.then_inc(s["osq"], 1)
                for h in range(GH):
                    j = first_job("orms") + h
                    bank_read(pe, j)
                    pe.wait_ge(s["odiag_ready"], h + 1)
                    pe.matmul(jbank(j)[:], ones[:], odiag[:, h, :], start=True, stop=True).then_inc(s["orms"], 1)
                for t in range(TC):
                    j = first_job("z_turned") + t
                    bank_read(pe, j)
                    for c in range(YC):
                        ins = pe.transpose(jbank(j)[:, c * P:(c + 1) * P], zf[:, c, t * P:(t + 1) * P], ident[:])
                    ins.then_inc(s["z_turned"], 1)
                pe.wait_ge(s["zt_read"], TC)
                pe.wait_ge(s["dft_in"], 32)
                for i in range(8):
                    w, r, part = i // 4, i // 2 % 2, i % 2
                    j = first_job("dft") + i
                    bank_read(pe, j)
                    for b in range(2):
                        ins = pe.matmul(jbank(j)[:], dft[:, b, (2 * part + r) * P:(2 * part + r + 1) * P],
                                        zt[:, 2 * w + b, :], start=(b == 0), stop=(b == 1))
                    ins.then_inc(s["dft"], 1)
                pe.wait_ge(s["spec_out"], 4)
                for c in range(YC):
                    j = first_job("idft") + c
                    bank_read(pe, j)
                    for w in range(2):
                        for f in range(4):
                            ins = pe.matmul(jbank(j)[:, w * SEQ:(w + 1) * SEQ], yspec[:, f, w, c * P:(c + 1) * P],
                                            idft[:, f, :], start=(f == 0), stop=(f == 3))
                    ins.then_inc(s["idft"], 1)
                order = list(range(YC, KC)) + list(range(YC))
                for c in range(KC):
                    bank_read(pe, first_job("e_out") + c)
                    project(first_unit("e_out") + c, first_job("e_out") + c, T, order=order,
                            each=(lambda at, k: pe.wait_ge(s["cat_ready"], at + 1)) if c == 0 else None)

            def odd_mixer():
                turn = rope[:, 2 * SEQ:2 * SEQ + P]
                first_four(4, O_U, O_J, [T] * KVH + [SEQ] * (4 - KVH))
                for h in range(4 - KVH, QH):
                    bank_read(pe, first_job("o_q") + h)
                    project(first_unit("o_q") + h, first_job("o_q") + h, SEQ)
                for m in range(2):
                    n = first_unit("o_v") + m
                    unit_split(n)
                    for kk in range(4):
                        k = 4 * m + kk
                        for t in range(TC):
                            ins = split_product(bank[4 + t][:, 0:KVH * HD],
                                                lambda part: A_IN[part][:, k, t * P:(t + 1) * P],
                                                w_tile(n, kk, KVH * HD), k == 0, k == KC - 1)
                    ins.then_inc(s["w_used"], 1)
                pe.wait_ge(s["k_read"], KVH)
                pe.wait_ge(s["odd_in"], 16)
                j = first_job("krot")
                bank_read(pe, j)
                for g in range(KVH):
                    ins = pe.matmul(jbank(j)[:, g * SEQ:(g + 1) * SEQ], turn, kg[:, g, 0:SEQ], start=True, stop=True)
                ins.then_inc(s["krot"], 1)
                j = first_job("ksq")
                bank_read(pe, j)
                for g in range(KVH):
                    for t in range(TC):
                        ins = pe.matmul(jbank(j)[:, g * TC + t:g * TC + t + 1], ksqr[:, g, t * P:(t + 1) * P],
                                        ones[:, 0:1], start=True, stop=True)
                ins.then_inc(s["ksq"], 1)
                for i in range(QH // 2):
                    j = first_job("qrot") + i
                    bank_read(pe, j)
                    pe.wait_ge(s["q_read"], 2 * i + 2)
                    pe.matmul(jbank(j)[:], turn, qg[:, 2 * i:2 * i + 2, :].rearrange("p a t -> p (a t)"),
                              start=True, stop=True).then_inc(s["qrot"], 1)
                j = first_job("qsq")
                bank_read(pe, j)
                for i in range(2 * QH):
                    h, qb = divmod(i, 2)
                    ins = pe.matmul(jbank(j)[:, i:i + 1], qsqr[:, h, qb * P:(qb + 1) * P], ones[:, 0:1],
                                    start=True, stop=True)
                ins.then_inc(s["qsq"], 1)
                for g in range(KVH):
                    j = first_job("krms") + g
                    bank_read(pe, j)
                    pe.wait_ge(s["kdiag_ready"], g + 1)
                    pe.matmul(jbank(j)[:], ones[:], kd[:, g, :], start=True, stop=True).then_inc(s["krms"], 1)
                pe.wait_ge(s["krms_read"], KVH)

                def scores(i):
                    h, qb = divmod(i, 2)
                    if i >= 4:
                        pe.wait_ge(s["scores_read"], i - 3)
                    pe.wait_ge(s["q_ready"], h // 2 + 1)
                    pe.matmul(bank[4 + i % 4][:], qg[:, h, qb * P:(qb + 1) * P], kT[:, h // (QH // KVH), :],
                              start=True, stop=True).then_inc(s["scores"], 1)

                def head_out(h):
                    j = plan.base[("attn_o", h)]
                    bank_read(pe, j)
                    pe.wait_ge(s["pt_read"], 2 * h + 2)
                    g = h // (QH // KVH)
                    for t in range(TC):
                        ins = pe.matmul(jbank(j)[:, 0:SEQ], vo[:, t, g * HD:(g + 1) * HD],
                                        pt[:, h % 2, t, :, :].rearrange("p a q -> p (a q)"),
                                        start=(t == 0), stop=(t == TC - 1))
                    ins.then_inc(s["attn_o"], 1)

                pe.wait_ge(s["ov_read"], TC)
                for i in range(3):
                    scores(i)
                for i in range(2 * QH):
                    if i + 3 < 2 * QH:
                        scores(i + 3)
                    j = plan.base[("turned", i)]
                    bank_read(pe, j)
                    pe.wait_ge(s["p_ready"], i + 1)
                    for t in range(TC):
                        ins = pe.transpose(jbank(j)[:, t * P:(t + 1) * P], prn[:, i % 3, t * P:(t + 1) * P], ident[:])
                    ins.then_inc(s["p_turned"], 1)
                    if i % 2 == 0 and i >= 2:
                        head_out(i // 2 - 1)
                head_out(QH - 1)
                for c in range(KC):
                    bank_read(pe, first_job("o_out") + c)
                    project(first_unit("o_out") + c, first_job("o_out") + c, SEQ,
                            each=(lambda at, k: pe.wait_ge(s["attn_o_read"], k + 1)) if c == 0 else None)

            filter_and_slot_0()
            sum_mods(0)
            ffn(0)
            layer_norm(0)
            even_mixer()
            layer_norm(1)
            ffn(1)
            layer_norm(2)
            ffn(2)
            layer_norm(3)
            odd_mixer()
            layer_norm(4)
            ffn(3)
            layer_norm(5)


def shape_tables():
    f = np.float64
    n = np.arange(SEQ, dtype=f)
    t = np.linspace(0.0, 1.0, SEQ)
    bands = np.linspace(1e-4, BANDS - 1, BANDS)
    ang = 2.0 * np.pi * n[:, None] * bands / SEQ
    feats = np.concatenate([t[:, None], np.cos(ang), -np.sin(ang)], 1).T
    deltas = np.abs(np.linspace(np.log(1e-2) / 1.5, np.log(1e-2) / 0.3, HYW))
    decay = np.exp(-t[:, None] * deltas).reshape(2, P, HYW)
    back = decay.copy()
    back[0, 0] = 0.0
    window = np.stack([decay[0], decay[1], back[0], back[1]], 1)
    fr = np.arange(SEQ, dtype=f)
    turn = 2.0 * np.pi * np.outer(n, fr) / NFREQ
    cos, sin = np.cos(turn), np.sin(turn)
    nyq = np.where(n % 2 == 0, 1.0, -1.0)
    fwd_sin, inv_sin = sin.copy(), 2.0 * sin
    fwd_sin[:, 0] = nyq
    inv_sin[:, 0] = nyq
    inv_cos = 2.0 * cos
    inv_cos[:, 0] = 1.0
    dft = np.concatenate([cos, fwd_sin], 1).reshape(2, P, NFREQ).transpose(1, 0, 2)
    inv = (np.concatenate([inv_cos, inv_sin], 1) / NFREQ).T.reshape(4, P, SEQ).transpose(1, 0, 2)
    key = np.arange(P)[:, None] % GCH
    q = np.arange(GCH)[None, :]
    keep = np.stack([key <= q, key >= q], 1)
    bound = np.stack([np.where(keep, BIG, 0.0), np.where(keep, -BIG, 0.0)], 1)
    pairs = HD // 4
    inv_freq = 10000.0 ** (-np.arange(pairs, dtype=f) / pairs)
    row, col = n // GRID_W, n % GRID_W
    angles = np.concatenate([np.outer(inv_freq, row)] * 2 + [np.outer(inv_freq, col)] * 2, 0)
    exchange = np.zeros((HD, HD))
    for b in (0, 2 * pairs):
        for r in range(pairs):
            exchange[b + pairs + r, b + r] = -1.0
            exchange[b + r, b + pairs + r] = 1.0
    rope = np.concatenate([np.cos(angles), np.sin(angles), exchange], 1)
    return [np.ascontiguousarray(a, dtype=np.float32) for a in (feats, window, dft, inv, bound, rope)]


def lay_out(i):
    cols = [
        i["ada_b"].reshape(-1, P), i["ln_g"].reshape(-1, P), i["ln_b"].reshape(-1, P),
        i["c"].reshape(-1, P), i["c_ctx"].reshape(-1, P),
        i["hyena_conv_w"].reshape(-1, P), i["hyena_conv_b"].reshape(-1, P), i["hyena_skip"].reshape(-1, P),
        i["gla_gate_b"].reshape(-1, P), i["gla_norm_g"].reshape(-1, P),
        i["attn_q_norm"].reshape(-1, P), i["attn_k_norm"].reshape(-1, P),
    ]
    cols += [np.concatenate([i[n], i[n]], 1) for n in ("hyena_f_b1", "hyena_f_fr1", "hyena_f_b2", "hyena_f_fr2")]
    par = np.concatenate(cols, 0).T
    x = np.concatenate([i["x"][0], i["ctx"][0]], 0).T.reshape(KC, P, T).transpose(1, 0, 2)

    def chunks(w):
        return w.reshape(KC, P, -1, P).transpose(2, 1, 0, 3).reshape(-1, P, KC * P)

    def rows(w, per):
        return w.reshape(KC // per, per, P, -1).transpose(0, 2, 1, 3).reshape(KC // per, P, -1)

    w1 = i["ffn_w1"].reshape(DEPTH, 2, KC, P, 2, HC, P).transpose(0, 1, 5, 4, 3, 2, 6).reshape(
        DEPTH, 2, HC, 2, P, KC * P)
    w2 = i["ffn_w2"].reshape(DEPTH, 2, 2, HH, P, KC, P).transpose(0, 1, 2, 5, 4, 3, 6).reshape(
        DEPTH, 2, 2, KC, P, HH * P)
    ada = i["ada_w"].reshape(DEPTH, KC, P, 3, 3 * D).transpose(0, 3, 1, 2, 4)
    w = i["even_w_in"][0]
    at = np.cumsum([0, 3 * HYW, GH * GDK, GH * GDK, GH * GDV, GH * GDV, 2 * RANK])
    hy, q, k, v, g, low = (w[:, a:b] for a, b in zip(at[:-1], at[1:]))
    low = np.concatenate([low, np.zeros((D, P - 2 * RANK), low.dtype)], 1)
    hy = hy.reshape(D, 3, YC, P).transpose(0, 2, 1, 3).reshape(D, -1)
    ew = chunks(np.concatenate([low, q, k, hy, g], 1))
    o = i["attn_w_in"][0]
    gu = np.zeros((2 * RANK, 2, 2 * P), np.float32)
    gu[0:RANK, 0], gu[RANK:, 1] = i["gla_gate_up"][0]
    fw3 = np.concatenate([i["hyena_f_w3"][0], i["hyena_f_b3"]], 0)
    feats, window, dft, inv, bound, rope = shape_tables()
    return [x, par, w1, w2, ada, ew, rows(v, 2), chunks(i["even_w_out"][0]),
            chunks(np.concatenate([o[:, QH * HD:(QH + KVH) * HD], o[:, :QH * HD]], 1)),
            rows(o[:, (QH + KVH) * HD:], 4), chunks(i["attn_w_out"][0]), gu,
            i["hyena_f_w1"][0], i["hyena_f_w2"][0], fw3, feats, window, dft, inv, bound, rope]


def kernel(**inputs):
    import concourse.bacc as _bacc
    from concourse.bass_utils import run_bass_kernel_spmd as _run

    nc = _bacc.Bacc("TRN2", target_bir_lowering=False, num_devices=1)
    arrays, args = {}, []
    for n, a in enumerate(lay_out({k: np.asarray(v) for k, v in inputs.items()})):
        a = np.ascontiguousarray(a)
        arrays[f"in_{n}_dram"] = a
        args.append(nc.dram_tensor(f"in_{n}_dram", a.shape, mybir.dt.from_np(a.dtype), kind="ExternalInput").ap())
    args.append(nc.dram_tensor("out_dram", (D, SEQ), F32, kind="ExternalOutput").ap())
    hybrid_trunk(nc, *args)
    r = _run(nc, [arrays], core_ids=[0])
    return np.ascontiguousarray(r.results[0]["out_dram"].T).reshape(1, SEQ, D)
```

```python
from contextlib import ExitStack

import numpy as np

import concourse.bass as bass
from concourse import mybir

ALU = mybir.AluOpType
ACT = mybir.ActivationFunctionType
F32 = mybir.dt.float32
F32R = mybir.dt.float32r
I32 = mybir.dt.int32
AX_X = mybir.AxisListType.X

P = 128
D = 1024
KC = D // P
SEQ = 256
CTX = 256
T = SEQ + CTX
TC = T // P
DEPTH = 2
FFN = ((8 * D // 3 + 255) // 256) * 256
HC = FFN // P
HH = HC // 2
ALPHA = (2.0 * DEPTH) ** 0.25
LN_EPS = 1e-5
RMS_EPS = 1e-6

HYW = D // 2
YC = HYW // P
NFREQ = 2 * SEQ
BANDS, FHID = 16, 64
EMB = 1 + 2 * BANDS

GH, GDV, GDK = 4, 128, 64
GCH = 64
NCH = T // GCH
RANK = 16
TAU = 16.0
NLAT = SEQ // GCH

DS_ORDER = (4, 7, 5, 6, 0, 3, 1, 2)

HD, QH, KVH = 128, 8, 2
GRID_W = 64

RING = 4
UCOL = 1024
UW2 = (6, 5)
ADA_PIECE = 3 * D // 2
PIECES = 2 * KC
MAGIC = 0x5F3759DF
ROUND = 12582912.0
TWO_PI_HI, TWO_PI_MID = 6.28125, 0.0019353071795864769
PI_LOW = 3.1415925
BIG = float(np.finfo(np.float32).max)


def column_map():
    at, n = {}, 0
    for name, k in (
        ("ada_b", DEPTH * 9 * KC), ("ln_g", DEPTH * 3 * KC), ("ln_b", DEPTH * 3 * KC), ("c", 2 * KC),
        ("conv_w", 3 * 3 * YC), ("conv_b", 3 * YC), ("skip", YC), ("gate_b", 4), ("gla_g", 1),
        ("q_norm", 1), ("k_norm", 1), ("f_b1", 1), ("f_fr1", 1), ("f_b2", 1), ("f_fr2", 1),
    ):
        at[name] = n
        n += k
    return at, n


COL, NCOL = column_map()

FFNS = [
    (0, 0, 0, T, [(0, 1), (0, 2)]),
    (0, 1, 2, T, [(1, 0), (1, 1)]),
    (1, 0, 0, T, [(1, 2), None]),
    (1, 1, 2, SEQ, [None, None]),
]
ADA_ORDER = [(0, 0), (0, 1), (0, 2), (1, 0), (1, 1), (1, 2)]
SUB_OF_FFN = (0, 2, 3, 5)


ADA_FIRST = ((6, 0, 1), (6, 1, 0))
ADA_BODY = ((0, 1, 1), (0, 0, 0), (3, 0, 0))
ADA_LAST = ((7, 0, 1), (7, 1, 0), (3, 1, 1), (4, 1, 0), (5, 1, 1))
ADA0_COLS = 2 * D


def ada_before(a):
    return 0 if a == 0 else KC + PIECES * (a - 1)


def ada_loads(a, buf):
    return 0 if a == 0 else KC // 2 + (9, 7)[buf] * (a - 1)


def turned_before(a):
    return 0 if a == 0 else 2 + 4 * (a - 1)


class Plan:

    def __init__(self):
        self.units = []
        self.ready = []
        self.free = []
        self.base = {}
        self.count = {}

    def bump(self, name, n=1):
        self.count[name] = self.count.get(name, 0) + n
        return self.count[name]

    def unit(self, *u):
        self.units.append(u)
        return len(self.units)

    def job(self, ready, free):
        self.ready.append(ready)
        self.free.append(free)
        return len(self.ready) - 1

    def mark(self, name):
        self.base[name] = (len(self.units), len(self.ready))


def make_plan():
    p = Plan()

    def ffn(fi):
        layer, f = FFNS[fi][:2]
        for half in range(2):
            p.mark(("w1", fi, half))
            for j in range(HH):
                m = (fi * 2 + half) * HH + j
                for g in range(2):
                    n = p.unit("w1", (layer, f, half * HH + j, g), UCOL)
                    p.job(("w_used", n), ("hraw_ready", m + 1))
            p.mark(("w2", fi, half))
            for oc in range(KC):
                for piece in range(2):
                    n = p.unit("w2", (layer, f, half, oc, piece), UW2[piece] * P)
                p.base[("z", SUB_OF_FFN[fi], half, oc)] = p.bump("z_ready")
                p.job(("w_used", n), ("z_ready", p.count["z_ready"]))

    def proj(name, n, free):
        p.mark((name, 0))
        for e in range(n):
            if free == "z_ready":
                p.base[("z", 1 if name == "e_out" else 4, 1, e)] = p.count["z_ready"] + 1
            u = p.unit(name, (e,), UCOL)
            p.job(("w_used", u), (free, p.bump(free)))

    def jobs(name, n, free):
        p.mark((name, 0))
        for _ in range(n):
            p.job((name, p.bump(name)), (free, p.bump(free)))

    jobs("filter_h", 2, "filter_h_read")
    jobs("filter_taps", 4, "taps_read")
    jobs("spectrum", 4, "spectrum_read")
    jobs("nyquist", 1, "nyquist_read")
    jobs("tap_norm", 1, "tap_norm_read")
    ffn(0)
    proj("e_low", 1, "low_read")
    proj("e_qk", 4, "qk_read")
    p.mark(("e_v", 0))
    for m in range(4):
        p.unit("e_v", (m,), UCOL)
    jobs("gate_pre", 4, "gate_read")
    proj("e_hy", 3 * YC, "hy_read")
    proj("e_g", GH, "g_read")
    jobs("z_turned", TC, "zt_read")
    jobs("dft", 8, "dft_read")
    jobs("idft", YC, "idft_read")
    jobs("ds", NCH, "ds_read")
    proj("e_out", KC, "z_ready")
    ffn(1)
    ffn(2)
    proj("o_k", KVH, "k_read")
    proj("o_q", QH, "q_read")
    p.mark(("o_v", 0))
    for m in range(2):
        p.unit("o_v", (m,), UCOL)
    jobs("krot", 1, "krot_read")
    jobs("ksq", 1, "ksq_read")
    jobs("qrot", QH // 2, "qrot_read")
    jobs("qsq", 1, "qsq_read")
    jobs("krms", KVH, "krms_read")
    p.mark(("attn", 0))
    for step in range(2 * QH + 1):
        if step < 2 * QH:
            p.base[("turned", step)] = p.job(("p_turned", p.bump("p_turned")), ("pt_read", p.bump("pt_read")))
        if step >= 2 and step % 2 == 0:
            p.base[("attn_o", step // 2 - 1)] = p.job(("attn_o", p.bump("attn_o")), ("attn_o_read", p.bump("attn_o_read")))
    proj("o_out", KC, "z_ready")
    ffn(3)
    return p


SEMAPHORES = (
    "x_in", "par_in", "filter_in", "taps_in", "window_in", "dft0_in",
    "gla_in", "dft_in", "odd_in", "ones_made", "fold_made", "rst_made", "silu_c",
    "hi_ready", "lo_ready", "w_used",
    "ada_used", "ada_product", "ada_turned", "acc_zeroed", "mods_summed", "mods_read", "mod_cols",
    "silu_ready", "hraw_ready", "hhi_ready", "h_ready",
    "mean_ready", "mean_diag", "mean_bcast", "z_ready", "s1_added", "sq_ready", "s2_added", "stat_sums", "diag_ready", "stat_bcast",
    "t_ready", "ahi_ready", "first_ready", "ah_ready", "a_ready", "out_ready", "out_stored", "dve_link", "act_link",
    "filter_h", "filter_h_read", "filter_sin", "filter_taps", "taps_read", "taps_mixed", "taps_squared", "squares_added",
    "spectrum", "spectrum_read", "nyquist", "nyquist_read", "tap_norm", "tap_norm_read",
    "low_read", "qk_read", "v_read", "gate_pre", "gate_read", "gate_abs", "gate_ln",
    "gate_rest", "gate_exp", "gla_ops", "hy_mid", "hy_read", "zf_ready", "att_even", "att", "att_read", "att_masked",
    "kst_turned", "kst_read", "ds", "ds_read", "state_ready", "g_read", "o_lower", "o_done", "o_sq",
    "o_scaled", "o_turned", "gla_out", "z_turned", "zt_read",
    "dft", "dft_read", "spec_out", "idft", "idft_read", "cat", "cat_hi", "cat_ready",
    "k_read", "ov_read", "krot", "krot_read", "ksq", "ksq_read", "kdiag_ready", "krms", "krms_read",
    "q_read", "qrot", "qrot_read", "q_ready", "qsq", "qsq_read", "scores", "scores_read", "smax",
    "p_ready", "p_turned", "pt_read", "attn_o", "attn_o_read", "attn_hi",
)


def hybrid_trunk(nc, x_t, par_d, w1_d, w2_d, ada_d, ew_d, ev_d, eo_d, ow_d, ov_d, oo_d, gu_d,
                 fw1_d, fw2_d, fw3_d, feats_d, window_d, dft_d, idft_d, bound_d, rope_d, out):
    plan = make_plan()
    NU = len(plan.units)

    with ExitStack() as ctx:
        s = {n: ctx.enter_context(nc.semaphore(n)) for n in SEMAPHORES}
        raw_in = [ctx.enter_context(nc.semaphore(f"raw_in{i}")) for i in range(RING)]
        ada_in = [ctx.enter_context(nc.semaphore(f"ada_in{i}")) for i in range(4)]

        top = [(nc.sbuf_base + 63) // 64 * 64]

        def put(name, shape, dt=F32, at=None):
            size = int(np.prod(shape[1:])) * 4
            if at is None:
                at = top[0]
                top[0] += (size + 31) // 32 * 32
            return nc.alloc_sbuf_tensor_at(name, shape, dt, offset=at)

        ident = put("ident", [P, P])
        ones = put("ones", [P, P])
        par = put("par", [P, NCOL])
        mods = put("mods", [P, 2, 3 * KC])
        acol = put("acol", [P, 6, 2, 3, KC])
        hcol = put("hcol", [P, 6, 2, KC])
        stat = put("stat", [P, 5, 16])
        FOLD = top[0]
        att_stat = put("att_stat", [P, 4, 2 * QH])
        fold = put("fold", [P, 32], at=FOLD)
        dec = put("dec", [P, 2, 2, NCH])
        kscale = put("kscale", [P, YC])
        scol = put("scol", [P, 2, KC])
        hz = put("hz", [P, KC, T])
        A_HI = top[0]
        a_hi = put("a_hi", [P, KC, T], F32R)
        A_LO = top[0]
        a_lo = put("a_lo", [P, KC, T], F32R)
        raw = put("raw", [P, RING, UCOL])
        w_hi = put("w_hi", [P, RING, UCOL], F32R)
        w_lo = put("w_lo", [P, RING, UCOL], F32R)
        ADA = top[0]
        ada = put("ada", [P, 2, ADA_PIECE])
        X = top[0]
        K = 1024
        acc = put("acc", [P, 2, 3 * D], at=X)
        h_hi = put("h_hi", [P, HH, T], F32R, at=X + 24 * K)
        h_lo = put("h_lo", [P, HH, T], F32R, at=X + 46 * K)
        tmp_a = put("tmp_a", [P, 2, T], at=X + 68 * K)
        tmp_b = put("tmp_b", [P, 2, T], at=X + 72 * K)
        sq = put("sq", [P, 2, T], at=X + 76 * K)
        sum1 = put("sum1", [P, T], at=X + 80 * K)
        sum2 = put("sum2", [P, T], at=X + 82 * K)
        spec = put("spec", [P, 5, HYW], at=X + 84 * K)
        assert X + 94 * K <= nc.sbuf_usable_end
        turned = put("turned", [P, 2, 3 * KC * 4], at=X + 94 * K)
        ada0 = put("ada0", [P, 2, ADA_PIECE], at=X + 70 * K)
        window = put("window", [P, 4, HYW], at=X + 24 * K)
        fw3 = put("fw3", [FHID + 1, 2 * HYW], at=X + 32 * K)
        fw1 = put("fw1", [EMB, FHID], at=X + 36 * K)
        fw2 = put("fw2", [FHID, FHID], at=X + 36 * K + 256)
        feats = put("feats", [EMB, SEQ], at=X + 37 * K)
        farg = put("farg", [FHID, 2, SEQ], at=X + 38 * K)
        fh = put("fh", [FHID + 1, 2, SEQ], at=X + 40 * K)
        taps = put("taps", [P, 4, HYW], at=X + 42 * K)
        tmix = put("tmix", [P, 4, HYW], at=X + 50 * K)
        dft0 = put("dft0", [P, 2, NFREQ], at=X + 58 * K)
        tsq = put("tsq", [P, 4, HYW], at=X + 62 * K)
        qk = put("qk", [P, 4, T], at=X)
        attm = put("attm", [P, TC, 2, GH, GCH], at=X)
        ga = put("ga", [P, 4, T], at=X + 8 * K)
        cv = put("cv", [P, 2, 2, T], at=X + 8 * K)
        kstt = put("kstt", [P, TC, 2, 2, P], at=X + 8 * K)
        gm = put("gm", [P, 4, T], at=X + 16 * K)
        cum = put("cum", [P, 4, T], at=X + 24 * K)
        ds = put("ds_sb", [P, NCH, 2, 2, P], at=X + 16 * K)
        qin = put("qin", [P, 4, T], at=X + 32 * K)
        kin = put("kin", [P, 4, T], at=X + 40 * K)
        kst = put("kst", [P, 4, T], at=X + 48 * K)
        state = put("state", [P, NCH, 2, 2, P], at=X + 40 * K)
        v = put("v", [P, TC, GH * GDV], at=X + 56 * K)
        zf = put("zf", [P, YC, T], at=X + 64 * K)
        part2 = put("part2", [P, YC, T], at=X + 72 * K)
        low = put("low", [2 * RANK, T], at=X + 80 * K)
        rst = put("rst", [P, T], at=X + 82 * K)
        bound = put("bound", [P, 2, 2, GCH], at=X + 94 * K)
        gu = put("gu", [2 * RANK, 2, 2 * P], at=X + 56 * K)
        dft = put("dft_sb", [P, 2, NFREQ], at=X + 16 * K)
        idft = put("idft_sb", [P, 4, SEQ], at=X + 20 * K)
        yt = put("yt", [P, YC, T], at=X + 40 * K)
        osqr = put("osqr", [P, TC, GH * GDV], at=X + 8 * K)
        o_sb = put("o_sb", [P, TC, GH * GDV], at=X + 16 * K)
        go = put("go", [P, GH, T], at=X + 24 * K)
        gs = put("gs", [P, GH, T], at=ADA)
        yspec = [put(f"yspec{i}", [P, 2, 2, HYW], at=at) for i, at in enumerate((A_HI, A_LO))]
        zt = put("zt", [P, TC, HYW], at=A_HI + 8 * K)
        prod = put("prod", [P, 4, HYW], at=A_LO + 8 * K)
        kg = put("kg", [P, KVH, T], at=X)
        krt = put("krt", [P, KVH, SEQ], at=X + 4 * K)
        ksqr = put("ksqr", [P, KVH, T], at=X + 6 * K)
        kd = put("kd", [P, KVH, T], at=X + 10 * K)
        kT = put("kT", [P, KVH, T], at=X + 14 * K)
        vo = put("vo", [P, TC, KVH * HD], at=X + 18 * K)
        rope = put("rope", [P, 2 * SEQ + P], at=X + 22 * K)
        qg = put("qg", [P, QH, SEQ], at=X + 26 * K)
        qsqr = put("qsqr", [P, QH, SEQ], at=X + 34 * K)
        qrt = put("qrt", [P, 2, 2, SEQ], at=X + 42 * K)
        pr = put("pr", [P, 4, T], at=X + 62 * K)
        prn = put("prn", [P, 3, T], at=X + 70 * K)
        pt = put("pt", [P, 2, TC, 2, P], at=X + 54 * K)
        assert X + 95 * K <= nc.sbuf_usable_end

        bank = [ctx.enter_context(nc.psum_tensor(f"bank{i}", [P, T], F32)) for i in range(8)]

        def ada_row(k):
            return (ada, ada0)[k % 2][:].rearrange("p a c -> p (a c)")

        def pcol(name, i=0, rows=P):
            return par[0:rows, COL[name] + i:COL[name] + i + 1]

        def jbank(j):
            return bank[j % 4]

        def wait_for(eng, pair, more=0):
            name, value = pair
            eng.wait_ge(s[name], value + more)

        def job_ready(eng, j, more=0):
            wait_for(eng, plan.ready[j], more)

        def bank_read(eng, j, more=0):
            if j >= 4:
                wait_for(eng, plan.free[j - 4], more)

        def z_count(n, c, half=1):
            return plan.base[("z", n, half, c)]

        def unit_source(n, i=0):
            kind, at, cols = plan.units[n]
            if kind == "w1":
                layer, f, j, g = at
                return w1_d[layer, f, j + 2 * i, g]
            if kind == "w2":
                layer, f, half, oc, piece = at
                lo = piece * UW2[0] * P
                return w2_d[layer, f, half, oc][:, lo:lo + cols]
            if kind == "e_low":
                return ew_d[0]
            if kind == "e_qk":
                return ew_d[1 + at[0]]
            if kind == "e_hy":
                return ew_d[5 + at[0]]
            if kind == "e_g":
                return ew_d[5 + 3 * YC + at[0]]
            if kind == "e_v":
                return ev_d[at[0]]
            if kind == "e_out":
                return eo_d[at[0]]
            if kind == "o_k":
                return ow_d[at[0]]
            if kind == "o_q":
                return ow_d[KVH + at[0]]
            if kind == "o_v":
                return ov_d[at[0]]
            return oo_d[at[0]]

        E_U, E_J = plan.base[("e_low", 0)]
        O_U, O_J = plan.base[("o_k", 0)]

        def first_job(name):
            return plan.base[(name, 0)][1]

        def first_unit(name):
            return plan.base[(name, 0)][0]

        def hidden(t, j, i, nt):
            if isinstance(i, int):
                return t[:, j, 0:nt]
            return t[:, bass.ds(j + 2 * i, 1), 0:nt].rearrange("p a t -> p (a t)")

        block = ctx.enter_context(nc.Block())


        @block.sync
        def _(sp):
            pos = [0]

            def load_unit(n, i=0):
                cols = plan.units[n][2]
                if n >= RING:
                    sp.wait_ge(s["lo_ready"], n - RING + 1 + 4 * i)
                sp.dma_start(raw[:, n % RING, 0:cols], unit_source(n, i)).then_inc(raw_in[n % RING], 16)

            def load_to(n):
                while pos[0] < min(n, NU):
                    load_unit(pos[0])
                    pos[0] += 1

            def load_ada(a, k, half, buf, after, i=0):
                if a is None:
                    return
                if after is not None:
                    sp.wait_ge(s["ada_used"], after)
                layer, slot = ADA_ORDER[a]
                sp.dma_start(ada[:, buf, :], ada_d[layer, slot, k + i][:, half * ADA_PIECE:(half + 1) * ADA_PIECE])\
                    .then_inc(ada_in[buf], 16)

            for t, d in ((feats, feats_d), (fw1, fw1_d), (fw2, fw2_d)):
                sp.dma_start(t[:], d).then_inc(s["filter_in"], 16)
            for k in range(KC):
                for part, cols in enumerate((slice(0, ADA0_COLS), slice(ADA0_COLS, 3 * D))):
                    if k >= 2:
                        sp.wait_ge(s[("ada_used", "ada_product")[part]], k - 1)
                    sp.dma_start(ada_row(k)[:, cols], ada_d[0, 0, k][:, cols]).then_inc(ada_in[2 * (k % 2) + part], 16)
                if k == 1:
                    sp.dma_start(window[:], window_d).then_inc(s["window_in"], 16)
                if k == 2:
                    sp.dma_start(dft0[:], dft_d).then_inc(s["dft0_in"], 16)
            load_to(RING)
            sp.dma_start(hz[:], x_t).then_inc(s["x_in"], 16)
            for fi, (_, _, _, _, adas) in enumerate(FFNS):
                for half in range(2):
                    a = ADA_ORDER.index(adas[half]) if adas[half] else None
                    n0, _ = plan.base[("w1", fi, half)]
                    used = ada_before(a) if a else 0
                    if a:
                        sp.wait_ge(s["ada_turned"], turned_before(a))
                        if a == 1:
                            sp.wait_ge(s["ada_product"], KC)
                        if a == 3:
                            sp.wait_ge(s["gla_out"], GH)
                    for j in range(2):
                        load_to(n0 + 6 + 2 * j)
                        load_ada(a, *ADA_FIRST[j], None)
                    with sp.Fori(0, 3) as i:
                        for jj in range(2):
                            load_unit(n0 + 8 + 2 * jj, i)
                            load_unit(n0 + 9 + 2 * jj, i)
                            for x in ((0, 1), (2,))[jj]:
                                load_ada(a, *ADA_BODY[x], used + (1, 2, 4)[x] + 3 * i, i)
                    pos[0] = n0 + 20
                    for x, piece in enumerate(ADA_LAST):
                        load_to(n0 + 22 + 2 * max(x - 1, 0))
                        load_ada(a, *piece, used + (9, 11, 12, 13, 14)[x])
                    load_to(n0 + 22 + 2 * KC + 2)
                if fi == 0 or fi == 2:
                    load_to(plan.base[("w1", fi + 1, 0)][0])

        @block.gpsimd
        def _(pool):
            g = nc.gpsimd
            g.memset(ident[:], 0.0).then_inc(s["ones_made"], 1)
            pool.wait_ge(s["ones_made"], 1)
            g.affine_select(out=ident[:], in_=ident[:], compare_op=ALU.not_equal, fill=1.0, base=0,
                            pattern=[[-1, P]], channel_multiplier=1).then_inc(s["ones_made"], 1)
            g.memset(ones[:], 1.0).then_inc(s["ones_made"], 1)
            g.memset(fh[:], 1.0).then_inc(s["ones_made"], 1)
            g.memset(acc[:, :, 0:ADA0_COLS], 0.0).then_inc(s["acc_zeroed"], 1)

            def add_squares(n):
                nt = T if n < 4 else SEQ
                for c in range(1, KC - 1):
                    pool.wait_ge(s["sq_ready"], KC * n + c + 1)
                    if c > 1:
                        pool.wait_ge(s["s2_added"], (KC - 2) * n + c - 1)
                    g.tensor_tensor(sum2[:, 0:nt], sum2[:, 0:nt], sq[:, c % 2, 0:nt],
                                    ALU.add).then_inc(s["s2_added"], 1)

            def zero_acc(a):
                pool.wait_ge(s["ada_turned"], turned_before(a))
                g.memset(acc[:], 0.0).then_inc(s["acc_zeroed"], 1)

            for i in range(1, 4):
                pool.wait_ge(s["taps_squared"], i + 1)
                if i > 1:
                    pool.wait_ge(s["squares_added"], i - 1)
                g.tensor_tensor(tsq[:, 0, :], tsq[:, 0, :], tsq[:, i, :], ALU.add).then_inc(s["squares_added"], 1)
            zero_acc(1)
            zero_acc(2)
            add_squares(0)
            pool.wait_ge(s["a_ready"], 2 * KC)
            pool.dma_start(bound[:], bound_d).then_inc(s["gla_in"], 16)
            pool.dma_start(gu[:], gu_d).then_inc(s["gla_in"], 16)
            g.memset(rst[:], 1.0).then_inc(s["rst_made"], 1)
            pool.wait_ge(s["rst_made"], 1)
            g.memset(rst[:].rearrange("p (c t) -> p c t", t=GCH)[:, :, 0:1], 0.0).then_inc(s["rst_made"], 1)
            pool.wait_ge(s["gate_rest"], 4)
            pool.dma_start(dft[:], dft_d).then_inc(s["dft_in"], 16)
            pool.dma_start(idft[:], idft_d).then_inc(s["dft_in"], 16)
            add_squares(1)
            pool.wait_ge(s["a_ready"], 3 * KC)
            zero_acc(3)
            zero_acc(4)
            add_squares(2)
            zero_acc(5)
            add_squares(3)
            pool.wait_ge(s["a_ready"], 5 * KC)
            pool.dma_start(rope[:], rope_d).then_inc(s["odd_in"], 16)
            add_squares(4)
            add_squares(5)

        @block.scalar
        def _(act):
            A = nc.scalar
            pos, links = [0], [0]

            act.dma_start(par[:], par_d).then_inc(s["par_in"], 16)
            act.dma_start(fw3[:], fw3_d).then_inc(s["taps_in"], 16)

            def link(ins):
                links[0] += 1
                ins.then_inc(s["act_link"], 1)
                act.wait_ge(s["act_link"], links[0])

            def split_hi(n, i=0):
                cols = plan.units[n][2]
                act.wait_ge(raw_in[n % RING], 16 * (n // RING + 1) + 16 * i)
                if n >= RING:
                    act.wait_ge(s["w_used"], n - RING + 1 + 4 * i)
                A.copy(w_hi[:, n % RING, 0:cols], raw[:, n % RING, 0:cols]).then_inc(s["hi_ready"], 1)

            def split_to(n):
                while pos[0] < min(n, NU):
                    split_hi(pos[0])
                    pos[0] += 1

            def apply_ln(n):
                nt = T if n < 5 else SEQ
                nz = T if n < 4 else SEQ
                act.wait_ge(s["mod_cols"], n + 1)
                for c in range(KC):
                    if n > 0:
                        act.wait_ge(s["t_ready"], KC * (n - 1) + c + 1)
                    t = tmp_a[:, c % 2, :] if n > 0 else hz[:, c, :]
                    if c >= 2:
                        act.wait_ge(s["a_ready"], KC * n + c - 1)
                    for dst in ((a_hi[:, c, :], tmp_b[:, c % 2, :]) if c == 0 else (tmp_b[:, c % 2, :],)):
                        for w in range(nt // SEQ):
                            cols = slice(w * SEQ, (w + 1) * SEQ)
                            ins = A.activation(dst[:, cols], t[:, cols], ACT.Identity,
                                               bias=acol[:, n, w, 1, c:c + 1], scale=acol[:, n, w, 0, c:c + 1])
                            if c == 0 and w == nt // SEQ - 1:
                                ins.then_inc(s["ahi_ready" if dst.dtype == F32R else "first_ready"], 1)
                    if c > 0:
                        link(ins)
                        A.copy(a_hi[:, c, 0:nt], tmp_b[:, c % 2, 0:nt]).then_inc(s["ahi_ready"], 1)
                    else:
                        act.wait_ge(s["first_ready"], n + 1)
                    A.activation(hz[:, c, 0:nz], t[:, 0:nz], ACT.Identity, bias=hcol[:, n, 1, c:c + 1],
                                 scale=hcol[:, n, 0, c:c + 1]).then_inc(s["ah_ready"], 1)

            def spread_mean(n):
                act.wait_ge(s["mean_ready"], n + 1)
                for t in range((T if n < 4 else SEQ) // P):
                    ins = A.activation(sq[:, 1, t * P:(t + 1) * P], ident[:], ACT.Copy, scale=stat[:, 0, t:t + 1])
                ins.then_inc(s["mean_diag"], 1)

            def square_z(n, c):
                nt = T if n < 4 else SEQ
                act.wait_ge(s["z_ready"], z_count(n, c))
                if c >= 3:
                    act.wait_ge(s["s2_added"], (KC - 2) * n + c - 2)
                A.activation(sum2[:, 0:nt] if c == 0 else sq[:, c % 2, 0:nt], hz[:, c, 0:nt],
                             ACT.Square).then_inc(s["sq_ready"], 1)

            def ffn(fi):
                nt = FFNS[fi][3]

                def hidden_step(n, m, j, i=0):
                    act.wait_ge(s["w_used"], n + 1 + 4 * i)
                    A.activation(tmp_a[:, m % 2, 0:nt], jbank(j0 + n - n0)[:, 0:nt], ACT.Silu)\
                        .then_inc(s["silu_ready"], 1)
                    split_hi(n + 4, i)
                    act.wait_ge(s["hraw_ready"], m + 1 + 2 * i)
                    A.copy(hidden(h_hi, j, i, nt), tmp_b[:, m % 2, 0:nt]).then_inc(s["hhi_ready"], 1)
                    split_hi(n + 5, i)

                for half in range(2):
                    n0, j0 = plan.base[("w1", fi, half)]
                    m0 = (2 * fi + half) * HH
                    split_to(n0 + 4)
                    for j in range(2):
                        hidden_step(n0 + 2 * j, m0 + j, j)
                    with act.Fori(0, 3) as i:
                        for j in (2, 3):
                            hidden_step(n0 + 2 * j, m0 + j, j, i)
                    for j in range(8, HH):
                        hidden_step(n0 + 2 * j, m0 + j, j)
                    pos[0] = n0 + 26
                    for oc in range(KC):
                        split_to(n0 + 22 + 2 * oc + 4)
                        if half == 1 and oc > 0:
                            square_z(SUB_OF_FFN[fi], oc - 1)
                square_z(SUB_OF_FFN[fi], KC - 1)

            def hyena_filter():
                for layer in range(2):
                    act.wait_ge(s["filter_h_read"], layer + 1)
                    act.wait_ge(s["ones_made"], 4)
                    A.activation(fh[0:FHID, layer, :], farg[:, layer, :], ACT.Sin).then_inc(s["filter_sin"], 1)
                for i in range(4):
                    act.wait_ge(s["taps_read"], i + 1)
                    A.activation(tsq[:, i, :], taps[:, i, :], ACT.Square).then_inc(s["taps_squared"], 1)
                j0 = first_job("spectrum")
                for i in range(4):
                    job_ready(act, j0 + i)
                    if i == 0:
                        A.copy(spec[:, 4, :], jbank(j0)[:])
                    A.copy(spec[:, i, :], jbank(j0 + i)[:]).then_inc(s["spectrum_read"], 1)
                    if i == 1:
                        split_to(RING)

            def even_mixer():
                for e in range(4):
                    split_to(E_U + e + 4)
                    job_ready(act, first_job("e_qk") + e)
                    A.copy(qk[:, e, :], jbank(first_job("e_qk") + e)[:]).then_inc(s["qk_read"], 1)
                split_to(first_unit("e_v") + 6)
                for e in range(4):
                    j = first_job("gate_pre") + e
                    job_ready(act, j)
                    A.activation(ga[:, e, :], jbank(j)[:], ACT.Abs, bias=pcol("gate_b", e)).then_inc(s["gate_abs"], 1)
                split_to(first_unit("e_hy") + 4)
                act.wait_ge(s["gate_abs"], 4)
                for e in range(4):
                    ins = A.activation(ga[:, e, :], ga[:, e, :], ACT.Exp, scale=-1.0)
                link(ins)
                for e in range(4):
                    A.activation(ga[:, e, :], ga[:, e, :], ACT.Ln, bias=1.0).then_inc(s["gate_ln"], 1)
                for e in range(4):
                    act.wait_ge(s["gate_rest"], e + 1)
                    A.activation(qin[:, e, :], cum[:, e, :], ACT.Exp, scale=1.0 / TAU)
                    A.activation(kin[:, e, :], cum[:, e, :], ACT.Exp, scale=-1.0 / TAU)
                    last = (GCH - 1) * (1 - e // 2)
                    A.activation(dec[:, e // 2, e % 2, :], cum[:, e, last::GCH], ACT.Exp, scale=1.0 / TAU)
                    A.activation(kst[:, e, :], kst[:, e, :], ACT.Exp, scale=1.0 / TAU).then_inc(s["gate_exp"], 1)
                for c in range(YC):
                    for part in range(3):
                        e = 3 * c + part
                        split_to(first_unit("e_hy") + e + 4)
                        j = first_job("e_hy") + e
                        job_ready(act, j)
                        if c >= 2 and part == 0:
                            act.wait_ge(s["zf_ready"], c - 1)
                        dst = part2[:, c, :] if part == 2 else cv[:, part, c % 2, :]
                        A.activation(dst, jbank(j)[:], ACT.Identity, bias=pcol("conv_b", YC * part + c),
                                     scale=pcol("conv_w", 3 * YC + YC * part + c)).then_inc(s["hy_mid"], 1)
                act.wait_ge(s["ada_turned"], turned_before(3))
                for h in range(GH):
                    split_to(first_unit("e_g") + h + 4)
                    j = first_job("e_g") + h
                    job_ready(act, j)
                    A.activation(gs[:, h, :], jbank(j)[:], ACT.Silu).then_inc(s["g_read"], 1)
                split_to(first_unit("e_out") + 4)
                for t in range(TC):
                    j = first_job("z_turned") + t
                    job_ready(act, j)
                    A.copy(zt[:, t, :], jbank(j)[:]).then_inc(s["zt_read"], 1)
                act.wait_ge(s["zf_ready"], YC)
                for t in range(TC):
                    act.wait_ge(s["kst_turned"], t + 1)
                    A.copy(kstt[:, t].rearrange("p a b c -> p (a b c)"), bank[4 + t][:]).then_inc(s["kst_read"], 1)
                act.wait_ge(s["idft"], YC)
                for c in range(YC):
                    act.wait_ge(s["cat"], c + 1)
                    A.copy(a_hi[:, c, :], yt[:, c, :]).then_inc(s["cat_hi"], 1)
                for at, cc in enumerate(DS_ORDER):
                    j = first_job("ds") + at
                    job_ready(act, j)
                    A.copy(ds[:, cc].rearrange("p a b c -> p (a b c)"), jbank(j)[:]).then_inc(s["ds_read"], 1)
                for t in range(TC):
                    act.wait_ge(s["o_done"], t + 1)
                    A.activation(osqr[:, t, :], bank[4 + t][:], ACT.Square).then_inc(s["o_sq"], 1)
                for h in range(GH):
                    act.wait_ge(s["gla_out"], h + 1)
                    A.copy(a_hi[:, YC + h, :], go[:, h, :]).then_inc(s["cat_hi"], 1)
                for c in range(KC):
                    split_to(first_unit("e_out") + c + 4)
                    if c > 0:
                        square_z(1, c - 1)
                square_z(1, KC - 1)

            def odd_mixer():
                for g in range(KVH):
                    split_to(O_U + g + 4)
                    j = O_J + g
                    job_ready(act, j)
                    A.activation(kg[:, g, :], jbank(j)[:], ACT.Identity, scale=pcol("k_norm"))
                    A.activation(ksqr[:, g, :], jbank(j)[:], ACT.Square).then_inc(s["k_read"], 1)
                for h in range(QH):
                    split_to(first_unit("o_q") + h + 4)
                    j = first_job("o_q") + h
                    job_ready(act, j)
                    A.activation(qg[:, h, :], jbank(j)[:, 0:SEQ], ACT.Identity, scale=pcol("q_norm"))
                    A.activation(qsqr[:, h, :], jbank(j)[:, 0:SEQ], ACT.Square).then_inc(s["q_read"], 1)


                def p_exp(i):
                    act.wait_ge(s["smax"], i + 1)
                    if i >= 4:
                        act.wait_ge(s["p_ready"], i - 3)
                    A.activation(pr[:, i % 4, :], bank[4 + i % 4][:], ACT.Exp,
                                 bias=att_stat[:, 1, i:i + 1], scale=att_stat[:, 0, i:i + 1],
                                 accum_out=att_stat[:, 2, i:i + 1]).then_inc(s["scores_read"], 1)

                def take_o(h):
                    act.wait_ge(s["attn_o"], h + 1)
                    A.copy(a_hi[:, h, 0:SEQ], jbank(plan.base[("attn_o", h)])[:, 0:SEQ]).then_inc(s["attn_hi"], 1)

                p_exp(0)
                p_exp(1)
                split_to(first_unit("o_v") + 5)
                for i in range(2 * QH):
                    if i + 2 < 2 * QH:
                        p_exp(i + 2)
                    j = plan.base[("turned", i)]
                    job_ready(act, j)
                    h, qb = divmod(i, 2)
                    if h >= 2:
                        act.wait_ge(s["attn_o"], h - 1)
                    A.copy(pt[:, h % 2, :, qb, :], jbank(j)[:].rearrange("p (c q) -> p c q", c=TC))\
                        .then_inc(s["pt_read"], 1)
                    if i % 2 == 1 and i >= 3:
                        take_o(i // 2 - 1)
                take_o(QH - 1)
                for c in range(KC):
                    split_to(first_unit("o_out") + c + 4)
                    if c > 0:
                        square_z(4, c - 1)
                square_z(4, KC - 1)

            act.wait_ge(s["par_in"], 16)
            A.activation(scol[:].rearrange("p a b -> p (a b)"), par[:, COL["c"]:COL["c"] + 2 * KC],
                         ACT.Silu).then_inc(s["silu_c"], 1)
            hyena_filter()
            act.wait_ge(s["x_in"], 16)
            apply_ln(0)
            ffn(0)
            split_to(E_U + 4)
            spread_mean(0)
            apply_ln(1)
            even_mixer()
            split_to(plan.base[("w1", 1, 0)][0] + 4)
            spread_mean(1)
            apply_ln(2)
            ffn(1)
            split_to(plan.base[("w1", 2, 0)][0] + 4)
            spread_mean(2)
            apply_ln(3)
            ffn(2)
            split_to(O_U + 4)
            spread_mean(3)
            apply_ln(4)
            odd_mixer()
            split_to(plan.base[("w1", 3, 0)][0] + 4)
            spread_mean(4)
            apply_ln(5)
            ffn(3)
            spread_mean(5)
            for c in range(KC):
                act.wait_ge(s["t_ready"], 5 * KC + c + 1)
                A.activation(hz[:, c, 0:SEQ], tmp_a[:, c % 2, 0:SEQ], ACT.Identity,
                             bias=pcol("ln_b", 5 * KC + c), scale=pcol("ln_g", 5 * KC + c)).then_inc(s["out_ready"], 1)
                act.wait_ge(s["out_ready"], c + 1)
                act.dma_start(out[c * P:(c + 1) * P, :], hz[:, c, 0:SEQ]).then_inc(s["out_stored"], 16)
            act.wait_ge(s["out_stored"], 16 * KC)

        @block.vector
        def _(dve):
            V = nc.vector
            pos, links = [0], [0]

            def link(ins):
                links[0] += 1
                ins.then_inc(s["dve_link"], 1)
                dve.wait_ge(s["dve_link"], links[0])

            def split_lo(n, i=0):
                cols = plan.units[n][2]
                dve.wait_ge(s["hi_ready"], n + 1 + 4 * i)
                V.tensor_tensor(w_lo[:, n % RING, 0:cols], raw[:, n % RING, 0:cols],
                                w_hi[:, n % RING, 0:cols].bitcast(F32), ALU.subtract).then_inc(s["lo_ready"], 1)

            def split_to(n):
                while pos[0] < min(n, NU):
                    split_lo(pos[0])
                    pos[0] += 1

            def add_ada(a, k, half, buf, before, loads, i=0):
                if a is None:
                    return
                if isinstance(before, int) and before == ada_before(a):
                    dve.wait_ge(s["acc_zeroed"], a + 1)
                else:
                    dve.wait_ge(s["ada_used"], before)
                dve.wait_ge(ada_in[buf], loads)
                cols = slice(half * ADA_PIECE, (half + 1) * ADA_PIECE)
                for w in range(2 if a < 5 else 1):
                    scalar = scol[:, w, k:k + 1] if isinstance(i, int) else scol[:, w, bass.ds(k + i, 1)]
                    ins = V.scalar_tensor_tensor(acc[:, w, cols], ada[:, buf, :], scalar, acc[:, w, cols],
                                                 ALU.mult, ALU.add)
                ins.then_inc(s["ada_used"], 1)

            def turn_ada(a, x):
                if a == 5 and x >= 2:
                    return
                w, half = divmod(x, 2)
                dve.wait_ge(s["ada_used"], ada_before(a + 1))
                if x >= 2:
                    dve.wait_ge(s["ada_turned"], turned_before(a) + x - 1)
                room = ada[:, x % 2, :]
                link(V.transpose(room, acc[:, w, half * ADA_PIECE:(half + 1) * ADA_PIECE]))
                n = ADA_PIECE // 32
                V.tensor_reduce(turned[:, w, half * n:(half + 1) * n], room.rearrange("p (b j) -> p b j", j=32),
                                AX_X, ALU.add).then_inc(s["ada_turned"], 1)

            def turn_slot_0(w):
                dve.wait_ge(s["ada_used"], KC)
                dve.wait_ge(s["ada_product"], KC)
                room = ada_row(w)[:, 0:ADA0_COLS]
                link(V.transpose(room, acc[:, w, 0:ADA0_COLS]))
                V.tensor_reduce(turned[:, w, 0:ADA0_COLS // 32], room.rearrange("p (b j) -> p b j", j=32),
                                AX_X, ALU.add).then_inc(s["ada_turned"], 1)

            def take_mods(a):
                nw = 2 if a < 5 else 1
                dve.wait_ge(s["mods_summed"], a + 1)
                for w in range(nw):
                    for cols, from_bank in ((slice(0, 2 * KC), 7), (slice(2 * KC, 3 * KC), 6 if a == 0 else 7)):
                        at, bias = w * 3 * KC, COL["ada_b"] + a * 3 * KC
                        ins = V.tensor_tensor(mods[:, w, cols], bank[from_bank][:, at + cols.start:at + cols.stop],
                                              par[:, bias + cols.start:bias + cols.stop], ALU.add)
                ins.then_inc(s["mods_read"], 1)
                dve.wait_ge(s["mods_read"], a + 1)
                for w in range(nw):
                    ins = V.tensor_scalar(mods[:, w, KC:2 * KC], mods[:, w, KC:2 * KC], 1.0, None, ALU.add)
                    V.tensor_scalar(acol[:, a, w, 2, :], mods[:, w, 2 * KC:3 * KC], 1.0 if a in (1, 4) else 0.5,
                                    None, ALU.mult)
                link(V.memset(hcol[:, a, 0, :], ALPHA))
                if a == 0:
                    V.memset(hcol[:, a, 1, :], 0.0)
                    for w in range(nw):
                        V.tensor_copy(acol[:, a, w, 0, :], mods[:, w, KC:2 * KC])
                        ins = V.tensor_copy(acol[:, a, w, 1, :], mods[:, w, 0:KC])
                else:
                    gain = par[:, COL["ln_g"] + (a - 1) * KC:COL["ln_g"] + a * KC]
                    bias = par[:, COL["ln_b"] + (a - 1) * KC:COL["ln_b"] + a * KC]
                    V.tensor_scalar(hcol[:, a, 0, :], gain, ALPHA, None, ALU.mult)
                    V.tensor_scalar(hcol[:, a, 1, :], bias, ALPHA, None, ALU.mult)
                    for w in range(nw):
                        V.tensor_tensor(acol[:, a, w, 0, :], mods[:, w, KC:2 * KC], gain, ALU.mult)
                        link(V.tensor_tensor(acol[:, a, w, 1, :], mods[:, w, KC:2 * KC], bias, ALU.mult))
                        ins = V.tensor_tensor(acol[:, a, w, 1, :], acol[:, a, w, 1, :], mods[:, w, 0:KC], ALU.add)
                ins.then_inc(s["mod_cols"], 1)

            def rsqrt(y, x, tmp):
                link(V.tensor_scalar(tmp.bitcast(I32), x.bitcast(I32), 1, None, ALU.logical_shift_right))
                link(V.tensor_scalar(y.bitcast(I32), tmp.bitcast(I32), -1, MAGIC, ALU.mult, ALU.add))
                for _ in range(3):
                    link(V.tensor_tensor(tmp, y, y, ALU.mult))
                    link(V.scalar_tensor_tensor(tmp, tmp, -0.5, x, ALU.mult, ALU.mult))
                    link(V.scalar_tensor_tensor(y, tmp, 1.5, y, ALU.add, ALU.mult))

            def sum_z(n, c, j, half=1):
                nt = T if n < 4 else SEQ
                job_ready(dve, j)
                if c == 0:
                    dve.wait_ge(s["ah_ready"], KC * (n + 1))
                if half == 1 and n in SUB_OF_FFN:
                    dve.wait_ge(s["z_ready"], z_count(n, c, 0))
                for w in range(nt // SEQ):
                    cols = slice(w * SEQ, (w + 1) * SEQ)
                    ins = V.scalar_tensor_tensor(hz[:, c, cols], jbank(j)[:, cols], acol[:, n, w, 2, c:c + 1],
                                                 hz[:, c, cols], ALU.mult, ALU.add)
                ins.then_inc(s["z_ready"], 1)
                if half == 0:
                    return
                if c == KC - 1:
                    return
                dve.wait_ge(s["z_ready"], z_count(n, c))
                if c == 0:
                    V.tensor_copy(sum1[:, 0:nt], hz[:, c, 0:nt]).then_inc(s["s1_added"], 1)
                else:
                    dve.wait_ge(s["s1_added"], (KC - 1) * n + c)
                    V.tensor_tensor(sum1[:, 0:nt], sum1[:, 0:nt], hz[:, c, 0:nt], ALU.add).then_inc(s["s1_added"], 1)

            def normalise(n, next_unit=None):
                nt = T if n < 4 else SEQ
                tc = nt // P
                mean, var, r, tmp = (stat[:, i, 0:tc] for i in range(4))
                dve.wait_ge(s["stat_sums"], n + 1)
                V.tensor_scalar(mean, bank[4][:, 0:tc], 1.0 / D, None, ALU.mult).then_inc(s["mean_ready"], 1)
                dve.wait_ge(s["mean_ready"], n + 1)
                link(V.scalar_tensor_tensor(tmp, mean, -1.0, mean, ALU.mult, ALU.mult))
                link(V.scalar_tensor_tensor(var, bank[4][:, TC:TC + tc], 1.0 / D, tmp, ALU.mult, ALU.add))
                link(V.tensor_scalar(var, var, 0.0, LN_EPS, ALU.max, ALU.add))
                rsqrt(r, var, tmp)
                for t in range(tc):
                    ins = V.tensor_scalar(sq[:, 0, t * P:(t + 1) * P], ident[:], r[:, t:t + 1], None, ALU.mult)
                ins.then_inc(s["diag_ready"], 1)
                if next_unit:
                    split_to(next_unit + 4)
                dve.wait_ge(s["mean_bcast"], n + 1)

                def centre(c):
                    if n == 5 and c >= 2:
                        dve.wait_ge(s["out_ready"], c - 1)
                    elif c >= 2:
                        dve.wait_ge(s["ah_ready"], KC * (n + 1) + c - 1)
                    return V.tensor_tensor(tmp_a[:, c % 2, 0:nt], hz[:, c, 0:nt], bank[6][:, 0:nt], ALU.subtract)

                centre(0)
                link(centre(1))
                dve.wait_ge(s["stat_bcast"], n + 1)

                def lower(c):
                    na = T if n + 1 < 5 else SEQ
                    dve.wait_ge(s["ahi_ready"], KC * (n + 1) + c + 1)
                    if c == 0:
                        dve.wait_ge(s["first_ready"], n + 2)
                    V.tensor_tensor(a_lo[:, c, 0:na], tmp_b[:, c % 2, 0:na], a_hi[:, c, 0:na].bitcast(F32),
                                    ALU.subtract).then_inc(s["a_ready"], 1)

                for c in range(KC):
                    if c >= 2:
                        link(centre(c))
                    V.tensor_tensor(tmp_a[:, c % 2, 0:nt], tmp_a[:, c % 2, 0:nt], bank[5][:, 0:nt],
                                    ALU.mult).then_inc(s["t_ready"], 1)
                    if n < 5 and c >= 1:
                        lower(c - 1)
                if n < 5:
                    lower(KC - 1)

            def ffn(fi):
                _, _, _, nt, adas = FFNS[fi]

                def hidden_step(n, m, j, i=0, between=None):
                    split_lo(n + 4, i)
                    if between:
                        between()
                    dve.wait_ge(s["silu_ready"], m + 1 + 2 * i)
                    dve.wait_ge(s["w_used"], n + 2 + 4 * i)
                    V.tensor_tensor(tmp_b[:, m % 2, 0:nt], tmp_a[:, m % 2, 0:nt], jbank(j0 + n - n0 + 1)[:, 0:nt],
                                    ALU.mult).then_inc(s["hraw_ready"], 1)
                    dve.wait_ge(s["hhi_ready"], m + 1 + 2 * i)
                    V.tensor_tensor(hidden(h_lo, j, i, nt), tmp_b[:, m % 2, 0:nt],
                                    hidden(h_hi, j, i, nt).bitcast(F32), ALU.subtract).then_inc(s["h_ready"], 1)
                    split_lo(n + 5, i)

                for half in range(2):
                    a = ADA_ORDER.index(adas[half]) if adas[half] else None
                    n0, j0 = plan.base[("w1", fi, half)]
                    m0 = (2 * fi + half) * HH
                    used = ada_before(a) if a else 0

                    def body_piece(x, i):
                        k, ah, buf = ADA_BODY[x]
                        loads = ada_loads(a, buf) + (2, 2, 3)[x]
                        add_ada(a, k, ah, buf, used + 2 + x + 3 * i, 16 * loads + 16 * (1, 2, 2)[x] * i, i)

                    def last_piece(x):
                        buf = ADA_LAST[x][2]
                        add_ada(a, *ADA_LAST[x], used + 11 + x, 16 * (ada_loads(a, buf) + (5, 8, 6, 9, 7)[x]))

                    split_to(n0 + 4)
                    for j in range(2):
                        hidden_step(n0 + 2 * j, m0 + j, j)
                        if a:
                            add_ada(a, *ADA_FIRST[j], used + j, 16 * (ada_loads(a, 1 - j) + 1))
                    with dve.Fori(0, 3) as i:
                        for j in (2, 3):
                            hidden_step(n0 + 2 * j, m0 + j, j, i, (lambda: body_piece(j - 2, i)) if a else None)
                        if a:
                            body_piece(2, i)
                    for j in range(8, HH):
                        hidden_step(n0 + 2 * j, m0 + j, j, 0, (lambda: last_piece(j - 8)) if a else None)
                    pos[0] = n0 + 26
                    j1 = plan.base[("w2", fi, half)][1]
                    for oc in range(KC):
                        split_to(n0 + 22 + 2 * oc + 4)
                        sum_z(SUB_OF_FFN[fi], oc, j1 + oc, half)
                        if a and oc < 2:
                            last_piece(3 + oc)
                        if a and 2 <= oc <= 5:
                            turn_ada(a, oc - 2)
                        if a and oc == (6 if half else 7):
                            take_mods(a)

            def filter_and_slot_0():
                def rows(k):
                    if k == 0:
                        dve.wait_ge(s["acc_zeroed"], 1)
                    else:
                        dve.wait_ge(s["ada_used"], k)
                    dve.wait_ge(ada_in[2 * (k % 2)], 16 * (k // 2 + 1))
                    for w in range(2):
                        ins = V.scalar_tensor_tensor(acc[:, w, 0:ADA0_COLS], ada_row(k)[:, 0:ADA0_COLS],
                                                     scol[:, w, k:k + 1], acc[:, w, 0:ADA0_COLS], ALU.mult, ALU.add)
                    ins.then_inc(s["ada_used"], 1)

                dve.wait_ge(s["par_in"], 16)
                dve.wait_ge(s["silu_c"], 1)
                rows(0)
                arg, turns, rest = (taps[0:FHID, i, 0:SEQ] for i in range(3))
                for layer in range(2):
                    j = first_job("filter_h") + layer
                    job_ready(dve, j)
                    b, fr = (("f_b1", "f_fr1"), ("f_b2", "f_fr2"))[layer]
                    link(V.tensor_scalar(arg, jbank(j)[0:FHID, 0:SEQ], pcol(b, 0, FHID), pcol(fr, 0, FHID),
                                         ALU.add, ALU.mult))
                    link(V.tensor_scalar(turns, arg, 1.0 / (2.0 * np.pi), ROUND, ALU.mult, ALU.add))
                    link(V.tensor_scalar(turns, turns, ROUND, None, ALU.subtract))
                    link(V.scalar_tensor_tensor(rest, turns, -TWO_PI_HI, arg, ALU.mult, ALU.add))
                    link(V.scalar_tensor_tensor(rest, turns, -TWO_PI_MID, rest, ALU.mult, ALU.add))
                    V.tensor_scalar(farg[:, layer, :], rest, PI_LOW, -PI_LOW, ALU.min, ALU.max)\
                        .then_inc(s["filter_h_read"], 1)
                    rows(layer + 1)
                j0 = first_job("filter_taps")
                dve.wait_ge(s["window_in"], 16)
                for i in range(4):
                    job_ready(dve, j0 + i)
                    V.tensor_tensor(taps[:, i, :], jbank(j0 + i)[:], window[:, i, :], ALU.mult)\
                        .then_inc(s["taps_read"], 1)
                dve.wait_ge(s["taps_read"], 4)
                for i, op in ((0, ALU.add), (1, ALU.add), (2, ALU.subtract), (3, ALU.subtract)):
                    V.tensor_tensor(tmix[:, i, :], taps[:, i % 2, :], taps[:, 2 + i % 2, :], op)\
                        .then_inc(s["taps_mixed"], 1)
                for k in range(3, KC):
                    rows(k)
                for w in range(2):
                    turn_slot_0(w)

            def end_filter():
                dve.wait_ge(s["spectrum_read"], 4)
                V.memset(spec[0:1, 2, :], 0.0)
                j = first_job("nyquist")
                job_ready(dve, j)
                V.tensor_copy(spec[0:1, 4, :], jbank(j)[0:1, :]).then_inc(s["nyquist_read"], 1)
                j = first_job("tap_norm")
                job_ready(dve, j)
                V.tensor_scalar(stat[:, 0, 0:YC], jbank(j)[:, 0:YC], RMS_EPS, None, ALU.add)\
                    .then_inc(s["tap_norm_read"], 1)
                dve.wait_ge(s["tap_norm_read"], 1)

            def even_mixer():
                split_to(E_U + 4)
                job_ready(dve, E_J)
                V.tensor_copy(low[:], jbank(E_J)[0:2 * RANK, :]).then_inc(s["low_read"], 1)
                split_to(first_unit("e_v") + 6)
                for e in range(4):
                    j = first_job("gate_pre") + e
                    dve.wait_ge(s["gate_abs"], e + 1)
                    V.tensor_scalar(gm[:, e, :], jbank(j)[:], pcol("gate_b", e), 0.0, ALU.add, ALU.min)\
                        .then_inc(s["gate_read"], 1)
                dve.wait_ge(s["w_used"], first_unit("e_v") + 4)
                for t in range(TC):
                    V.tensor_copy(v[:, t, :], bank[4 + t][:]).then_inc(s["v_read"], 1)
                split_to(first_unit("e_hy") + 4)
                dve.wait_ge(s["rst_made"], 2)
                for e in range(4):
                    dve.wait_ge(s["gate_ln"], e + 1)
                    dve.wait_ge(s["gate_read"], e + 1)
                    link(V.tensor_tensor(gm[:, e, :], gm[:, e, :], ga[:, e, :], ALU.subtract))
                    if e < 2:
                        ins = V.tensor_tensor_scan(cum[:, e, :], rst[:], gm[:, e, :], 0.0, ALU.mult, ALU.add)
                    else:
                        ins = V.tensor_tensor_scan(cum[:, e, ::-1], rst[:], gm[:, e, ::-1], 0.0, ALU.mult, ALU.add)
                    link(ins)
                    last = (GCH - 1) * (1 - e // 2)
                    by_chunk = cum[:, e, :].rearrange("p (c t) -> p c t", t=GCH)
                    V.tensor_tensor(kst[:, e, :].rearrange("p (c t) -> p c t", t=GCH),
                                    by_chunk[:, :, last:last + 1].to_broadcast([P, NCH, GCH]), by_chunk,
                                    ALU.subtract).then_inc(s["gate_rest"], 1)
                dve.wait_ge(s["qk_read"], 4)

                def gate_qk(e):
                    dve.wait_ge(s["gate_exp"], e + 1)
                    q, k = qk[:, e % 2, :], qk[:, 2 + e % 2, :]
                    V.scalar_tensor_tensor(qin[:, e, :], q, GDK ** -0.5, qin[:, e, :], ALU.mult, ALU.mult)
                    V.tensor_tensor(kin[:, e, :], k, kin[:, e, :], ALU.mult)
                    V.tensor_tensor(kst[:, e, :], k, kst[:, e, :], ALU.mult).then_inc(s["gla_ops"], 1)
                for c in range(YC):
                    for part in range(3):
                        e = 3 * c + part
                        split_to(first_unit("e_hy") + e + 4)
                        j = first_job("e_hy") + e
                        dve.wait_ge(s["hy_mid"], e + 1)
                        dst = (part2[:, c, :] if part == 2 else cv[:, part, c % 2, :]).rearrange(
                            "p (w t) -> p w t", w=2)
                        u = jbank(j)[:].rearrange("p (w t) -> p w t", w=2)
                        link(V.scalar_tensor_tensor(dst[:, :, 1:SEQ], u[:, :, 0:SEQ - 1],
                                                    pcol("conv_w", YC * part + c), dst[:, :, 1:SEQ],
                                                    ALU.mult, ALU.add))
                        V.scalar_tensor_tensor(dst[:, :, 0:SEQ - 1], u[:, :, 1:SEQ],
                                               pcol("conv_w", 6 * YC + YC * part + c), dst[:, :, 0:SEQ - 1],
                                               ALU.mult, ALU.add).then_inc(s["hy_read"], 1)
                        if part == 1:
                            dve.wait_ge(s["hy_read"], e + 1)
                            V.tensor_tensor(zf[:, c, :], cv[:, 0, c % 2, :], cv[:, 1, c % 2, :], ALU.mult)\
                                .then_inc(s["zf_ready"], 1)
                        if e % 2 == 1 and e < 8:
                            gate_qk(e // 2)
                split_to(first_unit("e_out") + 4)

                def spectra(i):
                    w, r = divmod(i, 2)
                    j = first_job("dft") + 2 * i
                    job_ready(dve, j)
                    if i:
                        dve.wait_ge(s["spec_out"], i)
                    V.tensor_tensor(prod[:, 0, :], jbank(j)[:], spec[:, r, :], ALU.mult)
                    V.tensor_tensor(prod[:, 1, :], jbank(j)[:], spec[:, 2 + r, :], ALU.mult).then_inc(s["dft_read"], 1)
                    job_ready(dve, j + 1)
                    V.tensor_tensor(prod[:, 2, :], jbank(j + 1)[:], spec[:, 2 + r, :], ALU.mult)
                    V.tensor_tensor(prod[:, 3, :], jbank(j + 1)[:], spec[:, 4 if r == 0 else 1, :], ALU.mult)\
                        .then_inc(s["dft_read"], 1)
                    dve.wait_ge(s["dft_read"], 2 * i + 2)
                    V.tensor_tensor(yspec[0][:, r, w, :], prod[:, 0, :], prod[:, 2, :], ALU.subtract)
                    V.tensor_tensor(yspec[1][:, r, w, :], prod[:, 1, :], prod[:, 3, :], ALU.add)\
                        .then_inc(s["spec_out"], 1)

                spectra(0)
                spectra(1)
                dve.wait_ge(s["gla_in"], 32)
                for t in range(TC):
                    dve.wait_ge(s["att"], t + 1)
                    u = bank[4 + t][:].rearrange("p (d h c) -> p d h c", d=2, h=GH)
                    lim = [bound[:, i].rearrange("p d (h c) -> p d h c", h=1).to_broadcast([P, 2, GH, GCH])
                           for i in range(2)]
                    V.tensor_tensor(attm[:, t], u, lim[0], ALU.min).then_inc(s["att_read"], 1)
                    dve.wait_ge(s["att_read"], t + 1)
                    link(V.tensor_tensor(attm[:, t], attm[:, t], lim[1], ALU.max))
                    V.tensor_tensor(attm[:, t, 0], attm[:, t, 0], attm[:, t, 1], ALU.add).then_inc(s["att_masked"], 1)
                spectra(2)
                spectra(3)
                for c in range(YC):
                    j = first_job("idft") + c
                    link(V.tensor_scalar(yt[:, c, :], zf[:, c, :], pcol("skip", c), None, ALU.mult))
                    job_ready(dve, j)
                    V.scalar_tensor_tensor(yt[:, c, :], jbank(j)[:], kscale[:, c:c + 1], yt[:, c, :],
                                           ALU.mult, ALU.add).then_inc(s["idft_read"], 1)
                    dve.wait_ge(s["idft_read"], c + 1)
                    V.tensor_tensor(yt[:, c, :], yt[:, c, :], part2[:, c, :], ALU.mult).then_inc(s["cat"], 1)
                for c in range(YC):
                    dve.wait_ge(s["cat_hi"], c + 1)
                    V.tensor_tensor(a_lo[:, c, :], yt[:, c, :], a_hi[:, c, :].bitcast(F32),
                                    ALU.subtract).then_inc(s["cat_ready"], 1)
                dve.wait_ge(s["kst_turned"], TC)
                dve.wait_ge(s["cat_ready"], YC)
                order = ([4, 5, 6, 7, 0, 1, 2, 3], [7, 6, 5, 4, 3, 2, 1, 0])
                for step in range(NCH - 1):
                    dve.wait_ge(s["ds_read"], (2, 4, 4, 4, 6, 8, 8)[step])
                    if step:
                        dve.wait_ge(s["state_ready"], step)
                    for d in range(2):
                        now, nxt = order[d][step], order[d][step + 1]
                        for hp in range(2):
                            if step == 0:
                                ins = V.tensor_copy(state[:, nxt, d, hp, :], ds[:, now, d, hp, :])
                            else:
                                ins = V.scalar_tensor_tensor(state[:, nxt, d, hp, :], state[:, now, d, hp, :],
                                                             dec[:, d, hp, now:now + 1], ds[:, now, d, hp, :],
                                                             ALU.mult, ALU.add)
                    ins.then_inc(s["state_ready"], 1)
                for t in range(TC):
                    dve.wait_ge(s["o_sq"], t + 1)
                    ins = V.tensor_reduce(stat[:, 0, t * GH:(t + 1) * GH],
                                          osqr[:, t, :].rearrange("p (h c) -> p h c", h=GH), AX_X, ALU.add)
                link(ins)
                link(V.tensor_scalar(stat[:, 0, :], stat[:, 0, :], 1.0 / GDV, RMS_EPS, ALU.mult, ALU.add))
                rsqrt(stat[:, 1, :], stat[:, 0, :], stat[:, 2, :])
                for t in range(TC):
                    r = stat[:, 1, t * GH:(t + 1) * GH].rearrange("p (h c) -> p h c", c=1)
                    V.tensor_tensor(o_sb[:, t, :].rearrange("p (h c) -> p h c", h=GH),
                                    bank[4 + t][:].rearrange("p (h c) -> p h c", h=GH),
                                    r.to_broadcast([P, GH, GDV]), ALU.mult).then_inc(s["o_scaled"], 1)
                for h in range(GH):
                    dve.wait_ge(s["o_turned"], h + 1)
                    dve.wait_ge(s["g_read"], h + 1)
                    V.scalar_tensor_tensor(go[:, h, :], bank[4 + h][:], pcol("gla_g"), gs[:, h, :],
                                           ALU.mult, ALU.mult).then_inc(s["gla_out"], 1)
                    if h >= 1:
                        dve.wait_ge(s["cat_hi"], YC + h)
                        V.tensor_tensor(a_lo[:, YC + h - 1, :], go[:, h - 1, :], a_hi[:, YC + h - 1, :].bitcast(F32),
                                        ALU.subtract).then_inc(s["cat_ready"], 1)
                dve.wait_ge(s["cat_hi"], KC)
                V.tensor_tensor(a_lo[:, KC - 1, :], go[:, GH - 1, :], a_hi[:, KC - 1, :].bitcast(F32),
                                ALU.subtract).then_inc(s["cat_ready"], 1)
                for c in range(KC):
                    split_to(first_unit("e_out") + c + 4)
                    sum_z(1, c, first_job("e_out") + c)

            def odd_mixer():
                cos, sin = rope[:, 0:SEQ], rope[:, SEQ:2 * SEQ]

                def both(x):
                    return x.rearrange("p (a t) -> p a t", a=1).to_broadcast([P, 2, SEQ])

                def rotate(x, turned, tmp, read, done):
                    V.tensor_tensor(tmp, turned, both(sin), ALU.mult).then_inc(s[read[0]], 1)
                    link(V.tensor_tensor(x, x, both(cos), ALU.mult))
                    ins = V.tensor_tensor(x, x, tmp, ALU.add)
                    if done:
                        ins.then_inc(s[done], 1)
                    return ins

                for e in range(KVH + QH):
                    split_to(O_U + e + 4)
                dve.wait_ge(s["odd_in"], 16)
                j = first_job("krot")
                job_ready(dve, j)
                link(rotate(kg[:, :, 0:SEQ], jbank(j)[:].rearrange("p (a t) -> p a t", a=2), krt[:],
                            ("krot_read",), None))
                j = first_job("ksq")
                job_ready(dve, j)
                nk = KVH * TC
                V.tensor_scalar(stat[:, 0, 0:nk], jbank(j)[:, 0:nk], 1.0 / HD, RMS_EPS, ALU.mult, ALU.add)\
                    .then_inc(s["ksq_read"], 1)
                dve.wait_ge(s["ksq_read"], 1)
                rsqrt(stat[:, 1, 0:nk], stat[:, 0, 0:nk], stat[:, 2, 0:nk])
                for g in range(KVH):
                    for t in range(TC):
                        ins = V.tensor_scalar(kd[:, g, t * P:(t + 1) * P], ident[:],
                                              stat[:, 1, g * TC + t:g * TC + t + 1], None, ALU.mult)
                    ins.then_inc(s["kdiag_ready"], 1)
                for i in range(QH // 2):
                    j = first_job("qrot") + i
                    job_ready(dve, j)
                    rotate(qg[:, 2 * i:2 * i + 2, :], jbank(j)[:].rearrange("p (a t) -> p a t", a=2), qrt[:, i % 2],
                           ("qrot_read",), "q_ready")
                j = first_job("qsq")
                job_ready(dve, j)
                V.tensor_scalar(stat[:, 0, :], jbank(j)[:, 0:16], 1.0 / HD, RMS_EPS, ALU.mult, ALU.add)\
                    .then_inc(s["qsq_read"], 1)
                dve.wait_ge(s["qsq_read"], 1)
                rsqrt(stat[:, 1, :], stat[:, 0, :], stat[:, 2, :])
                V.tensor_scalar(att_stat[:, 3, :], stat[:, 1, :], -(HD ** -0.5), None, ALU.mult)
                link(V.tensor_scalar(att_stat[:, 0, :], stat[:, 1, :], HD ** -0.5, None, ALU.mult))
                for g in range(KVH):
                    j = first_job("krms") + g
                    job_ready(dve, j)
                    V.tensor_tensor(kT[:, g, :], kg[:, g, :], jbank(j)[:], ALU.mult).then_inc(s["krms_read"], 1)
                dve.wait_ge(s["w_used"], first_unit("o_v") + 2)
                for t in range(TC):
                    V.tensor_copy(vo[:, t, :], bank[4 + t][:, 0:KVH * HD]).then_inc(s["ov_read"], 1)

                def row_max(i):
                    dve.wait_ge(s["scores"], i + 1)
                    link(V.tensor_reduce(stat[:, 3, i:i + 1], bank[4 + i % 4][:], AX_X, ALU.max))
                    V.tensor_tensor(att_stat[:, 1, i:i + 1], stat[:, 3, i:i + 1], att_stat[:, 3, i:i + 1],
                                    ALU.mult).then_inc(s["smax"], 1)

                def lower_o(h):
                    dve.wait_ge(s["attn_hi"], h + 1)
                    V.tensor_tensor(a_lo[:, h, 0:SEQ], jbank(plan.base[("attn_o", h)])[:, 0:SEQ],
                                    a_hi[:, h, 0:SEQ].bitcast(F32), ALU.subtract).then_inc(s["attn_o_read"], 1)

                for i in range(3):
                    row_max(i)
                for i in range(2 * QH):
                    dve.wait_ge(s["scores_read"], i + 1)
                    link(V.reciprocal(stat[:, 4, i:i + 1], att_stat[:, 2, i:i + 1]))
                    if i >= 3:
                        dve.wait_ge(s["p_turned"], i - 2)
                    V.tensor_scalar(prn[:, i % 3, :], pr[:, i % 4, :], stat[:, 4, i:i + 1], None, ALU.mult)\
                        .then_inc(s["p_ready"], 1)
                    if i + 3 < 2 * QH:
                        row_max(i + 3)
                    if i == 2:
                        split_to(first_unit("o_v") + 5)
                    if i % 2 == 0 and i >= 4:
                        lower_o(i // 2 - 2)
                for h in range(QH - 2, QH):
                    lower_o(h)
                for c in range(KC):
                    split_to(first_unit("o_out") + c + 4)
                    sum_z(4, c, first_job("o_out") + c)

            dve.wait_ge(s["ones_made"], 4)
            for q in range(4):
                V.tensor_copy(fold[32 * q:32 * (q + 1), :], ident[32 * q:32 * (q + 1), 32 * q:32 * (q + 1)])\
                    .then_inc(s["fold_made"], 1)
            filter_and_slot_0()
            split_to(RING)
            take_mods(0)
            end_filter()
            for c in range(KC):
                dve.wait_ge(s["ahi_ready"], c + 1)
                if c == 0:
                    dve.wait_ge(s["first_ready"], 1)
                V.tensor_tensor(a_lo[:, c, :], tmp_b[:, c % 2, :], a_hi[:, c, :].bitcast(F32),
                                ALU.subtract).then_inc(s["a_ready"], 1)
            rsqrt(kscale[:], stat[:, 0, 0:YC], stat[:, 1, 0:YC])
            ffn(0)
            normalise(0, E_U)
            even_mixer()
            normalise(1, plan.base[("w1", 1, 0)][0])
            ffn(1)
            normalise(2, plan.base[("w1", 2, 0)][0])
            ffn(2)
            normalise(3, O_U)
            odd_mixer()
            normalise(4, plan.base[("w1", 3, 0)][0])
            ffn(3)
            normalise(5)

        @block.tensor
        def _(pe):
            def split_product(dst, w_at, x_at, first, last):
                pe.matmul(dst, w_at(0), x_at(0), start=first, stop=False)
                pe.matmul(dst, w_at(1), x_at(0), start=False, stop=False)
                return pe.matmul(dst, w_at(0), x_at(1), start=False, stop=last)

            def w_tile(n, k, width=P):
                return lambda part: (w_hi, w_lo)[part][:, n % RING, k * width:(k + 1) * width]

            def tokens(pair, k, nt):
                return lambda part: pair[part][:, k, 0:nt]

            A_IN, H_IN = (a_hi, a_lo), (h_hi, h_lo)

            def unit_split(n, i=0):
                pe.wait_ge(s["lo_ready"], n + 1 + 4 * i)

            def project(n, j, nt, i=0, order=None, each=None):
                unit_split(n, i)
                order = order or range(KC)
                for at, k in enumerate(order):
                    if each:
                        each(at, k)
                    ins = split_product(jbank(j)[:, 0:nt], w_tile(n, k), tokens(A_IN, k, nt), at == 0, at == KC - 1)
                ins.then_inc(s["w_used"], 1)

            def sum_mods(a):
                nw = 2 if a < 5 else 1
                pe.wait_ge(s["fold_made"], 4)
                pe.wait_ge(s["ada_turned"], turned_before(a) + (2 if a in (0, 5) else 4))
                for q in range(4):
                    for w in range(nw):
                        n = 2 * KC if a == 0 else 3 * KC
                        ins = pe.matmul(bank[7][32 * q:32 * (q + 1), w * 3 * KC:w * 3 * KC + n], fold[:],
                                        turned[:, w, q:4 * n:4], start=True, stop=True)
                ins.then_inc(s["mods_summed"], 1)

            def ada_rows(k):
                pe.wait_ge(ada_in[2 * (k % 2) + 1], 16 * (k // 2 + 1))
                if k == 0:
                    pe.wait_ge(s["silu_c"], 1)
                for c in range(2 * KC, 3 * KC):
                    ins = pe.matmul(bank[6][:, c:6 * KC:3 * KC], ada_row(k)[:, c * P:(c + 1) * P], scol[:, :, k],
                                    start=(k == 0 and c == 2 * KC), stop=(k == KC - 1), skip_group_check=True)
                ins.then_inc(s["ada_product"], 1)

            def layer_norm(n):
                nt = T if n < 4 else SEQ
                for last in range(2):
                    for col, t in ((0, hz[:, KC - 1, :] if last else sum1[:]), (TC, sq[:, 1, :] if last else sum2[:])):
                        if last:
                            pe.wait_ge(*((s["z_ready"], z_count(n, KC - 1)) if col == 0
                                         else (s["sq_ready"], KC * (n + 1))))
                        else:
                            pe.wait_ge(*((s["s1_added"], (KC - 1) * (n + 1)) if col == 0
                                         else (s["s2_added"], (KC - 2) * (n + 1))))
                        for b in range(nt // P):
                            ins = pe.matmul(bank[4][:, col + b:col + b + 1], t[:, b * P:(b + 1) * P], ones[:, 0:1],
                                            start=(last == col == b == 0), stop=(last == 1), skip_group_check=True)
                ins.then_inc(s["stat_sums"], 1)
                pe.wait_ge(s["mean_diag"], n + 1)
                pe.matmul(bank[6][:, 0:nt], ones[:], sq[:, 1, 0:nt], start=True, stop=True)\
                    .then_inc(s["mean_bcast"], 1)
                pe.wait_ge(s["diag_ready"], n + 1)
                pe.matmul(bank[5][:, 0:nt], ones[:], sq[:, 0, 0:nt], start=True, stop=True)\
                    .then_inc(s["stat_bcast"], 1)

            def first_four(n_sub, n0, j0, nts):
                for u in range(4):
                    unit_split(n0 + u)
                    bank_read(pe, j0 + u)
                side = KC - 2
                for k in range(side):
                    for u in range(4):
                        if u == 0:
                            pe.wait_ge(s["ahi_ready"], KC * n_sub + k + 1)
                        for part in range(2):
                            pe.matmul(jbank(j0 + u)[:, 0:nts[u]], w_tile(n0 + u, k)(part), tokens(A_IN, k, nts[u])(0),
                                      start=(k == part == 0), stop=False)
                    pe.wait_ge(s["a_ready"], KC * n_sub + k + 1)
                    for u in range(4):
                        pe.matmul(jbank(j0 + u)[:, 0:nts[u]], w_tile(n0 + u, k)(0), tokens(A_IN, k, nts[u])(1),
                                  start=False, stop=False)
                for u in range(4):
                    for k in range(side, KC):
                        if u == 0:
                            pe.wait_ge(s["a_ready"], KC * n_sub + k + 1)
                        ins = split_product(jbank(j0 + u)[:, 0:nts[u]], w_tile(n0 + u, k), tokens(A_IN, k, nts[u]),
                                            False, k == KC - 1)
                    ins.then_inc(s["w_used"], 1)

            def ffn(fi):
                _, _, _, nt, adas = FFNS[fi]
                n_sub = SUB_OF_FFN[fi]
                for half in range(2):
                    n0, j0 = plan.base[("w1", fi, half)]
                    m0 = (2 * fi + half) * HH
                    if half == 0:
                        first_four(n_sub, n0, j0, [nt] * 4)
                    else:
                        for u in range(4):
                            bank_read(pe, j0 + u)
                            project(n0 + u, j0 + u, nt)
                    with pe.Fori(0, 4) as i:
                        for u in range(4, 8):
                            if u % 2 == 0:
                                pe.wait_ge(s["hraw_ready"], m0 + u // 2 - 1 + 2 * i)
                            project(n0 + u, j0 + u, nt, i)
                    for u in (20, 21):
                        bank_read(pe, j0 + u)
                        project(n0 + u, j0 + u, nt)
                    n1, j1 = plan.base[("w2", fi, half)]
                    for oc in range(KC):
                        if oc == 7 and adas[half]:
                            sum_mods(ADA_ORDER.index(adas[half]))
                        bank_read(pe, j1 + oc)
                        if oc == 0:
                            pe.wait_ge(s["h_ready"], m0 + HH - 1)
                        for piece in range(2):
                            n = n1 + 2 * oc + piece
                            unit_split(n)
                            for k in range(UW2[piece]):
                                j = piece * UW2[0] + k
                                if oc == 0 and j == HH - 1:
                                    pe.wait_ge(s["h_ready"], m0 + HH)
                                ins = split_product(jbank(j1 + oc)[:, 0:nt], w_tile(n, k), tokens(H_IN, j, nt),
                                                    j == 0, j == HH - 1)
                            ins.then_inc(s["w_used"], 1)

            def filter_and_slot_0():
                pe.wait_ge(s["filter_in"], 48)
                pe.wait_ge(s["ones_made"], 4)
                j = first_job("filter_h")
                pe.matmul(jbank(j)[0:FHID, 0:SEQ], fw1[:], feats[:], start=True, stop=True).then_inc(s["filter_h"], 1)
                ada_rows(0)
                pe.wait_ge(s["filter_sin"], 1)
                pe.matmul(jbank(j + 1)[0:FHID, 0:SEQ], fw2[:], fh[0:FHID, 0, :], start=True, stop=True)\
                    .then_inc(s["filter_h"], 1)
                ada_rows(1)
                pe.wait_ge(s["filter_sin"], 2)
                pe.wait_ge(s["taps_in"], 16)
                j = first_job("filter_taps")
                for i in range(4):
                    bank_read(pe, j + i)
                    pe.matmul(jbank(j + i)[:], fh[:, 1, (i % 2) * P:(i % 2 + 1) * P],
                              fw3[:, (i // 2) * HYW:(i // 2 + 1) * HYW], start=True, stop=True)\
                        .then_inc(s["filter_taps"], 1)
                for k in range(2, KC):
                    ada_rows(k)
                pe.wait_ge(s["taps_mixed"], 4)
                pe.wait_ge(s["dft0_in"], 16)
                j = first_job("spectrum")
                for i in range(4):
                    bank_read(pe, j + i)
                    for b in range(2):
                        ins = pe.matmul(jbank(j + i)[:], dft0[:, b, i * P:(i + 1) * P], tmix[:, (i // 2) * 2 + b, :],
                                        start=(b == 0), stop=(b == 1))
                    ins.then_inc(s["spectrum"], 1)
                j = first_job("nyquist")
                bank_read(pe, j)
                for b in range(2):
                    ins = pe.matmul(jbank(j)[0:1, :], dft0[:, b, SEQ:SEQ + 1], tmix[:, b, :],
                                    start=(b == 0), stop=(b == 1))
                ins.then_inc(s["nyquist"], 1)
                j = first_job("tap_norm")
                bank_read(pe, j)
                pe.wait_ge(s["squares_added"], 3)
                for c in range(YC):
                    ins = pe.matmul(jbank(j)[:, c:c + 1], tsq[:, 0, c * P:(c + 1) * P], ones[:, 0:1],
                                    start=True, stop=True)
                ins.then_inc(s["tap_norm"], 1)

            def even_mixer():
                first_four(1, E_U, E_J, [T] * 4)
                bank_read(pe, first_job("e_qk") + 3)
                project(first_unit("e_qk") + 3, first_job("e_qk") + 3, T)
                for m in range(4):
                    n = first_unit("e_v") + m
                    unit_split(n)
                    for kk in range(2):
                        k = 2 * m + kk
                        for t in range(TC):
                            ins = split_product(bank[4 + t][:], lambda part: A_IN[part][:, k, t * P:(t + 1) * P],
                                                w_tile(n, kk, GH * GDV), k == 0, k == KC - 1)
                    ins.then_inc(s["w_used"], 1)
                pe.wait_ge(s["low_read"], 1)
                pe.wait_ge(s["gla_in"], 32)
                for e in range(4):
                    j = first_job("gate_pre") + e
                    bank_read(pe, j)
                    pe.matmul(jbank(j)[:], gu[:, e // 2, (e % 2) * P:(e % 2 + 1) * P], low[:], start=True, stop=True)\
                        .then_inc(s["gate_pre"], 1)
                for e in range(3 * YC):
                    bank_read(pe, first_job("e_hy") + e)
                    project(first_unit("e_hy") + e, first_job("e_hy") + e, T)
                for h in range(GH):
                    bank_read(pe, first_job("e_g") + h)
                    project(first_unit("e_g") + h, first_job("e_g") + h, T)
                pe.wait_ge(s["zf_ready"], YC)
                for t in range(TC):
                    j = first_job("z_turned") + t
                    bank_read(pe, j)
                    for c in range(YC):
                        ins = pe.transpose(jbank(j)[:, c * P:(c + 1) * P], zf[:, c, t * P:(t + 1) * P], ident[:])
                    ins.then_inc(s["z_turned"], 1)
                pe.wait_ge(s["zt_read"], TC)
                pe.wait_ge(s["dft_in"], 32)

                def transform(i):
                    w, r, part = i // 4, i // 2 % 2, i % 2
                    j = first_job("dft") + i
                    bank_read(pe, j)
                    for b in range(2):
                        ins = pe.matmul(jbank(j)[:], dft[:, b, (2 * part + r) * P:(2 * part + r + 1) * P],
                                        zt[:, 2 * w + b, :], start=(b == 0), stop=(b == 1))
                    ins.then_inc(s["dft"], 1)

                for i in range(4):
                    transform(i)
                pe.wait_ge(s["gla_ops"], 4)
                pe.wait_ge(s["v_read"], TC)
                for odd in range(2):
                    if odd:
                        pe.wait_ge(s["att_even"], 1)
                    for t in range(TC):
                        for e in range(odd, 2 * GH, 2):
                            d, h = divmod(e, GH)
                            rows = slice(odd * GDK, (odd + 1) * GDK)
                            for b in range(2):
                                cols = slice((2 * t + b) * GCH, (2 * t + b + 1) * GCH)
                                ins = pe.matmul(bank[4 + t][b * GCH:(b + 1) * GCH, e * GCH:(e + 1) * GCH],
                                                kin[rows, 2 * d + h // 2, cols], qin[rows, 2 * d + h // 2, cols],
                                                start=True, stop=True)
                        if odd:
                            ins.then_inc(s["att"], 1)
                        elif t == TC - 1:
                            ins.then_inc(s["att_even"], 1)
                for i in range(4, 8):
                    transform(i)
                for t in range(TC):
                    pe.wait_ge(s["att_read"], t + 1)
                    for e in range(4):
                        ins = pe.transpose(bank[4 + t][:, e * P:(e + 1) * P], kst[:, e, t * P:(t + 1) * P], ident[:])
                    ins.then_inc(s["kst_turned"], 1)
                pe.wait_ge(s["spec_out"], 4)
                for c in range(YC):
                    j = first_job("idft") + c
                    bank_read(pe, j)
                    for w in range(2):
                        for f in range(4):
                            ins = pe.matmul(jbank(j)[:, w * SEQ:(w + 1) * SEQ],
                                            yspec[f // 2][:, f % 2, w, c * P:(c + 1) * P],
                                            idft[:, f, :], start=(f == 0), stop=(f == 3))
                    ins.then_inc(s["idft"], 1)
                pe.wait_ge(s["kst_read"], TC)
                for at_job, cc in enumerate(DS_ORDER):
                    j = first_job("ds") + at_job
                    t, b = divmod(cc, 2)
                    bank_read(pe, j)
                    rows = slice(b * GCH, (b + 1) * GCH)
                    for d in range(2):
                        for h in range(GH):
                            at = (2 * d + h // 2) * P
                            ins = pe.matmul(jbank(j)[(h % 2) * GDK:(h % 2 + 1) * GDK, at:at + P],
                                            kstt[rows, t, d, h // 2, (h % 2) * GDK:(h % 2 + 1) * GDK],
                                            v[rows, t, h * GDV:(h + 1) * GDV], start=True, stop=True)
                    ins.then_inc(s["ds"], 1)
                n0, j0 = first_unit("e_out"), first_job("e_out")

                def four_out(k, u):
                    ins = split_product(jbank(j0 + u)[:], w_tile(n0 + u, k), tokens(A_IN, k, T), k == 0, k == KC - 1)
                    if k == KC - 1:
                        ins.then_inc(s["w_used"], 1)

                for u in range(4):
                    unit_split(n0 + u)
                    bank_read(pe, j0 + u)
                pe.wait_ge(s["cat_ready"], 1)
                for u in range(4):
                    four_out(0, u)
                pe.wait_ge(s["att_masked"], TC)
                pe.wait_ge(s["state_ready"], NCH - 1)
                for top in range(2):
                    if top:
                        pe.wait_ge(s["o_lower"], 1)
                    rows = slice(top * GCH, (top + 1) * GCH)
                    for t in range(TC):
                        for b in range(2):
                            cc = 2 * t + b
                            cols = slice(cc * GCH, (cc + 1) * GCH)
                            terms = []
                            if b == top:
                                terms += [(h, attm[rows, t, 0, h, :], v[rows, t, h * GDV:(h + 1) * GDV])
                                          for h in range(GH)]
                            terms += [(h, qin[rows, 2 * d + h // 2, cols], state[rows, cc, d, h // 2, :])
                                      for h in range(top, GH, 2) for d in range(2) if cc != (NLAT, NCH - 1)[d]]
                            for at, (h, lhs, rhs) in enumerate(terms):
                                ins = pe.matmul(bank[4 + t][b * GCH:(b + 1) * GCH, h * GDV:(h + 1) * GDV], lhs, rhs,
                                                start=(top == 0 and at == 0),
                                                stop=(top == 1 and at == len(terms) - 1), skip_group_check=True)
                        if top:
                            ins.then_inc(s["o_done"], 1)
                        elif t == TC - 1:
                            ins.then_inc(s["o_lower"], 1)
                for k in range(1, YC):
                    pe.wait_ge(s["cat_ready"], k + 1)
                    for u in range(4):
                        four_out(k, u)
                pe.wait_ge(s["o_scaled"], TC)
                for h in range(GH):
                    for t in range(TC):
                        ins = pe.transpose(bank[4 + h][:, t * P:(t + 1) * P], o_sb[:, t, h * GDV:(h + 1) * GDV], ident[:])
                    ins.then_inc(s["o_turned"], 1)
                for k in range(YC, KC - 2):
                    pe.wait_ge(s["cat_ready"], k + 1)
                    for u in range(4):
                        four_out(k, u)
                pe.wait_ge(s["cat_ready"], KC)
                for u in range(4):
                    for k in range(KC - 2, KC):
                        four_out(k, u)
                for c in range(4, KC):
                    bank_read(pe, j0 + c)
                    project(n0 + c, j0 + c, T)

            def odd_mixer():
                turn = rope[:, 2 * SEQ:2 * SEQ + P]
                first_four(4, O_U, O_J, [T] * KVH + [SEQ] * (4 - KVH))
                for h in range(4 - KVH, QH):
                    bank_read(pe, first_job("o_q") + h)
                    project(first_unit("o_q") + h, first_job("o_q") + h, SEQ)
                pe.wait_ge(s["k_read"], KVH)
                pe.wait_ge(s["odd_in"], 16)
                j = first_job("krot")
                bank_read(pe, j)
                for g in range(KVH):
                    ins = pe.matmul(jbank(j)[:, g * SEQ:(g + 1) * SEQ], turn, kg[:, g, 0:SEQ], start=True, stop=True)
                ins.then_inc(s["krot"], 1)
                j = first_job("ksq")
                bank_read(pe, j)
                for g in range(KVH):
                    for t in range(TC):
                        ins = pe.matmul(jbank(j)[:, g * TC + t:g * TC + t + 1], ksqr[:, g, t * P:(t + 1) * P],
                                        ones[:, 0:1], start=True, stop=True)
                ins.then_inc(s["ksq"], 1)
                for i in range(QH // 2):
                    j = first_job("qrot") + i
                    bank_read(pe, j)
                    pe.wait_ge(s["q_read"], 2 * i + 2)
                    pe.matmul(jbank(j)[:], turn, qg[:, 2 * i:2 * i + 2, :].rearrange("p a t -> p (a t)"),
                              start=True, stop=True).then_inc(s["qrot"], 1)
                j = first_job("qsq")
                bank_read(pe, j)
                for i in range(2 * QH):
                    h, qb = divmod(i, 2)
                    ins = pe.matmul(jbank(j)[:, i:i + 1], qsqr[:, h, qb * P:(qb + 1) * P], ones[:, 0:1],
                                    start=True, stop=True)
                ins.then_inc(s["qsq"], 1)
                for g in range(KVH):
                    j = first_job("krms") + g
                    bank_read(pe, j)
                    pe.wait_ge(s["kdiag_ready"], g + 1)
                    pe.matmul(jbank(j)[:], ones[:], kd[:, g, :], start=True, stop=True).then_inc(s["krms"], 1)
                for m in range(2):
                    n = first_unit("o_v") + m
                    unit_split(n)
                    for kk in range(4):
                        k = 4 * m + kk
                        for t in range(TC):
                            ins = split_product(bank[4 + t][:, 0:KVH * HD],
                                                lambda part: A_IN[part][:, k, t * P:(t + 1) * P],
                                                w_tile(n, kk, KVH * HD), k == 0, k == KC - 1)
                    ins.then_inc(s["w_used"], 1)
                pe.wait_ge(s["krms_read"], KVH)

                def scores(i):
                    h, qb = divmod(i, 2)
                    if i >= 4:
                        pe.wait_ge(s["scores_read"], i - 3)
                    pe.wait_ge(s["q_ready"], h // 2 + 1)
                    pe.matmul(bank[4 + i % 4][:], qg[:, h, qb * P:(qb + 1) * P], kT[:, h // (QH // KVH), :],
                              start=True, stop=True).then_inc(s["scores"], 1)

                def head_out(h):
                    j = plan.base[("attn_o", h)]
                    bank_read(pe, j)
                    pe.wait_ge(s["pt_read"], 2 * h + 2)
                    g = h // (QH // KVH)
                    for t in range(TC):
                        ins = pe.matmul(jbank(j)[:, 0:SEQ], vo[:, t, g * HD:(g + 1) * HD],
                                        pt[:, h % 2, t, :, :].rearrange("p a q -> p (a q)"),
                                        start=(t == 0), stop=(t == TC - 1))
                    ins.then_inc(s["attn_o"], 1)

                pe.wait_ge(s["ov_read"], TC)
                for i in range(3):
                    scores(i)
                for i in range(2 * QH):
                    if i + 3 < 2 * QH:
                        scores(i + 3)
                    j = plan.base[("turned", i)]
                    bank_read(pe, j)
                    pe.wait_ge(s["p_ready"], i + 1)
                    for t in range(TC):
                        ins = pe.transpose(jbank(j)[:, t * P:(t + 1) * P], prn[:, i % 3, t * P:(t + 1) * P], ident[:])
                    ins.then_inc(s["p_turned"], 1)
                    if i % 2 == 0 and i >= 2:
                        head_out(i // 2 - 1)
                n0, j0 = first_unit("o_out"), first_job("o_out")

                def out_part(u, heads):
                    for k in heads:
                        pe.wait_ge(s["attn_o_read"], k + 1)
                        ins = split_product(jbank(j0 + u)[:, 0:SEQ], w_tile(n0 + u, k), tokens(A_IN, k, SEQ),
                                            k == 0, k == KC - 1)
                    if k == KC - 1:
                        ins.then_inc(s["w_used"], 1)

                for u in range(3):
                    unit_split(n0 + u)
                    bank_read(pe, j0 + u)
                    out_part(u, range(QH - 2))
                    if u == 0:
                        head_out(QH - 1)
                for u in range(3):
                    out_part(u, range(QH - 2, QH))
                for c in range(3, KC):
                    bank_read(pe, j0 + c)
                    project(n0 + c, j0 + c, SEQ)

            filter_and_slot_0()
            sum_mods(0)
            ffn(0)
            layer_norm(0)
            even_mixer()
            layer_norm(1)
            ffn(1)
            layer_norm(2)
            ffn(2)
            layer_norm(3)
            odd_mixer()
            layer_norm(4)
            ffn(3)
            layer_norm(5)


def shape_tables():
    f = np.float64
    n = np.arange(SEQ, dtype=f)
    t = np.linspace(0.0, 1.0, SEQ)
    bands = np.linspace(1e-4, BANDS - 1, BANDS)
    ang = 2.0 * np.pi * n[:, None] * bands / SEQ
    feats = np.concatenate([t[:, None], np.cos(ang), -np.sin(ang)], 1).T
    deltas = np.abs(np.linspace(np.log(1e-2) / 1.5, np.log(1e-2) / 0.3, HYW))
    decay = np.exp(-t[:, None] * deltas).reshape(2, P, HYW)
    back = decay.copy()
    back[0, 0] = 0.0
    window = np.stack([decay[0], decay[1], back[0], back[1]], 1)
    fr = np.arange(SEQ, dtype=f)
    turn = 2.0 * np.pi * np.outer(n, fr) / NFREQ
    cos, sin = np.cos(turn), np.sin(turn)
    nyq = np.where(n % 2 == 0, 1.0, -1.0)
    fwd_sin, inv_sin = sin.copy(), 2.0 * sin
    fwd_sin[:, 0] = nyq
    inv_sin[:, 0] = nyq
    inv_cos = 2.0 * cos
    inv_cos[:, 0] = 1.0
    dft = np.concatenate([cos, fwd_sin], 1).reshape(2, P, NFREQ).transpose(1, 0, 2)
    inv = (np.concatenate([inv_cos, inv_sin], 1) / NFREQ).T.reshape(4, P, SEQ).transpose(1, 0, 2)
    key = np.arange(P)[:, None] % GCH
    q = np.arange(GCH)[None, :]
    keep = np.stack([key <= q, key >= q], 1)
    bound = np.stack([np.where(keep, BIG, 0.0), np.where(keep, -BIG, 0.0)], 1)
    pairs = HD // 4
    inv_freq = 10000.0 ** (-np.arange(pairs, dtype=f) / pairs)
    row, col = n // GRID_W, n % GRID_W
    angles = np.concatenate([np.outer(inv_freq, row)] * 2 + [np.outer(inv_freq, col)] * 2, 0)
    exchange = np.zeros((HD, HD))
    for b in (0, 2 * pairs):
        for r in range(pairs):
            exchange[b + pairs + r, b + r] = -1.0
            exchange[b + r, b + pairs + r] = 1.0
    rope = np.concatenate([np.cos(angles), np.sin(angles), exchange], 1)
    return [np.ascontiguousarray(a, dtype=np.float32) for a in (feats, window, dft, inv, bound, rope)]


def lay_out(i):
    cols = [
        i["ada_b"].reshape(-1, P), i["ln_g"].reshape(-1, P), i["ln_b"].reshape(-1, P),
        i["c"].reshape(-1, P), i["c_ctx"].reshape(-1, P),
        i["hyena_conv_w"].reshape(-1, P), i["hyena_conv_b"].reshape(-1, P), i["hyena_skip"].reshape(-1, P),
        i["gla_gate_b"].reshape(-1, P), i["gla_norm_g"].reshape(-1, P),
        i["attn_q_norm"].reshape(-1, P), i["attn_k_norm"].reshape(-1, P),
    ]
    cols += [np.concatenate([i[n], i[n]], 1) for n in ("hyena_f_b1", "hyena_f_fr1", "hyena_f_b2", "hyena_f_fr2")]
    par = np.concatenate(cols, 0).T
    x = np.concatenate([i["x"][0], i["ctx"][0]], 0).T.reshape(KC, P, T).transpose(1, 0, 2)

    def chunks(w):
        return w.reshape(KC, P, -1, P).transpose(2, 1, 0, 3).reshape(-1, P, KC * P)

    def rows(w, per):
        return w.reshape(KC // per, per, P, -1).transpose(0, 2, 1, 3).reshape(KC // per, P, -1)

    w1 = i["ffn_w1"].reshape(DEPTH, 2, KC, P, 2, HC, P).transpose(0, 1, 5, 4, 3, 2, 6).reshape(
        DEPTH, 2, HC, 2, P, KC * P)
    w2 = i["ffn_w2"].reshape(DEPTH, 2, 2, HH, P, KC, P).transpose(0, 1, 2, 5, 4, 3, 6).reshape(
        DEPTH, 2, 2, KC, P, HH * P)
    ada = i["ada_w"].reshape(DEPTH, KC, P, 3, 3 * D).transpose(0, 3, 1, 2, 4)
    w = i["even_w_in"][0]
    at = np.cumsum([0, 3 * HYW, GH * GDK, GH * GDK, GH * GDV, GH * GDV, 2 * RANK])
    hy, q, k, v, g, low = (w[:, a:b] for a, b in zip(at[:-1], at[1:]))
    low = np.concatenate([low, np.zeros((D, P - 2 * RANK), low.dtype)], 1)
    hy = hy.reshape(D, 3, YC, P).transpose(0, 2, 1, 3).reshape(D, -1)
    ew = chunks(np.concatenate([low, q, k, hy, g], 1))
    o = i["attn_w_in"][0]
    gu = np.zeros((2 * RANK, 2, 2 * P), np.float32)
    gu[0:RANK, 0], gu[RANK:, 1] = i["gla_gate_up"][0]
    fw3 = np.concatenate([i["hyena_f_w3"][0], i["hyena_f_b3"]], 0)
    feats, window, dft, inv, bound, rope = shape_tables()
    return [x, par, w1, w2, ada, ew, rows(v, 2), chunks(i["even_w_out"][0]),
            chunks(np.concatenate([o[:, QH * HD:(QH + KVH) * HD], o[:, :QH * HD]], 1)),
            rows(o[:, (QH + KVH) * HD:], 4), chunks(i["attn_w_out"][0]), gu,
            i["hyena_f_w1"][0], i["hyena_f_w2"][0], fw3, feats, window, dft, inv, bound, rope]


def kernel(**inputs):
    import concourse.bacc as _bacc
    from concourse.bass_utils import run_bass_kernel_spmd as _run

    nc = _bacc.Bacc("TRN2", target_bir_lowering=False, num_devices=1)
    arrays, args = {}, []
    for n, a in enumerate(lay_out({k: np.asarray(v) for k, v in inputs.items()})):
        a = np.ascontiguousarray(a)
        arrays[f"in_{n}_dram"] = a
        args.append(nc.dram_tensor(f"in_{n}_dram", a.shape, mybir.dt.from_np(a.dtype), kind="ExternalInput").ap())
    args.append(nc.dram_tensor("out_dram", (D, SEQ), F32, kind="ExternalOutput").ap())
    hybrid_trunk(nc, *args)
    r = _run(nc, [arrays], core_ids=[0])
    return np.ascontiguousarray(r.results[0]["out_dram"].T).reshape(1, SEQ, D)
```
